# Optimizing a Trainium2 kernel written in Bass

```python
import math
import jax
import jax.numpy as jnp
from jax import lax
import numpy as np
import jax, jax.numpy as jnp

D_MODEL = 1024
BATCH = 1
SEQ = 256
DEPTH = 2

GDN_HEADS = 4
GDN_DK = 128
GDN_DV = 128
CONV_WIDTH = 4
GDN_CHUNK = 64
ATT_HEADS = 4
ATT_DH = 128
IDX_HEADS = 4
IDX_DH = 64
TOPK_MAX = 256
Q_BLOCK = 128
GLA_HEADS = 4
GLA_DK = D_MODEL // 2 // GLA_HEADS
GLA_DV = D_MODEL // GLA_HEADS
GLA_RANK = 16
GLA_TAU = 16.0
GLA_CHUNK = 64
N_GROUPS = 4
EXPERTS_PER_GROUP = 8
N_EXPERTS = N_GROUPS * EXPERTS_PER_GROUP
TOP_K_EXPERTS = 2
D_EXPERT = 512
MOE_BLOCK = 128
ROPE_THETA = 10000.0
EPS = 1e-6

GDN_QK = GDN_HEADS * GDN_DK
GDN_V = GDN_HEADS * GDN_DV
ATT_W = ATT_HEADS * ATT_DH
EVEN_SPLITS = [GDN_QK, GDN_QK, GDN_V, GDN_V, GDN_HEADS, GDN_HEADS,
               ATT_W, ATT_W, ATT_W, IDX_HEADS * IDX_DH, IDX_DH, IDX_HEADS]
EVEN_IN = int(sum(EVEN_SPLITS))
EVEN_MIX = GDN_V + ATT_W
ODD_SPLITS = [GLA_HEADS * GLA_DK, GLA_HEADS * GLA_DK, GLA_HEADS * GLA_DV,
              GLA_HEADS * GLA_DV, GLA_RANK]
ODD_IN = int(sum(ODD_SPLITS))
ODD_MIX = GLA_HEADS * GLA_DV


F32 = jnp.float32

def split_cols(t, sizes):
    idx = np.cumsum(sizes)[:-1].tolist()
    return jnp.split(t, idx, axis=-1)

def rms_norm(t, g):
    tf = t.astype(F32)
    y = tf * lax.rsqrt(jnp.mean(tf * tf, axis=-1, keepdims=True) + EPS)
    return (y * g.astype(F32)).astype(t.dtype)

def l2_normalize(t):
    tf = t.astype(F32)
    return (tf * lax.rsqrt(jnp.sum(tf * tf, axis=-1, keepdims=True) + EPS)).astype(t.dtype)

def modulate(hn, shift, scale):
    return hn * (1 + scale[:, None, :]) + shift[:, None, :]

def rope_tables(positions, dim):
    inv = 1.0 / (ROPE_THETA ** (jnp.arange(0, dim, 2, dtype=F32) / dim))
    ang = positions.astype(F32)[..., None] * inv
    return jnp.cos(ang), jnp.sin(ang)

def apply_rope(t, cos, sin):
    t1, t2 = jnp.split(t.astype(F32), 2, axis=-1)
    c = cos[:, :, None, :]
    s = sin[:, :, None, :]
    return jnp.concatenate([t1 * c - t2 * s, t2 * c + t1 * s], axis=-1).astype(t.dtype)

def causal_depthwise_conv(t, w):
    width = w.shape[0]
    return lax.conv_general_dilated(
        t, w[:, None, :].astype(t.dtype), window_strides=(1,),
        padding=((width - 1, 0),), dimension_numbers=('NWC', 'WIO', 'NWC'),
        feature_group_count=t.shape[-1])

def to_chunks(t, chunk):
    b, s, h = t.shape[:3]
    t = t.reshape((b, s // chunk, chunk, h) + t.shape[3:])
    return t.transpose((1, 0, 3, 2) + tuple(range(4, t.ndim)))

def from_chunks(t):
    n, b, h, c = t.shape[:4]
    t = t.transpose((1, 0, 3, 2) + tuple(range(4, t.ndim)))
    return t.reshape((b, n * c, h) + t.shape[4:])

def gated_delta_rule(q, k, v, g, beta):
    dtype = v.dtype
    b_, _, h, dk = q.shape
    dv = v.shape[-1]
    c = GDN_CHUNK
    q = to_chunks(q.astype(F32) * dk ** -0.5, c)
    k = to_chunks(k.astype(F32), c)
    v = to_chunks(v.astype(F32), c)
    g = to_chunks(g.astype(F32), c)
    beta = to_chunks(beta.astype(F32), c)
    gc = jnp.cumsum(g, axis=-1)
    incl = jnp.tril(jnp.ones((c, c), bool))
    strict = jnp.tril(jnp.ones((c, c), bool), -1)
    decay = jnp.exp(jnp.where(incl, gc[..., :, None] - gc[..., None, :], -jnp.inf))
    kb = k * beta[..., None]
    lmat = jnp.where(strict, jnp.einsum('nbhid,nbhjd->nbhij', kb, k) * decay, 0.0)
    eye = jnp.eye(c, dtype=F32)
    tmat = lax.linalg.triangular_solve(eye + lmat, jnp.broadcast_to(eye, lmat.shape),
                                       left_side=True, lower=True, unit_diagonal=True)
    w = tmat @ (kb * jnp.exp(gc)[..., None])
    u = tmat @ (v * beta[..., None])
    aqk = jnp.einsum('nbhid,nbhjd->nbhij', q, k) * decay
    qg = q * jnp.exp(gc)[..., None]
    glast = gc[..., -1:]
    kd = k * jnp.exp(glast - gc)[..., None]

    def step(state, xs):
        qg_i, aqk_i, w_i, u_i, kd_i, gl_i = xs
        v_new = u_i - w_i @ state
        o = qg_i @ state + aqk_i @ v_new
        state = state * jnp.exp(gl_i)[..., None] + jnp.swapaxes(kd_i, -1, -2) @ v_new
        return state, o

    s0 = jnp.zeros((b_, h, dk, dv), F32)
    _, o = lax.scan(step, s0, (qg, aqk, w, u, kd, glast))
    return from_chunks(o).astype(dtype)

def gla_chunked(q, k, v, log_a):
    dtype = v.dtype
    b_, _, h, dk = q.shape
    dv = v.shape[-1]
    c = GLA_CHUNK
    q = to_chunks(q.astype(F32) * dk ** -0.5, c)
    k = to_chunks(k.astype(F32), c)
    v = to_chunks(v.astype(F32), c)
    bcum = jnp.cumsum(to_chunks(log_a.astype(F32), c), axis=-2)
    incl = jnp.tril(jnp.ones((c, c), bool))

    def step(state, xs):
        q_i, k_i, v_i, b_i = xs
        bl = b_i[..., -1:, :]
        o_inter = (q_i * jnp.exp(b_i)) @ state
        diff = jnp.where(incl[..., None], b_i[..., :, None, :] - b_i[..., None, :, :], -jnp.inf)
        att = jnp.einsum('bhid,bhjd,bhijd->bhij', q_i, k_i, jnp.exp(diff))
        o = o_inter + att @ v_i
        state = (state * jnp.swapaxes(jnp.exp(bl), -1, -2)
                 + jnp.swapaxes(k_i * jnp.exp(bl - b_i), -1, -2) @ v_i)
        return state, o

    s0 = jnp.zeros((b_, h, dk, dv), F32)
    _, o = lax.scan(step, s0, (q, k, v, bcum))
    return from_chunks(o).astype(dtype)

def dsa_sparse_attention(q, k, v, q_idx, k_idx, w_idx):
    b_, s_, h, dh = q.shape
    topk = min(TOPK_MAX, s_ // 4)
    nblk = s_ // Q_BLOCK
    key_pos = jnp.arange(s_)
    k_idx32 = k_idx.astype(F32)

    def blockify(t):
        return jnp.swapaxes(t.reshape((b_, nblk, Q_BLOCK) + t.shape[2:]), 0, 1)

    def one_block(args):
        q_b, qi_b, wi_b, start = args
        q_pos = start + jnp.arange(Q_BLOCK)
        dots = jnp.einsum('bqhd,bsd->bqhs', qi_b.astype(F32), k_idx32)
        score = jnp.einsum('bqh,bqhs->bqs', wi_b.astype(F32), jax.nn.relu(dots))
        causal = key_pos[None, :] <= q_pos[:, None]
        score = jnp.where(causal[None], score, -jnp.inf)
        _, sel = lax.top_k(score, topk)
        k_sel = jax.vmap(lambda kk, ii: kk[ii])(k, sel)
        v_sel = jax.vmap(lambda vv, ii: vv[ii])(v, sel)
        logits = jnp.einsum('bqhd,bqkhd->bqhk', q_b, k_sel).astype(F32) * dh ** -0.5
        valid = sel <= q_pos[None, :, None]
        logits = jnp.where(valid[:, :, None, :], logits, -jnp.inf)
        p = jax.nn.softmax(logits, axis=-1).astype(v.dtype)
        return jnp.einsum('bqhk,bqkhd->bqhd', p, v_sel)

    starts = jnp.arange(nblk) * Q_BLOCK
    out = lax.map(one_block, (blockify(q), blockify(q_idx), blockify(w_idx), starts))
    return jnp.swapaxes(out, 0, 1).reshape(b_, s_, h, dh)

def even_mixer(h, cos_a, sin_a, cos_i, sin_i, w_in, conv_w, a_log, dt_bias, out_norm, w_out):
    b_, s_, _ = h.shape
    heads = lambda t, n: t.reshape(b_, s_, n, -1)
    proj = h @ w_in
    qa, ka, va, za, ba, aa, qb, kb, vb, qi, ki, wi = split_cols(proj, EVEN_SPLITS)
    qkv = jax.nn.silu(causal_depthwise_conv(jnp.concatenate([qa, ka, va], axis=-1), conv_w))
    qa, ka, va = split_cols(qkv, [GDN_QK, GDN_QK, GDN_V])
    qa = l2_normalize(heads(qa, GDN_HEADS))
    ka = l2_normalize(heads(ka, GDN_HEADS))
    va = heads(va, GDN_HEADS)
    beta = jax.nn.sigmoid(ba.astype(F32))
    g = -jnp.exp(a_log.astype(F32)) * jax.nn.softplus(aa.astype(F32) + dt_bias.astype(F32))
    oa = gated_delta_rule(qa, ka, va, g, beta)
    oa = rms_norm(oa, out_norm) * jax.nn.silu(heads(za, GDN_HEADS))
    qb = apply_rope(heads(qb, ATT_HEADS), cos_a, sin_a)
    kb = apply_rope(heads(kb, ATT_HEADS), cos_a, sin_a)
    vb = heads(vb, ATT_HEADS)
    qi = apply_rope(heads(qi, IDX_HEADS), cos_i, sin_i)
    ki = apply_rope(ki[:, :, None, :], cos_i, sin_i)[:, :, 0, :]
    wi = wi * (IDX_HEADS * IDX_DH) ** -0.5
    ob = dsa_sparse_attention(qb, kb, vb, qi, ki, wi)
    o = jnp.concatenate([oa.reshape(b_, s_, -1), ob.reshape(b_, s_, -1)], axis=-1)
    return o @ w_out

def gla_mixer(h, w_in, w_gate2, b_gate2, out_norm, w_out):
    b_, s_, _ = h.shape
    heads = lambda t: t.reshape(b_, s_, GLA_HEADS, -1)
    proj = h @ w_in
    q, k, v, r, glr = split_cols(proj, ODD_SPLITS)
    log_a = jax.nn.log_sigmoid((glr @ w_gate2 + b_gate2).astype(F32)) / GLA_TAU
    o = gla_chunked(heads(q), heads(k), heads(v), heads(log_a))
    o = rms_norm(o, out_norm) * jax.nn.silu(heads(r))
    return o.reshape(b_, s_, -1) @ w_out

def hier_moe(h, wg, bg, we, be, w1, w3, w2):
    b_, s_, d = h.shape
    t = b_ * s_
    xt = h.reshape(t, d)
    tok_ids = jnp.arange(t)
    g_logits = (xt @ wg + bg).astype(F32)
    g_prob = jax.nn.softmax(g_logits, axis=-1)
    g_sel = jnp.argmax(g_logits, axis=-1)
    g_gate = g_prob[tok_ids, g_sel]
    e_logits = (jnp.einsum('td,gde->tge', xt, we) + be).astype(F32)
    e_logits = e_logits[tok_ids, g_sel]
    top_l, top_i = lax.top_k(e_logits, TOP_K_EXPERTS)
    gates = g_gate[:, None] * jax.nn.softmax(top_l, axis=-1)
    eid = (g_sel[:, None] * EXPERTS_PER_GROUP + top_i).reshape(-1).astype(jnp.int32)
    wts = gates.reshape(-1)
    tok = jnp.repeat(tok_ids.astype(jnp.int32), TOP_K_EXPERTS)
    m = t * TOP_K_EXPERTS
    counts = jnp.bincount(eid, length=N_EXPERTS)
    padded = ((counts + MOE_BLOCK - 1) // MOE_BLOCK) * MOE_BLOCK
    pad_end = jnp.cumsum(padded)
    pad_start = pad_end - padded
    raw_start = jnp.cumsum(counts) - counts
    order = jnp.argsort(eid)
    se = eid[order]
    dest = pad_start[se] + (jnp.arange(m) - raw_start[se])
    p_rows = (-(-m // MOE_BLOCK) + N_EXPERTS) * MOE_BLOCK
    buf_tok = jnp.zeros((p_rows,), jnp.int32).at[dest].set(tok[order])
    buf_w = jnp.zeros((p_rows,), F32).at[dest].set(wts[order])
    nblk = p_rows // MOE_BLOCK
    blk_exp = jnp.clip(jnp.searchsorted(pad_end, jnp.arange(nblk) * MOE_BLOCK, side='right'),
                       0, N_EXPERTS - 1)
    xb = xt[buf_tok].reshape(nblk, MOE_BLOCK, d)

    def expert_block(args):
        xi, e = args
        hid = jax.nn.silu(xi @ w1[e]) * (xi @ w3[e])
        return hid @ w2[e]

    yb = lax.map(expert_block, (xb, blk_exp)).reshape(p_rows, d)
    y = jnp.zeros((t, d), h.dtype).at[buf_tok].add(yb * buf_w[:, None].astype(yb.dtype))
    return y.reshape(b_, s_, d)

def first_inputs(seed: int = 0) -> dict:
    key = jax.random.key(seed)
    d = D_MODEL
    n_even = (DEPTH + 1) // 2
    n_odd = DEPTH // 2

    def nrm(i, shape, scale):
        return jax.random.normal(jax.random.fold_in(key, i), shape, F32) * scale

    def gain(i, shape):
        return 1.0 + nrm(i, shape, 0.02)

    return {
        "x": nrm(0, (BATCH, SEQ, d), 1.0),
        "c": nrm(1, (BATCH, d), 1.0),
        "positions": jnp.broadcast_to(jnp.arange(SEQ, dtype=jnp.int32), (BATCH, SEQ)),
        "ada_w": nrm(2, (DEPTH, d, 6 * d), 0.5 * d ** -0.5),
        "ada_b": nrm(3, (DEPTH, 6 * d), 0.02),
        "norm_mix": gain(4, (DEPTH, d)),
        "norm_ffn": gain(5, (DEPTH, d)),
        "even_w_in": nrm(6, (n_even, d, EVEN_IN), d ** -0.5),
        "gdn_conv_w": nrm(7, (n_even, CONV_WIDTH, 2 * GDN_QK + GDN_V), CONV_WIDTH ** -0.5),
        "gdn_a_log": jnp.log(jax.random.uniform(jax.random.fold_in(key, 8), (n_even, GDN_HEADS), F32, 1.0, 16.0)),
        "gdn_dt_bias": nrm(9, (n_even, GDN_HEADS), 0.1),
        "gdn_out_norm": gain(10, (n_even, GDN_DV)),
        "even_w_out": nrm(11, (n_even, EVEN_MIX, d), EVEN_MIX ** -0.5),
        "gla_w_in": nrm(12, (n_odd, d, ODD_IN), d ** -0.5),
        "gla_w_gate2": nrm(13, (n_odd, GLA_RANK, GLA_HEADS * GLA_DK), GLA_RANK ** -0.5),
        "gla_b_gate2": nrm(14, (n_odd, GLA_HEADS * GLA_DK), 0.1),
        "gla_out_norm": gain(15, (n_odd, GLA_DV)),
        "gla_w_out": nrm(16, (n_odd, ODD_MIX, d), ODD_MIX ** -0.5),
        "router_group_w": nrm(17, (DEPTH, d, N_GROUPS), d ** -0.5),
        "router_group_b": nrm(18, (DEPTH, N_GROUPS), 0.01),
        "router_exp_w": nrm(19, (DEPTH, N_GROUPS, d, EXPERTS_PER_GROUP), d ** -0.5),
        "router_exp_b": nrm(20, (DEPTH, N_GROUPS, EXPERTS_PER_GROUP), 0.01),
        "exp_w1": nrm(21, (DEPTH, N_EXPERTS, d, D_EXPERT), d ** -0.5),
        "exp_w3": nrm(22, (DEPTH, N_EXPERTS, d, D_EXPERT), d ** -0.5),
        "exp_w2": nrm(23, (DEPTH, N_EXPERTS, D_EXPERT, d), D_EXPERT ** -0.5),
        "final_norm": gain(24, (d,)),
    }

def first_block(x, c, positions, ada_w, ada_b, norm_mix, norm_ffn,
              even_w_in, gdn_conv_w, gdn_a_log, gdn_dt_bias, gdn_out_norm, even_w_out,
              gla_w_in, gla_w_gate2, gla_b_gate2, gla_out_norm, gla_w_out,
              router_group_w, router_group_b, router_exp_w, router_exp_b,
              exp_w1, exp_w3, exp_w2, final_norm):
    cos_a, sin_a = rope_tables(positions, ATT_DH)
    cos_i, sin_i = rope_tables(positions, IDX_DH)
    cond = jax.nn.silu(c)
    for layer in range(DEPTH):
        mod = cond @ ada_w[layer] + ada_b[layer]
        sh_m, sc_m, gt_m, sh_f, sc_f, gt_f = jnp.split(mod, 6, axis=-1)
        h = modulate(rms_norm(x, norm_mix[layer]), sh_m, sc_m)
        i = layer // 2
        if layer % 2 == 0:
            mix = even_mixer(h, cos_a, sin_a, cos_i, sin_i, even_w_in[i], gdn_conv_w[i],
                             gdn_a_log[i], gdn_dt_bias[i], gdn_out_norm[i], even_w_out[i])
        else:
            mix = gla_mixer(h, gla_w_in[i], gla_w_gate2[i], gla_b_gate2[i],
                            gla_out_norm[i], gla_w_out[i])
        x = x + gt_m[:, None, :] * mix
        h = modulate(rms_norm(x, norm_ffn[layer]), sh_f, sc_f)
        x = x + gt_f[:, None, :] * hier_moe(h, router_group_w[layer], router_group_b[layer],
                                           router_exp_w[layer], router_exp_b[layer],
                                           exp_w1[layer], exp_w3[layer], exp_w2[layer])
    return rms_norm(x, final_norm)


N_MEM = 256
NORM_EPS = 1e-6
NEG_INF = -1e30
ATTN_BLOCK = 128

LRU_WIDTH = 1024
LRU_BLOCKS = 16
LRU_BLOCK_DIM = LRU_WIDTH // LRU_BLOCKS
LRU_C = 8.0
LRU_A_MIN = 0.9
LRU_A_MAX = 0.999

DIL_GROUPS = ((128, 1), (512, 4), (2048, 16))
DIL_HEADS = 4
DIL_HEAD_DIM = 128
DIL_WIDTH = DIL_HEADS * DIL_HEAD_DIM
DIL_QKV = len(DIL_GROUPS) * DIL_WIDTH

MEM_HEADS = 4
MEM_HEAD_DIM = 64
MEM_WIDTH = MEM_HEADS * MEM_HEAD_DIM

NSA_HEADS = 16
NSA_KV_GROUPS = 2
NSA_HEADS_PER_GROUP = NSA_HEADS // NSA_KV_GROUPS
NSA_HEAD_DIM = 64
NSA_WIDTH = NSA_HEADS * NSA_HEAD_DIM
NSA_KV = NSA_KV_GROUPS * NSA_HEAD_DIM
CMP_BLOCK = 32
CMP_STRIDE = 16
SLC_BLOCK = 64
SLC_TOP_N = 8
WIN_SIZE = 512
PHI_HIDDEN = 256
SEL_FORCE = 1e6

N_EVEN = (DEPTH + 1) // 2
N_ODD = DEPTH // 2

HAWK_IN_SPLITS = (LRU_WIDTH, LRU_WIDTH, DIL_QKV, DIL_QKV, DIL_QKV, DIL_WIDTH, MEM_WIDTH, MEM_WIDTH)
HAWK_IN = sum(HAWK_IN_SPLITS)
HAWK_OUT = LRU_WIDTH + DIL_WIDTH + MEM_WIDTH
NSA_IN_SPLITS = (NSA_WIDTH, 6 * NSA_KV, 3 * NSA_HEADS, NSA_WIDTH, MEM_WIDTH, MEM_WIDTH)
NSA_IN = sum(NSA_IN_SPLITS)
NSA_OUT = NSA_WIDTH + MEM_WIDTH


def rms_norm_2(x, g):
    xf = x.astype(jnp.float32)
    y = xf * lax.rsqrt(jnp.mean(xf * xf, axis=-1, keepdims=True) + NORM_EPS)
    return (y * g.astype(jnp.float32)).astype(x.dtype)

def split_cols_2(h, sizes):
    return jnp.split(h, np.cumsum(sizes)[:-1].tolist(), axis=-1)

def alibi_slopes(n):
    return np.exp2(-8.0 * np.arange(1, n + 1) / n).astype(np.float32)

def banded_attention(q, k, v, slopes, max_dist, pos_scale):
    n, g, r, length, hd = q.shape
    blk = ATTN_BLOCK
    nb = -(-length // blk)
    pad_end = nb * blk - length
    p = -(-max_dist // blk)
    width = (p + 1) * blk
    q = jnp.pad(q, ((0, 0), (0, 0), (0, 0), (0, pad_end), (0, 0)))
    k = jnp.pad(k, ((0, 0), (0, 0), (p * blk, pad_end), (0, 0))).reshape(n, g, nb + p, blk, hd)
    v = jnp.pad(v, ((0, 0), (0, 0), (p * blk, pad_end), (0, 0))).reshape(n, g, nb + p, blk, hd)
    k_win = jnp.concatenate([k[:, :, i:i + nb] for i in range(p + 1)], axis=3).transpose(2, 0, 1, 3, 4)
    v_win = jnp.concatenate([v[:, :, i:i + nb] for i in range(p + 1)], axis=3).transpose(2, 0, 1, 3, 4)
    q_blk = q.reshape(n, g, r, nb, blk, hd).transpose(3, 0, 1, 2, 4, 5)
    dist = p * blk + np.arange(blk)[:, None] - np.arange(width)[None, :]
    key_idx = (np.arange(nb)[:, None] - p) * blk + np.arange(width)[None, :]
    valid = (dist >= 0)[None] & (dist <= max_dist)[None] & (key_idx >= 0)[:, None, :]
    bias = -(slopes[:, :, None, None] * (dist * pos_scale).astype(np.float32)[None, None])
    scale = hd ** -0.5

    def one_block(args):
        qb, kb, vb, ok = args
        s = jnp.einsum('ngrqd,ngkd->ngrqk', qb, kb, preferred_element_type=jnp.float32) * scale + bias
        s = jnp.where(ok, s, NEG_INF)
        m = jnp.max(s, axis=-1, keepdims=True)
        e = jnp.exp(s - m)
        den = jnp.sum(e, axis=-1, keepdims=True)
        o = jnp.einsum('ngrqk,ngkd->ngrqd', (e / den).astype(vb.dtype), vb,
                       preferred_element_type=jnp.float32)
        return o.astype(qb.dtype), (m + jnp.log(den))[..., 0]

    o, lse = lax.map(one_block, (q_blk, k_win, v_win, jnp.asarray(valid)))
    o = o.transpose(1, 2, 3, 0, 4, 5).reshape(n, g, r, nb * blk, hd)[:, :, :, :length]
    lse = lse.transpose(1, 2, 3, 0, 4).reshape(n, g, r, nb * blk)[..., :length]
    return o, lse

def dilated_attention(q, k, v):
    b, s, _, hd = q.shape
    slopes_all = alibi_slopes(len(DIL_GROUPS) * DIL_HEADS).reshape(len(DIL_GROUPS), DIL_HEADS)
    outs, lses = [], []
    for gi, (window, dil) in enumerate(DIL_GROUPS):
        sub = s // dil

        def to_sub(t):
            t = t[:, :, gi * DIL_HEADS:(gi + 1) * DIL_HEADS]
            return t.reshape(b, sub, dil, DIL_HEADS, hd).transpose(0, 2, 3, 1, 4).reshape(
                b * dil, DIL_HEADS, sub, hd)

        o, lse = banded_attention(to_sub(q)[:, :, None], to_sub(k), to_sub(v),
                                  slopes_all[gi][:, None], window // dil, dil)
        outs.append(o[:, :, 0].reshape(b, dil, DIL_HEADS, sub, hd).transpose(0, 3, 1, 2, 4).reshape(
            b, s, DIL_HEADS, hd))
        lses.append(lse[:, :, 0].reshape(b, dil, DIL_HEADS, sub).transpose(0, 3, 1, 2).reshape(
            b, s, DIL_HEADS))
    w = jax.nn.softmax(jnp.stack(lses, axis=0), axis=0)
    o = jnp.einsum('gbsh,gbshd->bshd', w, jnp.stack(outs, axis=0).astype(jnp.float32))
    return o.astype(q.dtype)

def causal_depthwise_conv_2(x, w, bias):
    y = lax.conv_general_dilated(x, w[:, None, :], window_strides=(1,),
                                 padding=((CONV_WIDTH - 1, 0),),
                                 dimension_numbers=('NWC', 'WIO', 'NWC'),
                                 feature_group_count=x.shape[-1])
    return y + bias

def rg_lru(x, gate_a_w, gate_a_b, gate_x_w, gate_x_b, lam):
    b, s, w = x.shape
    xb = x.reshape(b, s, LRU_BLOCKS, LRU_BLOCK_DIM)
    r = jax.nn.sigmoid((jnp.einsum('bshi,hij->bshj', xb, gate_a_w) + gate_a_b).astype(jnp.float32)).reshape(b, s, w)
    i = jax.nn.sigmoid((jnp.einsum('bshi,hij->bshj', xb, gate_x_w) + gate_x_b).astype(jnp.float32)).reshape(b, s, w)
    log_a = -LRU_C * r * jax.nn.softplus(-lam.astype(jnp.float32))
    a = jnp.exp(log_a)
    mult = jnp.sqrt(-jnp.expm1(2.0 * log_a))
    mult = jnp.where((jnp.arange(s) == 0)[None, :, None], 1.0, mult)
    u = x.astype(jnp.float32) * i * mult

    def combine(c1, c2):
        a1, b1 = c1
        a2, b2 = c2
        return a1 * a2, a2 * b1 + b2

    _, h = lax.associative_scan(combine, (a, u), axis=1)
    return h.astype(x.dtype)

def memory_attention(q, mem_n, w_mem_kv):
    b, s, _ = q.shape
    k, v = jnp.split(mem_n @ w_mem_kv, 2, axis=-1)
    q = q.reshape(b, s, MEM_HEADS, MEM_HEAD_DIM)
    k = k.reshape(b, -1, MEM_HEADS, MEM_HEAD_DIM)
    v = v.reshape(b, -1, MEM_HEADS, MEM_HEAD_DIM)
    sc = jnp.einsum('bshd,bmhd->bhsm', q, k, preferred_element_type=jnp.float32) * MEM_HEAD_DIM ** -0.5
    p = jax.nn.softmax(sc, axis=-1)
    o = jnp.einsum('bhsm,bmhd->bshd', p.astype(v.dtype), v)
    return o.reshape(b, s, MEM_WIDTH)

def hawk_dilated_layer(x, mem, norm_g, w_in, conv_w, conv_b, ga_w, ga_b, gx_w, gx_b, lam,
                       mem_norm_g, w_mem_kv, w_out):
    b, s, _ = x.shape
    h = rms_norm_2(x, norm_g) @ w_in
    xa, za, q, k, v, zb, qm, zm = split_cols_2(h, HAWK_IN_SPLITS)
    ya = rg_lru(causal_depthwise_conv_2(xa, conv_w, conv_b), ga_w, ga_b, gx_w, gx_b, lam)
    nh = len(DIL_GROUPS) * DIL_HEADS
    shp = (b, s, nh, DIL_HEAD_DIM)
    yb = dilated_attention(q.reshape(shp), k.reshape(shp), v.reshape(shp)).reshape(b, s, DIL_WIDTH)
    ym = memory_attention(qm, rms_norm_2(mem, mem_norm_g), w_mem_kv)
    y = jnp.concatenate([ya * jax.nn.silu(za), yb * jax.nn.silu(zb), ym * jax.nn.silu(zm)], axis=-1)
    return x + (y.astype(x.dtype) @ w_out)

def compress_tokens(t, pe, w1, w2):
    s, hd = t.shape[2], t.shape[3]
    n_cmp = (s - CMP_BLOCK) // CMP_STRIDE + 1
    idx = np.arange(n_cmp)[:, None] * CMP_STRIDE + np.arange(CMP_BLOCK)[None, :]
    blocks = t[:, :, idx] + pe
    flat = blocks.reshape(blocks.shape[0], blocks.shape[1], n_cmp, CMP_BLOCK * hd)
    return jax.nn.silu(flat @ w1) @ w2

def compressed_attention(q, k, v, slopes):
    s, hd = q.shape[3], q.shape[4]
    n_cmp = k.shape[2]
    block_end = np.arange(n_cmp) * CMP_STRIDE + CMP_BLOCK - 1
    dist = (np.arange(s)[:, None] - block_end[None, :]).astype(np.float32)
    visible = dist >= 0
    bias = -jnp.asarray(slopes)[:, :, None, None] * jnp.asarray(dist)
    sc = jnp.einsum('bgrsd,bgnd->bgrsn', q, k, preferred_element_type=jnp.float32) * hd ** -0.5 + bias
    sc = jnp.where(visible, sc, NEG_INF)
    p = jax.nn.softmax(sc, axis=-1) * visible.any(axis=-1, keepdims=True).astype(np.float32)
    o = jnp.einsum('bgrsn,bgnd->bgrsd', p.astype(v.dtype), v)
    return o, p

def selected_attention(q, k, v, p_cmp, slopes):
    b, g, r, s, hd = q.shape
    n_slc = s // SLC_BLOCK
    top_n = min(SLC_TOP_N, n_slc)
    n_cmp = p_cmp.shape[-1]
    c_start = np.arange(n_cmp)[:, None] * CMP_STRIDE
    s_start = np.arange(n_slc)[None, :] * SLC_BLOCK
    overlap = ((c_start < s_start + SLC_BLOCK) & (c_start + CMP_BLOCK > s_start)).astype(np.float32)
    imp = jnp.einsum('bgrsn,nj->bgsj', p_cmp, overlap)
    cur = (np.arange(s) // SLC_BLOCK)[:, None]
    j = np.arange(n_slc)[None, :]
    forced = (j == 0) | (j == cur) | (j == cur - 1)
    imp = jnp.where(forced, SEL_FORCE, jnp.where(j > cur, -SEL_FORCE, imp))
    _, sel = lax.top_k(imp, top_n)
    nqb = s // ATTN_BLOCK
    k_blocks = k.reshape(b, g, n_slc, SLC_BLOCK, hd)
    v_blocks = v.reshape(b, g, n_slc, SLC_BLOCK, hd)
    q_blk = q.reshape(b, g, r, nqb, ATTN_BLOCK, hd).transpose(3, 0, 1, 2, 4, 5)
    sel_blk = sel.reshape(b, g, nqb, ATTN_BLOCK, top_n).transpose(2, 0, 1, 3, 4)
    qpos_blk = jnp.arange(s, dtype=jnp.int32).reshape(nqb, ATTN_BLOCK)
    bi = jnp.arange(b)[:, None, None]
    gi = jnp.arange(g)[None, :, None]
    slope_b = jnp.asarray(slopes)[None, :, :, None, None]
    n_keys = top_n * SLC_BLOCK

    def one_block(args):
        qb, ib, qpos = args
        flat = ib.reshape(b, g, ATTN_BLOCK * top_n)
        kg = k_blocks[bi, gi, flat].reshape(b, g, ATTN_BLOCK, n_keys, hd)
        vg = v_blocks[bi, gi, flat].reshape(b, g, ATTN_BLOCK, n_keys, hd)
        kpos = (ib[..., None] * SLC_BLOCK + jnp.arange(SLC_BLOCK)).reshape(b, g, ATTN_BLOCK, n_keys)
        dist = (qpos[None, None, :, None] - kpos)[:, :, None]
        sc = jnp.einsum('bgrqd,bgqkd->bgrqk', qb, kg, preferred_element_type=jnp.float32) * hd ** -0.5
        sc = jnp.where(dist >= 0, sc - slope_b * dist.astype(jnp.float32), NEG_INF)
        p = jax.nn.softmax(sc, axis=-1)
        return jnp.einsum('bgrqk,bgqkd->bgrqd', p.astype(vg.dtype), vg)

    o = lax.map(one_block, (q_blk, sel_blk, qpos_blk))
    return o.transpose(1, 2, 3, 0, 4, 5).reshape(b, g, r, s, hd)

def nsa_layer(x, mem, norm_g, w_in, pe_k, pe_v, phik_w1, phik_w2, phiv_w1, phiv_w2,
              mem_norm_g, w_mem_kv, w_out):
    b, s, _ = x.shape
    g, r, hd = NSA_KV_GROUPS, NSA_HEADS_PER_GROUP, NSA_HEAD_DIM
    h = rms_norm_2(x, norm_g) @ w_in
    q, kv, gate_logits, z, qm, zm = split_cols_2(h, NSA_IN_SPLITS)
    q = q.reshape(b, s, g, r, hd).transpose(0, 2, 3, 1, 4)
    kc, vc, ks, vs, kw, vw = [t.reshape(b, s, g, hd).transpose(0, 2, 1, 3)
                              for t in jnp.split(kv, 6, axis=-1)]
    slopes = alibi_slopes(NSA_HEADS).reshape(g, r)
    k_cmp = compress_tokens(kc, pe_k, phik_w1, phik_w2)
    v_cmp = compress_tokens(vc, pe_v, phiv_w1, phiv_w2)
    o_cmp, p_cmp = compressed_attention(q, k_cmp, v_cmp, slopes)
    o_slc = selected_attention(q, ks, vs, p_cmp, slopes)
    o_win, _ = banded_attention(q, kw, vw, slopes, WIN_SIZE - 1, 1)
    gates = jax.nn.sigmoid(gate_logits.astype(jnp.float32)).reshape(b, s, g, r, 3).transpose(0, 2, 3, 1, 4)
    o = gates[..., 0:1] * o_cmp + gates[..., 1:2] * o_slc + gates[..., 2:3] * o_win
    o = o.transpose(0, 3, 1, 2, 4).reshape(b, s, NSA_WIDTH).astype(x.dtype)
    ym = memory_attention(qm, rms_norm_2(mem, mem_norm_g), w_mem_kv)
    y = jnp.concatenate([o * jax.nn.silu(z), ym * jax.nn.silu(zm)], axis=-1)
    return x + (y.astype(x.dtype) @ w_out)

def second_inputs(seed: int = 0) -> dict:
    key = jax.random.key(seed)
    keys = iter(jax.random.split(key, 40))

    def nrm(shape, scale):
        return jax.random.normal(next(keys), shape, jnp.float32) * scale

    def gain(shape):
        return 1.0 + 0.02 * jax.random.normal(next(keys), shape, jnp.float32)

    x = nrm((BATCH, SEQ, D_MODEL), 1.0)
    mem = nrm((BATCH, N_MEM, D_MODEL), 1.0)
    u = jax.random.uniform(next(keys), (N_EVEN, LRU_WIDTH), jnp.float32, LRU_A_MIN, LRU_A_MAX)
    a_base = u ** (1.0 / LRU_C)
    hawk_lambda = jnp.log(a_base) - jnp.log1p(-a_base)
    phi_in = CMP_BLOCK * NSA_HEAD_DIM
    return {
        "x": x,
        "mem": mem,
        "hawk_norm": gain((N_EVEN, D_MODEL)),
        "hawk_w_in": nrm((N_EVEN, D_MODEL, HAWK_IN), D_MODEL ** -0.5),
        "hawk_conv_w": nrm((N_EVEN, CONV_WIDTH, LRU_WIDTH), CONV_WIDTH ** -0.5),
        "hawk_conv_b": nrm((N_EVEN, LRU_WIDTH), 0.02),
        "hawk_gate_a_w": nrm((N_EVEN, LRU_BLOCKS, LRU_BLOCK_DIM, LRU_BLOCK_DIM), LRU_BLOCK_DIM ** -0.5),
        "hawk_gate_a_b": nrm((N_EVEN, LRU_BLOCKS, LRU_BLOCK_DIM), 0.02),
        "hawk_gate_x_w": nrm((N_EVEN, LRU_BLOCKS, LRU_BLOCK_DIM, LRU_BLOCK_DIM), LRU_BLOCK_DIM ** -0.5),
        "hawk_gate_x_b": nrm((N_EVEN, LRU_BLOCKS, LRU_BLOCK_DIM), 0.02),
        "hawk_lambda": hawk_lambda,
        "hawk_mem_norm": gain((N_EVEN, D_MODEL)),
        "hawk_w_mem_kv": nrm((N_EVEN, D_MODEL, 2 * MEM_WIDTH), D_MODEL ** -0.5),
        "hawk_w_out": nrm((N_EVEN, HAWK_OUT, D_MODEL), HAWK_OUT ** -0.5),
        "nsa_norm": gain((N_ODD, D_MODEL)),
        "nsa_w_in": nrm((N_ODD, D_MODEL, NSA_IN), D_MODEL ** -0.5),
        "nsa_pe_k": nrm((N_ODD, CMP_BLOCK, NSA_HEAD_DIM), 0.1),
        "nsa_pe_v": nrm((N_ODD, CMP_BLOCK, NSA_HEAD_DIM), 0.1),
        "nsa_phi_k_w1": nrm((N_ODD, phi_in, PHI_HIDDEN), phi_in ** -0.5),
        "nsa_phi_k_w2": nrm((N_ODD, PHI_HIDDEN, NSA_HEAD_DIM), PHI_HIDDEN ** -0.5),
        "nsa_phi_v_w1": nrm((N_ODD, phi_in, PHI_HIDDEN), phi_in ** -0.5),
        "nsa_phi_v_w2": nrm((N_ODD, PHI_HIDDEN, NSA_HEAD_DIM), PHI_HIDDEN ** -0.5),
        "nsa_mem_norm": gain((N_ODD, D_MODEL)),
        "nsa_w_mem_kv": nrm((N_ODD, D_MODEL, 2 * MEM_WIDTH), D_MODEL ** -0.5),
        "nsa_w_out": nrm((N_ODD, NSA_OUT, D_MODEL), NSA_OUT ** -0.5),
        "final_norm": gain((D_MODEL,)),
    }

def second_block(x, mem, hawk_norm, hawk_w_in, hawk_conv_w, hawk_conv_b, hawk_gate_a_w, hawk_gate_a_b,
              hawk_gate_x_w, hawk_gate_x_b, hawk_lambda, hawk_mem_norm, hawk_w_mem_kv, hawk_w_out,
              nsa_norm, nsa_w_in, nsa_pe_k, nsa_pe_v, nsa_phi_k_w1, nsa_phi_k_w2, nsa_phi_v_w1,
              nsa_phi_v_w2, nsa_mem_norm, nsa_w_mem_kv, nsa_w_out, final_norm):
    for layer in range(DEPTH):
        i = layer // 2
        if layer % 2 == 0:
            x = hawk_dilated_layer(x, mem, hawk_norm[i], hawk_w_in[i], hawk_conv_w[i], hawk_conv_b[i],
                                   hawk_gate_a_w[i], hawk_gate_a_b[i], hawk_gate_x_w[i], hawk_gate_x_b[i],
                                   hawk_lambda[i], hawk_mem_norm[i], hawk_w_mem_kv[i], hawk_w_out[i])
        else:
            x = nsa_layer(x, mem, nsa_norm[i], nsa_w_in[i], nsa_pe_k[i], nsa_pe_v[i], nsa_phi_k_w1[i],
                          nsa_phi_k_w2[i], nsa_phi_v_w1[i], nsa_phi_v_w2[i], nsa_mem_norm[i],
                          nsa_w_mem_kv[i], nsa_w_out[i])
    return rms_norm_2(x, final_norm)


def setup_inputs(seed=0):
    out = dict(first_inputs(seed))
    for name, value in second_inputs(seed + 1).items():
        if name != "x":
            out[name + "_2"] = value
    return out


def reference(
    x, c, positions, ada_w, ada_b, norm_mix, norm_ffn, even_w_in, gdn_conv_w, gdn_a_log,
    gdn_dt_bias, gdn_out_norm, even_w_out, gla_w_in, gla_w_gate2, gla_b_gate2, gla_out_norm,
    gla_w_out, router_group_w, router_group_b, router_exp_w, router_exp_b, exp_w1, exp_w3,
    exp_w2, final_norm, mem_2, hawk_norm_2, hawk_w_in_2, hawk_conv_w_2, hawk_conv_b_2,
    hawk_gate_a_w_2, hawk_gate_a_b_2, hawk_gate_x_w_2, hawk_gate_x_b_2, hawk_lambda_2,
    hawk_mem_norm_2, hawk_w_mem_kv_2, hawk_w_out_2, nsa_norm_2, nsa_w_in_2, nsa_pe_k_2,
    nsa_pe_v_2, nsa_phi_k_w1_2, nsa_phi_k_w2_2, nsa_phi_v_w1_2, nsa_phi_v_w2_2, nsa_mem_norm_2,
    nsa_w_mem_kv_2, nsa_w_out_2, final_norm_2,
):
    x = first_block(
        x, c, positions, ada_w, ada_b, norm_mix, norm_ffn, even_w_in, gdn_conv_w, gdn_a_log,
        gdn_dt_bias, gdn_out_norm, even_w_out, gla_w_in, gla_w_gate2, gla_b_gate2, gla_out_norm,
        gla_w_out, router_group_w, router_group_b, router_exp_w, router_exp_b, exp_w1, exp_w3,
        exp_w2, final_norm,
    )
    return second_block(
        x, mem_2, hawk_norm_2, hawk_w_in_2, hawk_conv_w_2, hawk_conv_b_2, hawk_gate_a_w_2,
        hawk_gate_a_b_2, hawk_gate_x_w_2, hawk_gate_x_b_2, hawk_lambda_2, hawk_mem_norm_2,
        hawk_w_mem_kv_2, hawk_w_out_2, nsa_norm_2, nsa_w_in_2, nsa_pe_k_2, nsa_pe_v_2,
        nsa_phi_k_w1_2, nsa_phi_k_w2_2, nsa_phi_v_w1_2, nsa_phi_v_w2_2, nsa_mem_norm_2,
        nsa_w_mem_kv_2, nsa_w_out_2, final_norm_2,
    )


_drawn_inputs = setup_inputs


def setup_inputs(seed=0):
    import zlib

    import numpy as np

    out = dict(_drawn_inputs(seed))
    spreads = {}
    factors = {'norm_mix': 3.481,
     'norm_ffn': 2.97,
     'gdn_dt_bias': 8.0,
     'gdn_out_norm': 7.42,
     'gla_b_gate2': 4.635,
     'gla_out_norm': 8.0,
     'router_group_b': 8.0,
     'router_exp_b': 6.865,
     'hawk_norm_2': 6.181,
     'hawk_gate_a_b_2': 8.0,
     'hawk_gate_x_b_2': 8.0,
     'hawk_mem_norm_2': 8.0,
     'nsa_norm_2': 8.0,
     'nsa_pe_k_2': 8.0,
     'nsa_pe_v_2': 12.903,
     'nsa_mem_norm_2': 8.0,
     'final_norm_2': 7.961}
    for name, (base, spread) in spreads.items():
        noise = np.random.default_rng([zlib.crc32(name.encode()), seed]).standard_normal(out[name].shape)
        drawn = base * np.exp(spread * noise) if base else spread * noise
        out[name] = jnp.asarray(drawn.astype(out[name].dtype))
    for name, factor in factors.items():
        out[name] = (out[name] * factor).astype(out[name].dtype)
    return out
```

```python
from contextlib import ExitStack

import numpy as np
import concourse.bass as bass
from concourse import mybir

F32 = mybir.dt.float32
I32 = mybir.dt.int32
U32 = mybir.dt.uint32
ALU = mybir.AluOpType
ACT = mybir.ActivationFunctionType
AX = mybir.AxisListType

P = 128
T = 256
TT = T // P
D = 1024
KD = D // P
EPS = 1e-6
NEG = -1e30
TAKEN = -3e30
FAR = 1e32

SLOT = 4096
RING = 6

H = 4
CONV = 4
TOPK = 64
IDX_DH = 64
EXPERTS = 32
GROUPS = 4
PER_GROUP = EXPERTS // GROUPS
FE = 512
FT = FE // P
LEVELS = 7
CAP = 64
GLA_TAU = 16.0
ROPE_THETA = 10000.0

SLOPES_DIL = np.exp2(-8.0 * np.arange(1, 13) / 12).astype(np.float32)
SLOPES_NSA = np.exp2(-8.0 * np.arange(1, 17) / 16).astype(np.float32)
DIL = ((128, 1), (512, 4), (2048, 16))
NSA_H = 16
HD = 64
CMP_BLOCK = 32
CMP_STRIDE = 16
NCMP = (T - CMP_BLOCK) // CMP_STRIDE + 1
PHI = 256
LRU_C = 8.0

C_IDENT = 0
C_ONES = C_IDENT + P
C_TRIU = C_ONES + P
C_LEVEL = C_TRIU + P
C_CAUSAL = C_LEVEL + LEVELS * P
C_IOTA = C_CAUSAL + TT * T
C_INV = C_IOTA + EXPERTS
C_GRP = C_INV + 64 + 32
C_CDIST = C_GRP + EXPERTS
C_ANY = C_CDIST + TT * 16
C_SLOT = C_ANY + TT
C_END = C_SLOT + CAP
CD_END = 4 * TT * T


def constants():
    a = np.zeros((P, C_END), np.float32)
    r, c = np.arange(P)[:, None], np.arange(P)[None, :]
    a[:, C_IDENT:C_IDENT + P] = r == c
    a[:, C_ONES:C_ONES + P] = 1.0
    a[:, C_TRIU:C_TRIU + P] = r <= c
    for n in range(LEVELS):
        s = 1 << n
        a[:, C_LEVEL + n * P:C_LEVEL + (n + 1) * P] = (
            (r // (2 * s) == c // (2 * s)) & (r % (2 * s) < s) & (c % (2 * s) >= s))
    d = np.zeros((P, CD_END), np.float32)
    for t in range(TT):
        i = t * P + np.arange(P)[:, None]
        j = np.arange(T)[None, :]
        dist = (i - j).astype(np.float32)
        a[:, C_CAUSAL + t * T:C_CAUSAL + (t + 1) * T] = np.where(dist >= 0, 0.0, NEG)
        kinds = [dist >= 0] + [(dist >= 0) & (dist % dil == 0) & (dist <= w) for w, dil in DIL]
        for n, ok in enumerate(kinds):
            d[:, (n * TT + t) * T:(n * TT + t + 1) * T] = np.where(ok, dist, FAR)
        end = np.arange(NCMP)[None, :] * CMP_STRIDE + CMP_BLOCK - 1
        cd = (i - end).astype(np.float32)
        a[:, C_CDIST + t * 16:C_CDIST + t * 16 + NCMP] = np.where(cd >= 0, cd, FAR)
        a[:, C_ANY + t] = (cd >= 0).any(axis=1)
    a[:, C_SLOT:C_SLOT + CAP] = 1 + np.arange(CAP)
    a[:, C_IOTA:C_IOTA + EXPERTS] = np.arange(EXPERTS)
    a[:, C_GRP:C_GRP + EXPERTS] = np.arange(EXPERTS) // PER_GROUP
    for at, dim in ((C_INV, 128), (C_INV + 64, IDX_DH)):
        a[:, at:at + dim // 2] = 1.0 / (np.float32(ROPE_THETA) ** (np.arange(0, dim, 2, dtype=np.float32) / np.float32(dim)))
    return a, d


class Signal:

    def __init__(self, sem):
        self.sem, self.n, self.start = sem, 0, 0

    def up(self, k=1):
        self.n += k
        return self.sem

    def at(self, k):
        return self.start + k


COL_A = {}
for _name, _rows in (("norm_mix", 16), ("norm_ffn", 16), ("hawk_norm_2", 8), ("nsa_norm_2", 8), ("hawk_mem_norm_2", 8),
                     ("nsa_mem_norm_2", 8), ("hawk_conv_b_2", 8), ("hawk_gate_a_b_2", 8), ("hawk_gate_x_b_2", 8),
                     ("hawk_lambda_2", 8), ("gla_b_gate2", 4), ("c", 8)):
    COL_A[_name] = (sum(n for _, n in COL_A.values()), _rows)
ROWS_A = sum(n for _, n in COL_A.values())
COL_B = {}
for _name, _rows in (("gdn_conv_w", 48), ("hawk_conv_w_2", 32), ("nsa_pe_k_2", 16), ("nsa_pe_v_2", 16)):
    COL_B[_name] = (sum(n for _, n in COL_B.values()), _rows)
ROWS_B = sum(n for _, n in COL_B.values())


def flat(ap):
    names = " ".join(f"d{i}" for i in range(len(ap.shape)))
    return ap.rearrange(f"{names} -> ({names})")


def program(nc, A, consts, dists, out, last_stage=None):
    with ExitStack() as ctx:
        names = {}

        def sb(stack, name, shape, dt=F32):
            names[name] = names.get(name, 0) + 1
            return stack.enter_context(nc.sbuf_tensor(name if names[name] == 1 else f"{name}_{names[name]}", shape, dt))

        def sem(name):
            return ctx.enter_context(nc.semaphore(name))

        ctx.enter_context(nc.allow_non_contiguous_dma(reason="vectors, position columns and narrow weights"))

        ring = sb(ctx, "ring", [P, RING, SLOT])
        x = sb(ctx, "x", [P, TT, D])
        hT = sb(ctx, "hT", [P, KD, T])
        kc = sb(ctx, "kc", [P, C_END])
        colA = sb(ctx, "colA", [P, ROWS_A])
        colB = sb(ctx, "colB", [P, ROWS_B])
        bank = [ctx.enter_context(nc.psum_tensor(f"bank{i}", [P, 512], F32)) for i in range(8)]
        expert_out = [nc.dram_tensor(f"expert_out{i}", (EXPERTS * CAP, D), F32, kind="Internal").ap() for i in range(2)]
        gate_rows = nc.dram_tensor("gate_rows", (2, EXPERTS, T), F32, kind="Internal").ap()

        ident = kc[:, C_IDENT:C_IDENT + P]
        ones = kc[:, C_ONES:C_ONES + P]
        triu = kc[:, C_TRIU:C_TRIU + P]

        def level(n):
            return kc[:, C_LEVEL + n * P:C_LEVEL + (n + 1) * P]

        causal = kc[:, C_CAUSAL:C_CAUSAL + TT * T].rearrange("p (t s) -> p t s", t=TT)
        iota = kc[:, C_IOTA:C_IOTA + EXPERTS]
        group_of = kc[:, C_GRP:C_GRP + EXPERTS]
        slot_number = kc[:, C_SLOT:C_SLOT + CAP]
        cmp_dist = kc[:, C_CDIST:C_CDIST + TT * 16].rearrange("p (t n) -> p t n", t=TT)

        def col(name, k0=0, n=None):
            table, where = (colA, COL_A) if name in COL_A else (colB, COL_B)
            at, rows = where[name]
            return table[:, at + k0:at + (rows if n is None else k0 + n)]

        vector_steps = Signal(sem("vector_steps"))
        scalar_steps = Signal(sem("scalar_steps"))
        landed = [Signal(sem(f"slot{i}_landed")) for i in range(RING)]
        chunk_used = Signal(sem("chunk_used"))

        chunks = []

        def cols_of(w, k0, nk, parts):
            width = sum(n for _, n in parts)
            dmas, at = [], 0
            for c0, n in parts:
                src = w[k0 * P:(k0 + nk) * P, c0:c0 + n].rearrange("(k p) n -> p k n", p=P)
                dmas.append((at, n, src))
                at += n
            chunks.append((nk, width, dmas))

        def experts(layer):
            for e in range(EXPERTS):
                chunks.append((KD, FE, [(0, FE, A["exp_w1"][layer, e].rearrange("(k p) n -> p k n", p=P))]))
                chunks.append((KD, FE, [(0, FE, A["exp_w3"][layer, e].rearrange("(k p) n -> p k n", p=P))]))
                chunks.append((FT, D, [(0, D, A["exp_w2"][layer, e].rearrange("(k p) n -> p k n", p=P))]))

        first = {}

        def group(name):
            first[name] = len(chunks)

        for layer in range(2):
            group(f"ada{layer}")
            for j in range(12):
                cols_of(A["ada_w"][layer], 0, KD, [(512 * j, 512)])
            if layer == 0:
                group("even_in")
                w = A["even_w_in"][0]
                for c0 in (0, 512, 1024, 1536, 2056, 2568, 3080):
                    cols_of(w, 0, KD, [(c0, 512)])
                cols_of(w, 0, KD, [(2048, 8), (3592, 324)])
                group("even_out")
                for half in range(2):
                    cols_of(A["even_w_out"][0], 0, KD, [(512 * half, 512)])
            else:
                group("gla_in")
                for j in range(6):
                    cols_of(A["gla_w_in"][0], 0, KD, [(512 * j, 512)])
                cols_of(A["gla_w_in"][0], 0, KD, [(3072, 16)])
                group("gla_out")
                for half in range(2):
                    cols_of(A["gla_w_out"][0], 0, KD, [(512 * half, 512)])
            group(f"experts{layer}")
            experts(layer)
        group("hawk_mem")
        cols_of(A["hawk_w_mem_kv_2"][0], 0, KD, [(0, 512)])
        group("hawk_in")
        for j in range(15):
            cols_of(A["hawk_w_in_2"][0], 0, KD, [(512 * j, 512)])
        group("hawk_out")
        for half in range(2):
            cols_of(A["hawk_w_out_2"][0], 0, 8, [(512 * half, 512)])
            cols_of(A["hawk_w_out_2"][0], 8, 6, [(512 * half, 512)])
        group("nsa_mem")
        cols_of(A["nsa_w_mem_kv_2"][0], 0, KD, [(0, 512)])
        group("nsa_in")
        w = A["nsa_w_in_2"][0]
        for j in range(2):
            cols_of(w, 0, KD, [(512 * j, 512)])
        cols_of(w, 0, KD, [(1024, 64)] * 2 + [(1088, 64)] * 2 + [(1152, 64)] * 2 + [(1216, 64)] * 2)
        cols_of(w, 0, KD, [(1280, 64)] * 2 + [(1344, 64)] * 2 + [(1536, 64)] * 2 + [(1600, 64)] * 2)
        cols_of(w, 0, KD, [(1408, 128), (1664, 128), (1792, 48)])
        for j in range(3):
            cols_of(w, 0, KD, [(1840 + 512 * j, 512)])
        group("nsa_phi")
        for name in ("nsa_phi_k_w1_2", "nsa_phi_v_w1_2"):
            cols_of(A[name][0], 0, 16, [(0, PHI)])
        group("nsa_out")
        for half in range(2):
            cols_of(A["nsa_w_out_2"][0], 0, 8, [(512 * half, 512)])
            cols_of(A["nsa_w_out_2"][0], 8, 2, [(512 * half, 512)])

        landed_at = {}
        freed = {}
        issued = [0]

        def slot(c):
            nk, width, _ = chunks[c]
            return ring[:, c % RING, 0:nk * width].rearrange("p (k n) -> p k n", k=nk)

        def load_chunk(sp, c):
            for at, n, src in chunks[c][2]:
                sp.dma_start(slot(c)[:, :, at:at + n], src).then_inc(landed[c % RING].up(16), 16)
            landed_at[c] = landed[c % RING].n

        for c in range(len(chunks)):
            before = landed_at.get(c - RING, 0)
            landed_at[c] = before + 16 * len(chunks[c][2])

        def fill_ring(sp, last):
            while issued[0] < min(len(chunks), last + 1 + RING):
                c = issued[0]
                if c >= RING:
                    s, n = freed[c - RING]
                    sp.wait_ge(s, n)
                load_chunk(sp, c)
                issued[0] += 1

        def arrived(pe, c):
            pe.wait_ge(landed[c % RING].sem, landed_at[c])

        def frees(c0, n):
            for j in range(n):
                freed[c0 + j] = (chunk_used.sem, chunk_used.n + j + 1)

        signals = {}

        def signal(name):
            s = signals.setdefault(name, None) or Signal(sem(name))
            signals[name] = s
            s.start = s.n
            return s

        with ExitStack() as st:
            rowsA = sb(st, "rowsA", [ROWS_A, P])
            rowsB = sb(st, "rowsB", [ROWS_B, P])
            consts_in, vectors_in, turned = signal("consts_in"), signal("vectors_in"), signal("tiles_turned")
            n_vec = len(COL_A) + len(COL_B)
            with nc.Block() as block:
                @block.sync
                def _(sp):
                    fill_ring(sp, -1)

                @block.scalar
                def _(act):
                    act.dma_start(kc[:, :], consts).then_inc(consts_in.up(16), 16)
                    for stage_rows, table in ((rowsA, COL_A), (rowsB, COL_B)):
                        for name, (at, n) in table.items():
                            act.dma_start(stage_rows[at:at + n, :],
                                                        flat(A[name]).rearrange("(r p) -> r p", p=P)).then_inc(vectors_in.up(16), 16)
                    act.dma_start(x[:, :, :], A["x"][0].rearrange("(t p) d -> p t d", p=P)).then_inc(vectors_in.up(16), 16)

                @block.tensor
                def _(pe):
                    pe.wait_ge(consts_in.sem, consts_in.at(16))
                    pe.wait_ge(vectors_in.sem, vectors_in.at(16 * (n_vec + 1)))
                    nc.tensor.transpose(bank[0][:, 0:ROWS_A], rowsA[:, :], ident[0:ROWS_A, 0:ROWS_A])
                    nc.tensor.transpose(bank[1][:, 0:ROWS_B], rowsB[:, :], ident[0:ROWS_B, 0:ROWS_B]).then_inc(turned.up(), 1)

                @block.vector
                def _(dve):
                    dve.wait_ge(turned.sem, turned.at(1))
                    nc.vector.tensor_copy(colA[:, :], bank[0][:, 0:ROWS_A]).then_inc(vector_steps.up(), 1)
                    dve.wait_ge(vector_steps.sem, vector_steps.n)
                    nc.vector.tensor_copy(colB[:, :], bank[1][:, 0:ROWS_B]).then_inc(vector_steps.up(), 1)
                    dve.wait_ge(vector_steps.sem, vector_steps.n)

        def turn_tiles(pe, src, per_bank):
            for b in range(4):
                for k in (2 * b, 2 * b + 1):
                    for t in range(TT):
                        at = (k % 2) * T + t * P
                        last = nc.tensor.transpose(bank[b][:, at:at + P], src[:, t, k * P:(k + 1) * P], ident)
                last.then_inc(per_bank.up(), 1)

        def norm_stage(src, gain, shift, dst, load=None, xn=None):
            with ExitStack() as st:
                if xn is None:
                    xn = sb(st, "xn", [P, TT, D])
                stat = sb(st, "stat", [P, 3, TT])
                squares, root = signal("mean_square_ready"), signal("root_ready")
                normed, turned = signal("normed"), signal("tiles_turned")
                src_in = signal("operands_in")
                with nc.Block() as block:
                    @block.vector
                    def _(dve):
                        if load is not None:
                            dve.wait_ge(src_in.sem, src_in.at(16))
                        for t in range(TT):
                            nc.vector.tensor_tensor_reduce(xn[:, t, :], src[:, t, :], src[:, t, :], 1.0, 0.0, ALU.mult,
                                                                    ALU.add, stat[:, 0, t:t + 1]).then_inc(vector_steps.up(), 1)
                            dve.wait_ge(vector_steps.sem, vector_steps.n)
                        nc.vector.tensor_scalar(stat[:, 1, :], stat[:, 0, :], 1.0 / D, EPS, ALU.mult, ALU.add).then_inc(squares.up(), 1)
                        dve.wait_ge(root.sem, root.at(1))
                        nc.vector.reciprocal(stat[:, 0, :], stat[:, 2, :]).then_inc(vector_steps.up(), 1)
                        dve.wait_ge(vector_steps.sem, vector_steps.n)
                        for t in range(TT):
                            nc.vector.tensor_scalar(xn[:, t, :], src[:, t, :], stat[:, 0, t:t + 1], None, ALU.mult).then_inc(normed.up(), 1)
                        for k in range(KD):
                            if k % 2 == 0:
                                dve.wait_ge(turned.sem, turned.at(k // 2 + 1))
                            at = (k % 2) * T
                            if shift is None:
                                ins = nc.vector.tensor_scalar(dst[:, k, :], bank[k // 2][:, at:at + T], gain[:, k:k + 1], None, ALU.mult)
                            else:
                                ins = nc.vector.tensor_scalar(dst[:, k, :], bank[k // 2][:, at:at + T], gain[:, k:k + 1],
                                                              shift[:, k:k + 1], ALU.mult, ALU.add)
                        ins.then_inc(vector_steps.up(), 1)
                        dve.wait_ge(vector_steps.sem, vector_steps.n)

                    @block.scalar
                    def _(act):
                        if load is not None:
                            act.dma_start(src[:, :, :], load).then_inc(src_in.up(16), 16)
                        act.wait_ge(squares.sem, squares.at(1))
                        nc.scalar.activation(stat[:, 2, :], stat[:, 1, :], ACT.Sqrt).then_inc(root.up(), 1)

                    @block.tensor
                    def _(pe):
                        pe.wait_ge(normed.sem, normed.at(TT))
                        turn_tiles(pe, xn, turned)

        def turn_stage(src, dst):
            turned = signal("tiles_turned")
            with nc.Block() as block:
                @block.tensor
                def _(pe):
                    turn_tiles(pe, src, turned)

                @block.vector
                def _(dve):
                    for b in range(4):
                        dve.wait_ge(turned.sem, turned.at(b + 1))
                        ins = nc.vector.tensor_copy(dst[:, 2 * b:2 * b + 2, :],
                                                    bank[b][:, :].rearrange("p (k t) -> p k t", k=2))
                    ins.then_inc(vector_steps.up(), 1)
                    dve.wait_ge(vector_steps.sem, vector_steps.n)

        def project_tokens(pe, c, pair, src):
            w = slot(c)
            n = chunks[c][1]
            for t in range(TT):
                for k in range(KD):
                    last = nc.tensor.matmul(pair[t][:, 0:n], src[:, k, t * P:(t + 1) * P], w[:, k, :],
                                            start=(k == 0), stop=(k == KD - 1))
            return last

        def project_channels(pe, c, pair, src):
            w = slot(c)
            n = chunks[c][1]
            for m in range(-(-n // P)):
                rows = min(P, n - m * P)
                for k in range(KD):
                    last = nc.tensor.matmul(pair[m // 2][0:rows, (m % 2) * T:(m % 2 + 1) * T], w[:, k, m * P:m * P + rows],
                                            src[:, k, :], start=(k == 0), stop=(k == KD - 1))
            return last

        def project_keys_values(pe, c, pair, src):
            w = slot(c)
            for m in range(2):
                for k in range(KD):
                    nc.tensor.matmul(pair[0][:, m * T:(m + 1) * T], w[:, k, m * P:(m + 1) * P], src[:, k, :],
                                     start=(k == 0), stop=(k == KD - 1))
            for t in range(TT):
                for k in range(KD):
                    last = nc.tensor.matmul(pair[1][:, t * T:(t + 1) * T], src[:, k, t * P:(t + 1) * P], w[:, k, 256:512],
                                            start=(k == 0), stop=(k == KD - 1))
            return last

        def project_stage(c0, plan, src):
            frees(c0, len(plan))
            used0 = chunk_used.n
            out_even, out_odd = signal("even_chunk_evacuated"), signal("odd_chunk_evacuated")
            pairs = [(bank[2 * i], bank[2 * i + 1]) for i in range(4)]
            with nc.Block() as block:
                @block.sync
                def _(sp):
                    fill_ring(sp, c0 + len(plan) - 1)

                @block.tensor
                def _(pe):
                    for j, (kind, _) in enumerate(plan):
                        arrived(pe, c0 + j)
                        if j >= 4:
                            out = (out_even, out_odd)[j % 2]
                            pe.wait_ge(out.sem, out.at((j - 4) // 2 + 1))
                        project = {"token": project_tokens, "channel": project_channels, "keys_values": project_keys_values}[kind]
                        project(pe, c0 + j, pairs[j % 4], src).then_inc(chunk_used.up(), 1)

                @block.scalar
                def _(act):
                    for j, (_, evacuate) in enumerate(plan):
                        if j % 2 == 0:
                            act.wait_ge(chunk_used.sem, used0 + j + 1)
                            for d, s, scale in evacuate(pairs[j % 4]):
                                ins = nc.scalar.activation(d, s, ACT.Copy, scale=scale)
                            ins.then_inc(out_even.up(), 1)
                    act.wait_ge(out_even.sem, out_even.n)

                @block.vector
                def _(dve):
                    for j, (_, evacuate) in enumerate(plan):
                        if j % 2 == 1:
                            dve.wait_ge(chunk_used.sem, used0 + j + 1)
                            for d, s, scale in evacuate(pairs[j % 4]):
                                ins = nc.vector.tensor_scalar(d, s, scale, None, ALU.mult)
                            ins.then_inc(out_odd.up(), 1)

        def to_tokens(dst, at=0, n=512, scale=1.0, src_at=0):
            return lambda pair: [(dst[:, t, at:at + n], pair[t][:, src_at:src_at + n], scale) for t in range(TT)]

        def to_channels(dst, m0, scale=1.0):
            return lambda pair: [(dst[:, m0 + 2 * b:m0 + 2 * b + 2, :], pair[b][:, :].rearrange("p (m t) -> p m t", m=2), scale)
                                 for b in range(2)]

        def out_stage(c0, parts, src, gate):
            n = 2 * len(parts)
            frees(c0, n)
            used0 = chunk_used.n
            last_k = parts[-1][0] + parts[-1][1] - 1
            with ExitStack() as st:
                gated = sb(st, "gated", [P, 512])
                with nc.Block() as block:
                    @block.sync
                    def _(sp):
                        fill_ring(sp, c0 + n - 1)

                    @block.tensor
                    def _(pe):
                        for half in range(2):
                            for i, (k0, nk) in enumerate(parts):
                                c = c0 + half * len(parts) + i
                                arrived(pe, c)
                                w = slot(c)
                                for t in range(TT):
                                    for k in range(nk):
                                        last = nc.tensor.matmul(bank[2 * half + t][:, :], src[:, k0 + k, t * P:(t + 1) * P],
                                                                w[:, k, :], start=(k0 + k == 0), stop=(k0 + k == last_k))
                                last.then_inc(chunk_used.up(), 1)

                    @block.vector
                    def _(dve):
                        for half in range(2):
                            dve.wait_ge(chunk_used.sem, used0 + (half + 1) * len(parts))
                            for t in range(TT):
                                part = bank[2 * half + t][:, :]
                                if gate is not None:
                                    nc.vector.tensor_tensor(gated[:, :], part, gate[:, half * 512:(half + 1) * 512], ALU.mult).then_inc(vector_steps.up(), 1)
                                    dve.wait_ge(vector_steps.sem, vector_steps.n)
                                    part = gated[:, :]
                                xs = x[:, t, half * 512:(half + 1) * 512]
                                nc.vector.tensor_tensor(xs, xs, part, ALU.add).then_inc(vector_steps.up(), 1)
                                dve.wait_ge(vector_steps.sem, vector_steps.n)

        def modulation_stage(layer, gates, mod):
            c0 = first[f"ada{layer}"]
            frees(c0, 12)
            used0 = chunk_used.n
            with ExitStack() as st:
                cond = sb(st, "cond", [P, KD, P])
                silu_c = sb(st, "silu_c", [P, KD])
                bias = sb(st, "ada_bias", [1, 6 * D])
                row = sb(st, "mod_row", [1, 4 * D])
                cols = sb(st, "mod_cols", [P, 4, KD])
                bias_in, silu_ready, cond_ready = signal("operands_in"), signal("silu_c_ready"), signal("cond_ready")
                evac, turned = signal("mod_evacuated"), signal("tiles_turned")
                kinds = [0, 1, None, 2, 3, None]
                with nc.Block() as block:
                    @block.sync
                    def _(sp):
                        fill_ring(sp, c0 + 11)

                    @block.scalar
                    def _(act):
                        act.dma_start(bias[:, :], A["ada_b"][layer:layer + 1, :]).then_inc(bias_in.up(16), 16)
                        nc.scalar.activation(silu_c[:, :], col("c"), ACT.Silu).then_inc(silu_ready.up(), 1)
                        for j in range(12):
                            act.wait_ge(chunk_used.sem, used0 + j + 1)
                            q = j // 2
                            if kinds[q] is None:
                                dst, src = gates[:, q // 3, (j % 2) * 512:(j % 2 + 1) * 512], bank[j % 4][:, :]
                            else:
                                at = kinds[q] * D + (j % 2) * 512
                                dst, src = row[:, at:at + 512], bank[j % 4][0:1, :]
                            nc.scalar.copy(dst, src).then_inc(evac.up(), 1)

                    @block.vector
                    def _(dve):
                        dve.wait_ge(silu_ready.sem, silu_ready.at(1))
                        nc.vector.tensor_copy(cond[:, :, :], silu_c[:, :].unsqueeze(2).to_broadcast([P, KD, P])).then_inc(cond_ready.up(), 1)
                        dve.wait_ge(turned.sem, turned.at(1))
                        nc.vector.tensor_copy(cols[:, :, :], bank[4][:, 0:4 * KD].rearrange("p (q k) -> p q k", q=4)).then_inc(vector_steps.up(), 1)
                        dve.wait_ge(vector_steps.sem, vector_steps.n)
                        for half, name in ((0, "norm_mix"), (1, "norm_ffn")):
                            nc.vector.tensor_copy(mod[:, 2 * half + 1, :], cols[:, 2 * half, :]).then_inc(vector_steps.up(), 1)
                            dve.wait_ge(vector_steps.sem, vector_steps.n)
                            nc.vector.scalar_tensor_tensor(mod[:, 2 * half, :], cols[:, 2 * half + 1, :], 1.0,
                                                                    col(name, 8 * layer, KD), ALU.add, ALU.mult).then_inc(vector_steps.up(), 1)
                            dve.wait_ge(vector_steps.sem, vector_steps.n)

                    @block.tensor
                    def _(pe):
                        pe.wait_ge(cond_ready.sem, cond_ready.at(1))
                        pe.wait_ge(bias_in.sem, bias_in.at(16))
                        for j in range(12):
                            arrived(pe, c0 + j)
                            if j >= 4:
                                pe.wait_ge(evac.sem, evac.at(j - 3))
                            acc = bank[j % 4][:, :]
                            nc.tensor.matmul(acc, ones[0:1, :], bias[:, 512 * j:512 * (j + 1)], start=True, stop=False)
                            for k in range(KD):
                                last = nc.tensor.matmul(acc, cond[:, k, :], slot(c0 + j)[:, k, :], start=False, stop=(k == KD - 1))
                            last.then_inc(chunk_used.up(), 1)
                        pe.wait_ge(evac.sem, evac.at(12))
                        for j in range(4 * KD):
                            last = nc.tensor.transpose(bank[4][:, j:j + 1], row[:, j * P:(j + 1) * P], ident[0:1, 0:1])
                        last.then_inc(turned.up(), 1)

        def even_mixer(mixed):
            with ExitStack() as st:
                conv = sb(st, "conv", [P, 12, T])
                za = sb(st, "za", [P, TT, 512])
                small = sb(st, "small", [P, TT, 332])
                with ExitStack() as st_att:
                    qb = sb(st_att, "qb", [P, TT, 512])
                    kb = sb(st_att, "kb", [P, TT, 512])
                    vb = sb(st_att, "vb", [P, TT, 512])
                    with ExitStack() as st_raw:
                        raw = sb(st_raw, "raw", [P, 12, T + CONV - 1])

                        def to_raw(m0):
                            return lambda pair: [(raw[:, m0 + 2 * b:m0 + 2 * b + 2, CONV - 1:], pair[b][:, :].rearrange("p (m t) -> p m t", m=2), 1.0)
                                                 for b in range(2)]
                        project_stage(first["even_in"], [("channel", to_raw(0)), ("channel", to_raw(4)), ("channel", to_raw(8)),
                                                         ("token", to_tokens(za)), ("token", to_tokens(qb)), ("token", to_tokens(kb)),
                                                         ("token", to_tokens(vb)), ("token", to_tokens(small, 0, 332))], hT)
                        convolve(raw, conv, 12, "gdn_conv_w", None)
                    silu_stage(conv)
                    sparse_attention(mixed, qb, kb, vb, small)
                delta_rule(mixed, conv, za, small)

        def convolve(raw, conv, tiles, weights, bias):
            with nc.Block() as block:
                @block.vector
                def _(dve):
                    nc.vector.memset(raw[:, :, 0:CONV - 1], 0.0).then_inc(vector_steps.up(), 1)
                    dve.wait_ge(vector_steps.sem, vector_steps.n)
                    for i in range(CONV):
                        for m in range(tiles):
                            w = col(weights, i * tiles + m, 1)
                            if i == 0 and bias is not None:
                                ins = nc.vector.tensor_scalar(conv[:, m, :], raw[:, m, 0:T], w, col(bias, m, 1), ALU.mult, ALU.add)
                            elif i == 0:
                                ins = nc.vector.tensor_scalar(conv[:, m, :], raw[:, m, 0:T], w, None, ALU.mult)
                            else:
                                ins = nc.vector.scalar_tensor_tensor(conv[:, m, :], raw[:, m, i:i + T], w, conv[:, m, :], ALU.mult, ALU.add)
                        ins.then_inc(vector_steps.up(), 1)
                        dve.wait_ge(vector_steps.sem, vector_steps.n)

        def silu_stage(t):
            with nc.Block() as block:
                @block.scalar
                def _(act):
                    nc.scalar.activation(t[:, :, :], t[:, :, :], ACT.Silu).then_inc(scalar_steps.up(), 1)
                    act.wait_ge(scalar_steps.sem, scalar_steps.n)

        def rope_tables(angle, sin, cos):
            turn = 2.0 * np.pi
            c1 = 6.28125
            c2 = float(np.float32(np.floor((turn - c1) * 2.0 ** 20) / 2.0 ** 20))
            c3 = float(np.float32(turn - c1 - c2))
            magic = 1.5 * 2.0 ** 23
            with ExitStack() as st:
                pos_i = sb(st, "pos_i", [P, TT], I32)
                pos = sb(st, "pos", [P, TT])
                turns = sb(st, "turns", [P, TT, 96])
                pos_in, reduced, folded = signal("operands_in"), signal("angle_reduced"), signal("angle_folded")
                with nc.Block() as block:
                    @block.scalar
                    def _(act):
                        act.dma_start(pos_i[:, :], A["positions"].rearrange("a (t p) -> p (a t)", p=P)).then_inc(pos_in.up(16), 16)
                        act.wait_ge(reduced.sem, reduced.at(1))
                        nc.scalar.activation(sin[:, :, :], angle[:, :, :], ACT.Sin).then_inc(scalar_steps.up(), 1)
                        act.wait_ge(scalar_steps.sem, scalar_steps.n)
                        act.wait_ge(folded.sem, folded.at(1))
                        nc.scalar.activation(cos[:, :, :], turns[:, :, :], ACT.Sin).then_inc(scalar_steps.up(), 1)
                        act.wait_ge(scalar_steps.sem, scalar_steps.n)

                    @block.vector
                    def _(dve):
                        dve.wait_ge(pos_in.sem, pos_in.at(16))
                        nc.vector.tensor_copy(pos[:, :], pos_i[:, :]).then_inc(vector_steps.up(), 1)
                        dve.wait_ge(vector_steps.sem, vector_steps.n)
                        for t in range(TT):
                            nc.vector.tensor_scalar(angle[:, t, :], kc[:, C_INV:C_INV + 96], pos[:, t:t + 1], None, ALU.mult).then_inc(vector_steps.up(), 1)
                            dve.wait_ge(vector_steps.sem, vector_steps.n)
                        nc.vector.tensor_scalar(turns[:, :, :], angle[:, :, :], 1.0 / turn, magic, ALU.mult, ALU.add).then_inc(vector_steps.up(), 1)
                        dve.wait_ge(vector_steps.sem, vector_steps.n)
                        nc.vector.tensor_scalar(turns[:, :, :], turns[:, :, :], magic, None, ALU.subtract).then_inc(vector_steps.up(), 1)
                        dve.wait_ge(vector_steps.sem, vector_steps.n)
                        for part in (c1, c2, c3):
                            nc.vector.scalar_tensor_tensor(angle[:, :, :], turns[:, :, :], -part, angle[:, :, :], ALU.mult, ALU.add).then_inc(vector_steps.up(), 1)
                            dve.wait_ge(vector_steps.sem, vector_steps.n)
                        nc.vector.tensor_scalar(angle[:, :, :], angle[:, :, :], 3.1415925, -3.1415925, ALU.min, ALU.max).then_inc(reduced.up(), 1)
                        dve.wait_ge(reduced.sem, reduced.n)
                        nc.vector.scalar_tensor_tensor(turns[:, :, :], angle[:, :, :], -1.0, angle[:, :, :], ALU.mult, ALU.min).then_inc(vector_steps.up(), 1)
                        dve.wait_ge(vector_steps.sem, vector_steps.n)
                        nc.vector.tensor_scalar(turns[:, :, :], turns[:, :, :], float(np.pi / 2), None, ALU.add).then_inc(folded.up(), 1)

        def rotate(dve, dst, src, heads, half, cos, sin, t1, t2):
            def table(a):
                return a.unsqueeze(2).to_broadcast([P, TT, heads, half])
            a, b = src[:, :, :, 0:half], src[:, :, :, half:2 * half]
            nc.vector.tensor_tensor(t1, a, table(cos), ALU.mult)
            nc.vector.tensor_tensor(t2, b, table(sin), ALU.mult).then_inc(vector_steps.up(), 1)
            dve.wait_ge(vector_steps.sem, vector_steps.n)
            nc.vector.tensor_tensor(dst[:, :, :, 0:half], t1, t2, ALU.subtract).then_inc(vector_steps.up(), 1)
            dve.wait_ge(vector_steps.sem, vector_steps.n)
            nc.vector.tensor_tensor(t1, b, table(cos), ALU.mult)
            nc.vector.tensor_tensor(t2, a, table(sin), ALU.mult).then_inc(vector_steps.up(), 1)
            dve.wait_ge(vector_steps.sem, vector_steps.n)
            nc.vector.tensor_tensor(dst[:, :, :, half:2 * half], t1, t2, ALU.add).then_inc(vector_steps.up(), 1)
            dve.wait_ge(vector_steps.sem, vector_steps.n)

        def sparse_attention(mixed, qb, kb, vb, small):
            scale = float(P) ** -0.5
            with ExitStack() as st:
                qT = sb(st, "qT", [P, H, T])
                kT = sb(st, "kT", [P, H, T])
                iT = sb(st, "iT", [P, 3, T])
                with ExitStack() as st_rope:
                    angle = sb(st_rope, "angle", [P, TT, 96])
                    sin = sb(st_rope, "sin", [P, TT, 96])
                    cos = sb(st_rope, "cos", [P, TT, 96])
                    qr = sb(st_rope, "qr", [P, TT, H, P])
                    kr = sb(st_rope, "kr", [P, TT, H, P])
                    ir = sb(st_rope, "ir", [P, TT, 6, IDX_DH])
                    t1 = sb(st_rope, "rope_t1", [P, TT, 6 * 64])
                    t2 = sb(st_rope, "rope_t2", [P, TT, 6 * 64])
                    rope_tables(angle, sin, cos)
                    rotated, turned = signal("rotated"), signal("tiles_turned")

                    def temps(heads, half):
                        return [t[:, :, 0:heads * half].rearrange("p t (h d) -> p t h d", h=heads) for t in (t1, t2)]

                    with nc.Block() as block:
                        @block.vector
                        def _(dve):
                            for src, dst in ((qb, qr), (kb, kr)):
                                rotate(dve, dst, src[:, :, :].rearrange("p t (h d) -> p t h d", h=H), H, 64,
                                       cos[:, :, 0:64], sin[:, :, 0:64], *temps(H, 64))
                            rotate(dve, ir[:, :, 0:5, :], small[:, :, 8:328].rearrange("p t (h d) -> p t h d", h=5), 5, 32,
                                   cos[:, :, 64:96], sin[:, :, 64:96], *temps(5, 32))
                            nc.vector.tensor_copy(ir[:, :, 5, :], ir[:, :, 4, :]).then_inc(rotated.up(), 1)
                            for n, (dst, m0, m, s) in enumerate(((qT, 0, 2, scale), (qT, 2, 2, scale), (kT, 0, 2, 1.0), (kT, 2, 2, 1.0),
                                                                 (iT, 0, 2, 1.0), (iT, 2, 1, 1.0))):
                                dve.wait_ge(turned.sem, turned.at(n + 1))
                                ins = nc.vector.tensor_scalar(dst[:, m0:m0 + m, :], bank[n][:, 0:m * T].rearrange("p (m t) -> p m t", m=m),
                                                              s, None, ALU.mult)
                            ins.then_inc(vector_steps.up(), 1)
                            dve.wait_ge(vector_steps.sem, vector_steps.n)

                        @block.tensor
                        def _(pe):
                            pe.wait_ge(rotated.sem, rotated.at(1))
                            tiles = [qr[:, :, h, :] for h in range(H)] + [kr[:, :, h, :] for h in range(H)]
                            tiles += [ir[:, :, 2 * m:2 * m + 2, :] for m in range(3)]
                            for n, tile in enumerate(tiles):
                                for t in range(TT):
                                    at = (n % 2) * T + t * P
                                    src = tile[:, t] if n < 8 else tile[:, t].rearrange("p h d -> p (h d)")
                                    last = nc.tensor.transpose(bank[n // 2][:, at:at + P], src, ident)
                                if n % 2 == 1 or n == 10:
                                    last.then_inc(turned.up(), 1)

                wi = sb(st, "wi", [P, TT, H])
                rel = sb(st, "rel", [P, H, T])
                score = sb(st, "score", [P, T])
                top8 = sb(st, "top8", [P, 8])
                keep = sb(st, "keep", [P, T])
                logits = sb(st, "logits", [P, H, T])
                stat = sb(st, "att_stat", [P, 4, H])
                probs = sb(st, "probs", [P, H, T])
                probsT = sb(st, "probsT", [P, H, TT, P])
                dots_ready, logits_ready = signal("index_dots_ready"), signal("att_logits_ready")
                shifted, exped, normal = signal("att_max_ready"), signal("att_exp_ready"), signal("att_probs_ready")
                turned, probsT_ready, out_ready = signal("att_probs_turned"), signal("att_probsT_ready"), signal("att_out_ready")
                tile_done = signal("att_tile_done")
                with nc.Block() as block:
                    @block.tensor
                    def _(pe):
                        for t in range(TT):
                            if t:
                                pe.wait_ge(tile_done.sem, tile_done.at(t))
                            for h in range(H):
                                lo = (h % 2) * IDX_DH
                                last = nc.tensor.matmul(bank[h % 2][:, (h // 2) * T:(h // 2 + 1) * T],
                                                        iT[lo:lo + IDX_DH, h // 2, t * P:(t + 1) * P], iT[lo:lo + IDX_DH, 2, :],
                                                        start=True, stop=True)
                            last.then_inc(dots_ready.up(), 1)
                            for h in range(H):
                                last = nc.tensor.matmul(bank[2 + h // 2][:, (h % 2) * T:(h % 2 + 1) * T],
                                                        qT[:, h, t * P:(t + 1) * P], kT[:, h, :], start=True, stop=True)
                            last.then_inc(logits_ready.up(), 1)
                            pe.wait_ge(normal.sem, normal.at(t + 1))
                            for h in range(H):
                                for b in range(TT):
                                    at = ((h % 2) * TT + b) * P
                                    last = nc.tensor.transpose(bank[4 + h // 2][:, at:at + P], probs[:, h, b * P:(b + 1) * P], ident)
                            last.then_inc(turned.up(), 1)
                            pe.wait_ge(probsT_ready.sem, probsT_ready.at(t + 1))
                            for h in range(H):
                                for b in range(TT):
                                    last = nc.tensor.matmul(bank[6][:, h * P:(h + 1) * P], probsT[:, h, b, :], vb[:, b, h * P:(h + 1) * P],
                                                            start=(b == 0), stop=(b == TT - 1))
                            last.then_inc(out_ready.up(), 1)

                    @block.vector
                    def _(dve):
                        nc.vector.tensor_scalar(wi[:, :, :], small[:, :, 328:332], (H * IDX_DH) ** -0.5, None, ALU.mult).then_inc(vector_steps.up(), 1)
                        dve.wait_ge(vector_steps.sem, vector_steps.n)
                        for t in range(TT):
                            dve.wait_ge(dots_ready.sem, dots_ready.at(t + 1))
                            for h in range(H):
                                ins = nc.vector.tensor_scalar(rel[:, h, :], bank[h % 2][:, (h // 2) * T:(h // 2 + 1) * T], 0.0, wi[:, t, h:h + 1],
                                                              ALU.max, ALU.mult)
                            ins.then_inc(vector_steps.up(), 1)
                            dve.wait_ge(vector_steps.sem, vector_steps.n)
                            nc.vector.tensor_tensor(score[:, :], rel[:, 0, :], rel[:, 1, :], ALU.add).then_inc(vector_steps.up(), 1)
                            dve.wait_ge(vector_steps.sem, vector_steps.n)
                            nc.vector.tensor_tensor(score[:, :], score[:, :], rel[:, 2, :], ALU.add).then_inc(vector_steps.up(), 1)
                            dve.wait_ge(vector_steps.sem, vector_steps.n)
                            nc.vector.tensor_tensor(score[:, :], score[:, :], rel[:, 3, :], ALU.add).then_inc(vector_steps.up(), 1)
                            dve.wait_ge(vector_steps.sem, vector_steps.n)
                            nc.vector.tensor_tensor(score[:, :], score[:, :], causal[:, t, :], ALU.add).then_inc(vector_steps.up(), 1)
                            dve.wait_ge(vector_steps.sem, vector_steps.n)
                            for _ in range(TOPK // 8):
                                nc.vector.max(top8[:, :], score[:, :]).then_inc(vector_steps.up(), 1)
                                dve.wait_ge(vector_steps.sem, vector_steps.n)
                                nc.vector.match_replace(score[:, :], top8[:, :], score[:, :], TAKEN).then_inc(vector_steps.up(), 1)
                                dve.wait_ge(vector_steps.sem, vector_steps.n)
                            nc.vector.tensor_scalar(keep[:, :], score[:, :], TAKEN, -NEG, ALU.is_equal, ALU.mult).then_inc(vector_steps.up(), 1)
                            dve.wait_ge(vector_steps.sem, vector_steps.n)
                            nc.vector.scalar_tensor_tensor(keep[:, :], keep[:, :], NEG, causal[:, t, :], ALU.add, ALU.add).then_inc(vector_steps.up(), 1)
                            dve.wait_ge(vector_steps.sem, vector_steps.n)
                            dve.wait_ge(logits_ready.sem, logits_ready.at(t + 1))
                            for b in range(2):
                                ins = nc.vector.tensor_tensor(logits[:, 2 * b:2 * b + 2, :], bank[2 + b][:, :].rearrange("p (h s) -> p h s", h=2),
                                                              keep[:, :].unsqueeze(1).to_broadcast([P, 2, T]), ALU.add)
                            ins.then_inc(vector_steps.up(), 1)
                            dve.wait_ge(vector_steps.sem, vector_steps.n)
                            nc.vector.tensor_reduce(stat[:, 0, :], logits[:, :, :], AX.X, ALU.max, negate=True).then_inc(shifted.up(), 1)
                            dve.wait_ge(exped.sem, exped.at(t + 1))
                            nc.vector.reciprocal(stat[:, 2, :], stat[:, 1, :]).then_inc(vector_steps.up(), 1)
                            dve.wait_ge(vector_steps.sem, vector_steps.n)
                            nc.vector.tensor_tensor(probs[:, :, :], probs[:, :, :], stat[:, 2, :].unsqueeze(2).to_broadcast([P, H, T]), ALU.mult).then_inc(normal.up(), 1)
                            dve.wait_ge(turned.sem, turned.at(t + 1))
                            for b in range(2):
                                ins = nc.vector.tensor_copy(probsT[:, 2 * b:2 * b + 2, :, :].rearrange("p h b s -> p (h b s)"), bank[4 + b][:, :])
                            ins.then_inc(probsT_ready.up(), 1)
                            dve.wait_ge(out_ready.sem, out_ready.at(t + 1))
                            nc.vector.tensor_copy(mixed[:, t, 512:1024], bank[6][:, :]).then_inc(tile_done.up(), 1)

                    @block.scalar
                    def _(act):
                        for t in range(TT):
                            act.wait_ge(shifted.sem, shifted.at(t + 1))
                            for h in range(H):
                                ins = nc.scalar.activation(probs[:, h, :], logits[:, h, :], ACT.Exp, bias=stat[:, 0, h:h + 1],
                                                           accum_out=stat[:, 1, h:h + 1])
                            ins.then_inc(exped.up(), 1)

        def delta_rule(mixed, conv, za, small):
            U = TT * H
            with ExitStack() as st:
                gates = sb(st, "gdn_gates", [P, 8, U])
                beta, g, gc, egc, kscale, tmp, tmp2 = (gates[:, i, :] for i in range(7))
                invT = sb(st, "invT", [P, U, P])
                aqk = sb(st, "aqk", [P, U, P])
                qg = sb(st, "qg", [P, H, P])
                with ExitStack() as st_n:
                    sq = sb(st_n, "qk_sq", [P, 8, T])
                    rn = sb(st_n, "qk_rn", [P, 8, T])
                    squared, summed, rooted = signal("qk_squared"), signal("qk_summed"), signal("root_ready")
                    with nc.Block() as block:
                        @block.vector
                        def _(dve):
                            nc.vector.tensor_tensor(sq[:, :, :], conv[:, 0:8, :], conv[:, 0:8, :], ALU.mult).then_inc(squared.up(), 1)
                            for b in range(4):
                                dve.wait_ge(rooted.sem, rooted.at(b + 1))
                                s = slice(2 * b, 2 * b + 2)
                                nc.vector.reciprocal(rn[:, s, :], sq[:, s, :]).then_inc(vector_steps.up(), 1)
                                dve.wait_ge(vector_steps.sem, vector_steps.n)
                                nc.vector.scalar_tensor_tensor(conv[:, s, :], conv[:, s, :], float(P) ** -0.5 if b < 2 else 1.0,
                                                                        rn[:, s, :], ALU.mult, ALU.mult).then_inc(vector_steps.up(), 1)
                                dve.wait_ge(vector_steps.sem, vector_steps.n)

                        @block.tensor
                        def _(pe):
                            pe.wait_ge(squared.sem, squared.at(1))
                            for b in range(4):
                                nc.tensor.matmul(bank[b][:, :], ones, sq[:, 2 * b:2 * b + 2, :].rearrange("p h t -> p (h t)"),
                                                           start=True, stop=True).then_inc(summed.up(), 1)

                        @block.scalar
                        def _(act):
                            for b in range(4):
                                act.wait_ge(summed.sem, summed.at(b + 1))
                                nc.scalar.activation(sq[:, 2 * b:2 * b + 2, :].rearrange("p h t -> p (h t)"), bank[b][:, :], ACT.Sqrt,
                                                               bias=EPS).then_inc(rooted.up(), 1)

                def qT(u):
                    return conv[:, u % H, (u // H) * P:(u // H + 1) * P]

                def kT(u):
                    return conv[:, H + u % H, (u // H) * P:(u // H + 1) * P]

                with ExitStack() as st_d:
                    vec = sb(st_d, "gdn_vec", [P, 2, H])
                    decay = sb(st_d, "decay", [P, U, P])
                    wide = sb(st_d, "wide", [P, U, P])
                    inv = sb(st_d, "inv", [P, U, P])
                    step = sb(st_d, "inv_step", [P, U, P])
                    lower = sb(st_d, "lower", [P, U, P])
                    vec_in, softened, exp1, exp2 = signal("operands_in"), signal("gdn_gate_in"), signal("gdn_exp1"), signal("gdn_exp2")
                    g_ready, cum, diff, decayed = signal("gdn_g_ready"), signal("gdn_cum_ready"), signal("gdn_diff_ready"), signal("gdn_decay_ready")
                    products, masked, turned0 = signal("gdn_products_ready"), signal("gdn_masked"), signal("gdn_first_turned")
                    level_in, x_ready, x_copied, x2_ready = signal("level_in"), signal("level_x_ready"), signal("level_x_copied"), signal("level_terms_ready")

                    def halves(t):
                        return [t[:, 4 * b:4 * b + 4, :].rearrange("p u i -> p (u i)") for b in range(2)]

                    with nc.Block() as block:
                        @block.scalar
                        def _(act):
                            act.dma_start(vec[:, 0, :], A["gdn_a_log"][0].partition_broadcast(P)).then_inc(vec_in.up(16), 16)
                            act.dma_start(vec[:, 1, :], A["gdn_dt_bias"][0].partition_broadcast(P)).then_inc(vec_in.up(16), 16)
                            act.wait_ge(softened.sem, softened.at(1))
                            nc.scalar.activation(gates[:, 5, :], gates[:, 5, :], ACT.Exp, scale=-1.0)
                            nc.scalar.activation(vec[:, 0, :], vec[:, 0, :], ACT.Exp)
                            nc.scalar.activation(beta, beta, ACT.Exp, scale=-1.0).then_inc(scalar_steps.up(), 1)
                            act.wait_ge(scalar_steps.sem, scalar_steps.n)
                            nc.scalar.activation(gates[:, 5, :], gates[:, 5, :], ACT.Ln, bias=1.0).then_inc(exp1.up(), 1)
                            act.wait_ge(diff.sem, diff.at(1))
                            nc.scalar.activation(decay[:, :, :], decay[:, :, :], ACT.Exp)
                            nc.scalar.activation(egc, gc, ACT.Exp)
                            nc.scalar.activation(kscale, kscale, ACT.Exp)
                            nc.scalar.activation(qg[:, :, :], qg[:, :, :], ACT.Exp).then_inc(decayed.up(), 1)

                        @block.vector
                        def _(dve):
                            for t in range(TT):
                                nc.vector.tensor_copy(beta[:, t * H:(t + 1) * H], small[:, t, 0:H]).then_inc(vector_steps.up(), 1)
                                dve.wait_ge(vector_steps.sem, vector_steps.n)
                            dve.wait_ge(vec_in.sem, vec_in.at(32))
                            for t in range(TT):
                                nc.vector.tensor_tensor(g[:, t * H:(t + 1) * H], small[:, t, H:2 * H], vec[:, 1, :], ALU.add).then_inc(vector_steps.up(), 1)
                                dve.wait_ge(vector_steps.sem, vector_steps.n)
                            nc.vector.scalar_tensor_tensor(gates[:, 5, :], g, -1.0, g, ALU.mult, ALU.max).then_inc(softened.up(), 1)
                            dve.wait_ge(exp1.sem, exp1.at(1))
                            nc.vector.tensor_scalar(beta, beta, 1.0, None, ALU.add).then_inc(vector_steps.up(), 1)
                            dve.wait_ge(vector_steps.sem, vector_steps.n)
                            nc.vector.reciprocal(beta, beta).then_inc(vector_steps.up(), 1)
                            dve.wait_ge(vector_steps.sem, vector_steps.n)
                            nc.vector.scalar_tensor_tensor(g, g, 0.0, gates[:, 5, :], ALU.max, ALU.add).then_inc(vector_steps.up(), 1)
                            dve.wait_ge(vector_steps.sem, vector_steps.n)
                            for t in range(TT):
                                nc.vector.scalar_tensor_tensor(g[:, t * H:(t + 1) * H], g[:, t * H:(t + 1) * H], -1.0, vec[:, 0, :],
                                                                        ALU.mult, ALU.mult).then_inc(vector_steps.up(), 1)
                                dve.wait_ge(vector_steps.sem, vector_steps.n)
                            nc.vector.tensor_copy(step[:, :, :], beta.unsqueeze(2).to_broadcast([P, U, P]))
                            nc.vector.tensor_copy(wide[:, :, :], g.unsqueeze(2).to_broadcast([P, U, P])).then_inc(g_ready.up(), 1)
                            dve.wait_ge(cum.sem, cum.at(1))
                            nc.vector.tensor_copy(gc, bank[0][:, 0:U]).then_inc(vector_steps.up(), 1)
                            dve.wait_ge(vector_steps.sem, vector_steps.n)
                            for u in range(U):
                                row = bank[1 + u // H][:, (u % H) * P:(u % H + 1) * P]
                                nc.vector.tensor_scalar(decay[:, u, :], row, gc[:, u:u + 1], 0.0, ALU.subtract, ALU.min)
                            for h in range(H):
                                ins = nc.vector.tensor_scalar(kscale[:, h:h + 1], bank[1][:, h * P + P - 1:h * P + P], gc[:, h:h + 1], None, ALU.subtract)
                            for h in range(H):
                                nc.vector.tensor_copy(kscale[:, H + h:H + h + 1], gc[:, H + h:H + h + 1])
                            nc.vector.tensor_copy(qg[:, :, :], bank[2][:, :].rearrange("p (h i) -> p h i", h=H)).then_inc(diff.up(), 1)
                            dve.wait_ge(decayed.sem, decayed.at(1))
                            dve.wait_ge(products.sem, products.at(1))
                            nc.vector.tensor_tensor(wide[:, :, :], decay[:, :, :], triu.unsqueeze(1).to_broadcast([P, U, P]), ALU.mult).then_inc(vector_steps.up(), 1)
                            dve.wait_ge(vector_steps.sem, vector_steps.n)
                            for b in range(2):
                                nc.vector.tensor_tensor(halves(aqk)[b], bank[5 + b][:, :], halves(wide)[b], ALU.mult).then_inc(vector_steps.up(), 1)
                                dve.wait_ge(vector_steps.sem, vector_steps.n)
                                nc.vector.tensor_tensor(halves(lower)[b], bank[3 + b][:, :], halves(decay)[b], ALU.mult).then_inc(vector_steps.up(), 1)
                                dve.wait_ge(vector_steps.sem, vector_steps.n)
                                nc.vector.tensor_tensor(halves(lower)[b], halves(lower)[b], bank[(7, 0)[b]][:, :], ALU.mult).then_inc(vector_steps.up(), 1)
                                dve.wait_ge(vector_steps.sem, vector_steps.n)
                            wideI = ident.unsqueeze(1).to_broadcast([P, U, P])
                            nc.vector.tensor_tensor(wide[:, :, :], lower[:, :, :], level(0).unsqueeze(1).to_broadcast([P, U, P]), ALU.mult).then_inc(vector_steps.up(), 1)
                            dve.wait_ge(vector_steps.sem, vector_steps.n)
                            nc.vector.tensor_tensor(invT[:, :, :], wideI, wide[:, :, :], ALU.subtract).then_inc(masked.up(), 1)
                            dve.wait_ge(turned0.sem, turned0.at(1))
                            for b in range(2):
                                nc.vector.tensor_copy(halves(inv)[b], bank[1 + b][:, :]).then_inc(vector_steps.up(), 1)
                                dve.wait_ge(vector_steps.sem, vector_steps.n)
                            for n in range(1, LEVELS):
                                nc.vector.tensor_tensor(wide[:, :, :], lower[:, :, :], level(n).unsqueeze(1).to_broadcast([P, U, P]), ALU.mult).then_inc(level_in.up(), 1)
                                dve.wait_ge(x_ready.sem, x_ready.at(n))
                                for b in range(2):
                                    ins = nc.vector.tensor_copy(halves(step)[b], bank[1 + b][:, :])
                                ins.then_inc(x_copied.up(), 1)
                                dve.wait_ge(x2_ready.sem, x2_ready.at(n))
                                for b in range(2):
                                    nc.vector.tensor_tensor(halves(invT)[b], halves(invT)[b], bank[3 + b][:, :], ALU.subtract).then_inc(vector_steps.up(), 1)
                                    dve.wait_ge(vector_steps.sem, vector_steps.n)
                                    if n < LEVELS - 1:
                                        nc.vector.tensor_tensor(halves(inv)[b], halves(inv)[b], bank[5 + b][:, :], ALU.subtract).then_inc(vector_steps.up(), 1)
                                        dve.wait_ge(vector_steps.sem, vector_steps.n)

                        @block.tensor
                        def _(pe):
                            pe.wait_ge(g_ready.sem, g_ready.at(1))
                            for t in range(TT):
                                nc.tensor.matmul(bank[0][:, t * H:(t + 1) * H], triu, g[:, t * H:(t + 1) * H], start=True, stop=True)
                            for u in range(U):
                                last = nc.tensor.matmul(bank[1 + u // H][:, (u % H) * P:(u % H + 1) * P], wide[:, u, :], triu, start=True, stop=True)
                            last.then_inc(cum.up(), 1)
                            for u in range(U):
                                nc.tensor.matmul(bank[3 + u // H][:, (u % H) * P:(u % H + 1) * P], kT(u), kT(u), start=True, stop=True)
                                nc.tensor.matmul(bank[5 + u // H][:, (u % H) * P:(u % H + 1) * P], kT(u), qT(u), start=True, stop=True)
                            pe.wait_ge(decayed.sem, decayed.at(1))
                            for u in range(U):
                                last = nc.tensor.matmul(bank[(7, 0)[u // H]][:, (u % H) * P:(u % H + 1) * P], step[:, u, :], ident, start=True, stop=True)
                            last.then_inc(products.up(), 1)
                            pe.wait_ge(masked.sem, masked.at(1))
                            for u in range(U):
                                last = nc.tensor.transpose(bank[1 + u // H][:, (u % H) * P:(u % H + 1) * P], invT[:, u, :], ident)
                            last.then_inc(turned0.up(), 1)
                            for n in range(1, LEVELS):
                                pe.wait_ge(level_in.sem, level_in.at(n))
                                for u in range(U):
                                    last = nc.tensor.matmul(bank[1 + u // H][:, (u % H) * P:(u % H + 1) * P], wide[:, u, :], inv[:, u, :], start=True, stop=True)
                                last.then_inc(x_ready.up(), 1)
                                pe.wait_ge(x_copied.sem, x_copied.at(n))
                                for u in range(U):
                                    cols = slice((u % H) * P, (u % H + 1) * P)
                                    last = nc.tensor.matmul(bank[3 + u // H][:, cols], step[:, u, :], invT[:, u, :], start=True, stop=True)
                                    if n < LEVELS - 1:
                                        last = nc.tensor.matmul(bank[5 + u // H][:, cols], invT[:, u, :], step[:, u, :], start=True, stop=True)
                                last.then_inc(x2_ready.up(), 1)

                with ExitStack() as st_o:
                    ktok = sb(st_o, "ktok", [P, U, P])
                    vtok = sb(st_o, "vtok", [P, U, P])
                    kd = sb(st_o, "kd", [P, H, P])
                    wT = sb(st_o, "wT", [P, H, P])
                    state = sb(st_o, "state", [P, H, P])
                    vnew = sb(st_o, "vnew", [P, U, P])
                    norm_row = sb(st_o, "gdn_norm_row", [P, P])
                    turned, scaled = signal("gdn_kv_turned"), signal("gdn_kv_scaled")
                    u_ready, v0_ready, s_ready, s_copied = signal("gdn_u_ready"), signal("gdn_v0_ready"), signal("gdn_state_ready"), signal("gdn_state_copied")
                    ws_ready, v1_ready, o_ready = signal("gdn_ws_ready"), signal("gdn_v1_ready"), signal("heads_out_ready")
                    ms_ready, root, row_in, z_ready = signal("mean_square_ready"), signal("root_ready"), signal("gain_row_in"), signal("silu_gate_ready")

                    def unit_cols(b0, u):
                        return bank[b0 + u // H][:, (u % H) * P:(u % H + 1) * P]

                    def half(t, b):
                        return t[:, 4 * b:4 * b + 4, :]

                    def psum3(b):
                        return bank[b][:, :].rearrange("p (u i) -> p u i", u=4)

                    with nc.Block() as block:
                        @block.tensor
                        def _(pe):
                            for u in range(U):
                                nc.tensor.transpose(unit_cols(0, u), kT(u), ident)
                                vT = conv[:, 2 * H + u % H, (u // H) * P:(u // H + 1) * P]
                                last = nc.tensor.transpose(unit_cols(2, u), vT, ident)
                            last.then_inc(turned.up(), 1)
                            pe.wait_ge(scaled.sem, scaled.at(1))
                            for u in range(U):
                                nc.tensor.matmul(unit_cols(4, u), invT[:, u, :], vtok[:, u, :], start=True, stop=True)
                            for h in range(H):
                                last = nc.tensor.matmul(unit_cols(6, h), ktok[:, H + h, :], invT[:, H + h, :], start=True, stop=True)
                            last.then_inc(u_ready.up(), 1)
                            pe.wait_ge(v0_ready.sem, v0_ready.at(1))
                            for h in range(H):
                                last = nc.tensor.matmul(unit_cols(7, h), kd[:, h, :], vnew[:, h, :], start=True, stop=True)
                            last.then_inc(s_ready.up(), 1)
                            for h in range(H):
                                nc.tensor.matmul(unit_cols(0, h), aqk[:, h, :], vnew[:, h, :], start=True, stop=True)
                            pe.wait_ge(s_copied.sem, s_copied.at(1))
                            for h in range(H):
                                last = nc.tensor.matmul(unit_cols(2, h), wT[:, h, :], state[:, h, :], start=True, stop=True)
                            last.then_inc(ws_ready.up(), 1)
                            pe.wait_ge(v1_ready.sem, v1_ready.at(1))
                            for h in range(H):
                                nc.tensor.matmul(unit_cols(1, h), qg[:, h, :], state[:, h, :], start=True, stop=False)
                                last = nc.tensor.matmul(unit_cols(1, h), aqk[:, H + h, :], vnew[:, H + h, :], start=False, stop=True)
                            last.then_inc(o_ready.up(), 1)

                        @block.vector
                        def _(dve):
                            nc.vector.tensor_tensor(qg[:, :, :], qg[:, :, :], conv[:, 0:H, P:2 * P], ALU.mult).then_inc(vector_steps.up(), 1)
                            dve.wait_ge(vector_steps.sem, vector_steps.n)
                            dve.wait_ge(turned.sem, turned.at(1))
                            nc.vector.tensor_tensor(tmp, beta, egc, ALU.mult).then_inc(vector_steps.up(), 1)
                            dve.wait_ge(vector_steps.sem, vector_steps.n)
                            nc.vector.tensor_tensor(kd[:, :, :], psum3(0), kscale[:, 0:H].unsqueeze(2).to_broadcast([P, H, P]), ALU.mult).then_inc(vector_steps.up(), 1)
                            dve.wait_ge(vector_steps.sem, vector_steps.n)
                            for b in range(2):
                                nc.vector.tensor_tensor(half(ktok, b), psum3(b), tmp[:, 4 * b:4 * b + 4].unsqueeze(2).to_broadcast([P, H, P]), ALU.mult).then_inc(vector_steps.up(), 1)
                                dve.wait_ge(vector_steps.sem, vector_steps.n)
                                ins = nc.vector.tensor_tensor(half(vtok, b), psum3(2 + b), beta[:, 4 * b:4 * b + 4].unsqueeze(2).to_broadcast([P, H, P]), ALU.mult)
                            ins.then_inc(scaled.up(), 1)
                            dve.wait_ge(u_ready.sem, u_ready.at(1))
                            nc.vector.tensor_copy(wT[:, :, :], psum3(6)).then_inc(vector_steps.up(), 1)
                            dve.wait_ge(vector_steps.sem, vector_steps.n)
                            nc.vector.tensor_copy(half(vnew, 0), psum3(4)).then_inc(v0_ready.up(), 1)
                            nc.vector.tensor_copy(half(vnew, 1), psum3(5)).then_inc(vector_steps.up(), 1)
                            dve.wait_ge(vector_steps.sem, vector_steps.n)
                            dve.wait_ge(s_ready.sem, s_ready.at(1))
                            nc.vector.tensor_copy(state[:, :, :], psum3(7)).then_inc(s_copied.up(), 1)
                            dve.wait_ge(ws_ready.sem, ws_ready.at(1))
                            nc.vector.tensor_tensor(half(vnew, 1), half(vnew, 1), psum3(2), ALU.subtract).then_inc(v1_ready.up(), 1)
                            dve.wait_ge(o_ready.sem, o_ready.at(1))
                            for t in range(TT):
                                om = mixed[:, t, 0:512].rearrange("p (h d) -> p h d", h=H)
                                nc.vector.tensor_copy(om, psum3(t)).then_inc(vector_steps.up(), 1)
                                dve.wait_ge(vector_steps.sem, vector_steps.n)
                                nc.vector.tensor_tensor(half(vtok, t), om, om, ALU.mult).then_inc(vector_steps.up(), 1)
                                dve.wait_ge(vector_steps.sem, vector_steps.n)
                            nc.vector.tensor_reduce(tmp, vtok[:, :, :], AX.X, ALU.add).then_inc(vector_steps.up(), 1)
                            dve.wait_ge(vector_steps.sem, vector_steps.n)
                            nc.vector.tensor_scalar(tmp, tmp, 1.0 / P, EPS, ALU.mult, ALU.add).then_inc(ms_ready.up(), 1)
                            dve.wait_ge(root.sem, root.at(1))
                            dve.wait_ge(z_ready.sem, z_ready.at(1))
                            dve.wait_ge(row_in.sem, row_in.at(16))
                            nc.vector.reciprocal(tmp2, tmp2).then_inc(vector_steps.up(), 1)
                            dve.wait_ge(vector_steps.sem, vector_steps.n)
                            for t in range(TT):
                                om = mixed[:, t, 0:512].rearrange("p (h d) -> p h d", h=H)
                                nc.vector.tensor_tensor(om, om, tmp2[:, t * H:(t + 1) * H].unsqueeze(2).to_broadcast([P, H, P]), ALU.mult).then_inc(vector_steps.up(), 1)
                                dve.wait_ge(vector_steps.sem, vector_steps.n)
                                nc.vector.tensor_tensor(om, om, norm_row[:, :].unsqueeze(1).to_broadcast([P, H, P]), ALU.mult).then_inc(vector_steps.up(), 1)
                                dve.wait_ge(vector_steps.sem, vector_steps.n)
                                nc.vector.tensor_tensor(mixed[:, t, 0:512], mixed[:, t, 0:512], za[:, t, :], ALU.mult).then_inc(vector_steps.up(), 1)
                                dve.wait_ge(vector_steps.sem, vector_steps.n)

                        @block.scalar
                        def _(act):
                            act.dma_start(norm_row[:, :], A["gdn_out_norm"][0].partition_broadcast(P)).then_inc(row_in.up(16), 16)
                            nc.scalar.activation(za[:, :, :], za[:, :, :], ACT.Silu).then_inc(z_ready.up(), 1)
                            act.wait_ge(ms_ready.sem, ms_ready.at(1))
                            nc.scalar.activation(tmp2, tmp, ACT.Sqrt).then_inc(root.up(), 1)

        def routing_stage(layer, st, gate_free, routes):
            gains, slots, row, most = routes
            wr = sb(st, "router_w", [P, KD, GROUPS + EXPERTS])
            br = sb(st, "router_b", [1, GROUPS + EXPERTS])
            g8 = sb(st, "group_logits", [P, TT, 8])
            el = sb(st, "expert_logits", [P, TT, EXPERTS])
            best = sb(st, "best", [P, TT, 2, 8])
            index = sb(st, "index", [P, TT, 2, 8], U32)
            indexf = sb(st, "indexf", [P, TT, 2, 8])
            stat = sb(st, "route_stat", [P, TT, 8])
            gexp = sb(st, "group_exp", [P, TT, GROUPS])
            weight = sb(st, "expert_weight", [P, TT, 2, EXPERTS])
            choice = sb(st, "expert_choice", [P, TT, 3, EXPERTS])
            place = sb(st, "expert_place", [P, TT, EXPERTS])
            rowf = sb(st, "expert_row", [P, TT, 2])
            mostf = sb(st, "expert_most", [P, 1])
            rows = sb(st, "weight_rows", [EXPERTS, T])
            w_in, logits, shifted, exped = signal("operands_in"), signal("router_logits"), signal("route_max_ready"), signal("route_exp_ready")
            chosen, ranked = signal("experts_chosen"), signal("tokens_ranked")
            weighed, turned, rows_ready, stored = signal("route_weighed"), signal("route_turned"), signal("gate_rows_ready"), signal("gate_rows_stored")
            with nc.Block() as block:
                @block.scalar
                def _(act):
                    act.dma_start(wr[:, :, 0:GROUPS], A["router_group_w"][layer].rearrange("(k p) g -> p k g", p=P)).then_inc(w_in.up(16), 16)
                    for g in range(GROUPS):
                        at = GROUPS + PER_GROUP * g
                        act.dma_start(wr[:, :, at:at + PER_GROUP], A["router_exp_w"][layer, g].rearrange("(k p) e -> p k e", p=P)).then_inc(w_in.up(16), 16)
                    act.dma_start(br[:, 0:GROUPS], A["router_group_b"][layer:layer + 1, :]).then_inc(w_in.up(16), 16)
                    act.dma_start(br[:, GROUPS:], A["router_exp_b"][layer:layer + 1].rearrange("a g e -> a (g e)")).then_inc(w_in.up(16), 16)
                    act.wait_ge(shifted.sem, shifted.at(1))
                    for t in range(TT):
                        nc.scalar.activation(gexp[:, t, :], g8[:, t, 0:GROUPS], ACT.Exp, bias=stat[:, t, 0:1], accum_out=stat[:, t, 1:2])
                        ins = nc.scalar.activation(stat[:, t, 3:4], stat[:, t, 2:3], ACT.Exp)
                    ins.then_inc(exped.up(), 1)
                    act.wait_ge(rows_ready.sem, rows_ready.at(1))
                    act.dma_start(gate_rows[layer], rows[:, :]).then_inc(stored.up(16), 16)

                @block.tensor
                def _(pe):
                    pe.wait_ge(w_in.sem, w_in.at(16 * (GROUPS + 3)))
                    for t in range(TT):
                        acc = bank[t][:, 0:GROUPS + EXPERTS]
                        nc.tensor.matmul(acc, ones[0:1, :], br[:, :], start=True, stop=False)
                        for k in range(KD):
                            last = nc.tensor.matmul(acc, hT[:, k, t * P:(t + 1) * P], wr[:, k, :], start=False, stop=(k == KD - 1))
                    last.then_inc(logits.up(), 1)
                    pe.wait_ge(chosen.sem, chosen.at(1))
                    for t in range(TT):
                        for b in range(t + 1):
                            nc.tensor.matmul(bank[3][:, t * EXPERTS:(t + 1) * EXPERTS], triu if b == t else ones, choice[:, b, 2, :],
                                             start=(b == 0), stop=(b == t))
                    for b in range(TT):
                        last = nc.tensor.matmul(bank[3][:, TT * EXPERTS:(TT + 1) * EXPERTS], ones, choice[:, b, 2, :],
                                                start=(b == 0), stop=(b == TT - 1))
                    last.then_inc(ranked.up(), 1)
                    pe.wait_ge(weighed.sem, weighed.at(1))
                    for t in range(TT):
                        last = nc.tensor.transpose(bank[2][0:EXPERTS, t * P:(t + 1) * P], weight[:, t, 0, :], ident)
                    last.then_inc(turned.up(), 1)

                @block.vector
                def _(dve):
                    nc.vector.memset(g8[:, :, :], NEG).then_inc(vector_steps.up(), 1)
                    dve.wait_ge(vector_steps.sem, vector_steps.n)
                    dve.wait_ge(logits.sem, logits.at(1))
                    for t in range(TT):
                        nc.vector.tensor_copy(g8[:, t, 0:GROUPS], bank[t][:, 0:GROUPS]).then_inc(vector_steps.up(), 1)
                        dve.wait_ge(vector_steps.sem, vector_steps.n)
                        nc.vector.max(best[:, t, 0, :], g8[:, t, :]).then_inc(vector_steps.up(), 1)
                        dve.wait_ge(vector_steps.sem, vector_steps.n)
                        nc.vector.max_index(index[:, t, 0, :], best[:, t, 0, :], g8[:, t, :]).then_inc(vector_steps.up(), 1)
                        dve.wait_ge(vector_steps.sem, vector_steps.n)
                        nc.vector.tensor_copy(indexf[:, t, 0, :], index[:, t, 0, :]).then_inc(vector_steps.up(), 1)
                        dve.wait_ge(vector_steps.sem, vector_steps.n)
                        nc.vector.tensor_scalar(el[:, t, :], group_of, indexf[:, t, 0, 0:1], NEG, ALU.not_equal, ALU.mult).then_inc(vector_steps.up(), 1)
                        dve.wait_ge(vector_steps.sem, vector_steps.n)
                        nc.vector.tensor_tensor(el[:, t, :], el[:, t, :], bank[t][:, GROUPS:GROUPS + EXPERTS], ALU.add).then_inc(vector_steps.up(), 1)
                        dve.wait_ge(vector_steps.sem, vector_steps.n)
                        nc.vector.max(best[:, t, 1, :], el[:, t, :]).then_inc(vector_steps.up(), 1)
                        dve.wait_ge(vector_steps.sem, vector_steps.n)
                        nc.vector.max_index(index[:, t, 1, :], best[:, t, 1, :], el[:, t, :]).then_inc(vector_steps.up(), 1)
                        dve.wait_ge(vector_steps.sem, vector_steps.n)
                        nc.vector.tensor_copy(indexf[:, t, 1, :], index[:, t, 1, :]).then_inc(vector_steps.up(), 1)
                        dve.wait_ge(vector_steps.sem, vector_steps.n)
                        nc.vector.tensor_scalar(stat[:, t, 0:1], best[:, t, 0, 0:1], -1.0, None, ALU.mult).then_inc(vector_steps.up(), 1)
                        dve.wait_ge(vector_steps.sem, vector_steps.n)
                        ins = nc.vector.tensor_tensor(stat[:, t, 2:3], best[:, t, 1, 1:2], best[:, t, 1, 0:1], ALU.subtract)
                    ins.then_inc(shifted.up(), 1)
                    for t in range(TT):
                        for n in range(2):
                            ins = nc.vector.tensor_scalar(choice[:, t, n, :], iota, indexf[:, t, 1, n:n + 1], None, ALU.is_equal)
                    ins.then_inc(vector_steps.up(), 1)
                    dve.wait_ge(vector_steps.sem, vector_steps.n)
                    nc.vector.tensor_tensor(choice[:, :, 2, :], choice[:, :, 0, :], choice[:, :, 1, :], ALU.add).then_inc(chosen.up(), 1)
                    dve.wait_ge(ranked.sem, ranked.at(1))
                    dve.wait_ge(chosen.sem, chosen.n)
                    placed = bank[3][:, 0:TT * EXPERTS].rearrange("p (t e) -> p t e", t=TT)
                    nc.vector.memset(slots[:, :, EXPERTS:], 0.0)
                    nc.vector.tensor_tensor(slots[:, :, 0:EXPERTS], placed, choice[:, :, 2, :], ALU.mult)
                    nc.vector.tensor_reduce(mostf[:, :], bank[3][:, TT * EXPERTS:(TT + 1) * EXPERTS], AX.X, ALU.max)
                    nc.vector.scalar_tensor_tensor(place[:, :, :], iota.unsqueeze(1).to_broadcast([P, TT, EXPERTS]), float(CAP), placed,
                                                   ALU.mult, ALU.add).then_inc(vector_steps.up(), 1)
                    dve.wait_ge(vector_steps.sem, vector_steps.n)
                    nc.vector.tensor_copy(most[:, :], mostf[:, :])
                    nc.vector.tensor_tensor(choice[:, :, 0:2, :], choice[:, :, 0:2, :], place[:, :, :].unsqueeze(2).to_broadcast([P, TT, 2, EXPERTS]),
                                            ALU.mult).then_inc(vector_steps.up(), 1)
                    dve.wait_ge(vector_steps.sem, vector_steps.n)
                    nc.vector.tensor_reduce(rowf[:, :, :], choice[:, :, 0:2, :], AX.X, ALU.add).then_inc(vector_steps.up(), 1)
                    dve.wait_ge(vector_steps.sem, vector_steps.n)
                    nc.vector.tensor_scalar(rowf[:, :, :], rowf[:, :, :], -1.0, None, ALU.add).then_inc(vector_steps.up(), 1)
                    dve.wait_ge(vector_steps.sem, vector_steps.n)
                    nc.vector.tensor_copy(row[:, :, :], rowf[:, :, :]).then_inc(vector_steps.up(), 1)
                    dve.wait_ge(vector_steps.sem, vector_steps.n)
                    dve.wait_ge(exped.sem, exped.at(1))
                    for t in range(TT):
                        nc.vector.tensor_scalar(stat[:, t, 4:5], stat[:, t, 3:4], 1.0, stat[:, t, 1:2], ALU.add, ALU.mult).then_inc(vector_steps.up(), 1)
                        dve.wait_ge(vector_steps.sem, vector_steps.n)
                        nc.vector.reciprocal(stat[:, t, 5:6], stat[:, t, 4:5]).then_inc(vector_steps.up(), 1)
                        dve.wait_ge(vector_steps.sem, vector_steps.n)
                        nc.vector.tensor_tensor(stat[:, t, 6:7], stat[:, t, 5:6], stat[:, t, 3:4], ALU.mult).then_inc(vector_steps.up(), 1)
                        dve.wait_ge(vector_steps.sem, vector_steps.n)
                        for n in range(2):
                            nc.vector.tensor_scalar(weight[:, t, n, :], iota, indexf[:, t, 1, n:n + 1], stat[:, t, 5 + n:6 + n],
                                                             ALU.is_equal, ALU.mult).then_inc(vector_steps.up(), 1)
                            dve.wait_ge(vector_steps.sem, vector_steps.n)
                        ins = nc.vector.tensor_tensor(weight[:, t, 0, :], weight[:, t, 0, :], weight[:, t, 1, :], ALU.add)
                    ins.then_inc(weighed.up(), 1)
                    nc.vector.tensor_copy(gains[:, :, :], stat[:, :, 5:7]).then_inc(vector_steps.up(), 1)
                    dve.wait_ge(vector_steps.sem, vector_steps.n)
                    dve.wait_ge(turned.sem, turned.at(1))
                    nc.vector.memset(stat[:, :, 7], 0.0).then_inc(gate_free.up(), 1)
                    nc.vector.memset(best[:, 0, 0, 0:1], 0.0).then_inc(gate_free.up(), 1)
                    nc.vector.tensor_copy(rows[:, :], bank[2][0:EXPERTS, 0:T]).then_inc(rows_ready.up(), 1)

                @block.gpsimd
                def _(pool):
                    pool.wait_ge(stored.sem, stored.at(16))

        def experts_stage(layer, gates, xn, gain, shift):
            c0 = first[f"experts{layer}"]
            PAIRS = EXPERTS // 2

            def layer_signal(name):
                return signal(f"{name}{layer}")

            with ExitStack() as st:
                gains = sb(st, "route_gains", [P, TT, 2])
                slots = sb(st, "route_slots", [P, TT, EXPERTS + 2])
                row = sb(st, "route_rows", [P, TT, 2], I32)
                most = sb(st, "route_most", [P, 1], I32)
                hid_free = layer_signal("hidden_free")
                with ExitStack() as st_r:
                    routing_stage(layer, st_r, hid_free, (gains, slots, row, most))
                hid_ready, y_done = layer_signal("hidden_ready"), layer_signal("expert_out_ready")
                gate_b = sb(st, "gate_b", [P, 2, T])
                act_h = sb(st, "silu_h", [P, 2, T])
                gated = sb(st, "gated_h", [P, 2, T])
                hid = sb(st, "hidden", [P, FT, T])
                zero = sb(st, "zero", [P, 512])
                gate_in = [layer_signal(f"gate{q}_in_") for q in range(2)]
                silu_done, gated_done = layer_signal("silu_done"), layer_signal("gated_done")
                zeroed, summed, sum_steps = layer_signal("zero_ready"), layer_signal("experts_summed"), layer_signal("sum_steps")
                y = [[bank[4 + 2 * t + half] for half in range(2)] for t in range(TT)]
                member = sb(st, "member", [P, 2, TT, CAP])
                own_rows = sb(st, "own_rows", [P, 512])
                own = sb(st, "own_tokens", [P, 2, KD // 2, 2, CAP])
                own_silu = sb(st, "own_silu", [P, 2, FE // 2])
                own_hid = sb(st, "own_hidden", [P, FE // 2])
                own_hidT = sb(st, "own_hiddenT", [P, 2, FT // 2, 2, CAP])
                own_y = sb(st, "own_out", [P, 2, 512])
                taken = sb(st, "taken_rows", [P, TT, 2, D])
                member_ready, sorted_out, rows_copied = layer_signal("member_ready"), layer_signal("tokens_sorted"), layer_signal("own_rows_copied")
                rows_turned, own_scaled, own_ready = layer_signal("own_rows_turned"), layer_signal("own_tokens_scaled"), layer_signal("own_tokens_ready")
                own_silu_done, own_hid_done = layer_signal("own_silu_done"), layer_signal("own_hidden_done")
                hid_turned, hidT_ready = layer_signal("own_hidden_turned"), layer_signal("own_hiddenT_ready")
                y_copied, taken_in, merge_steps = layer_signal("own_out_copied"), layer_signal("rows_taken"), layer_signal("merge_steps")
                y_stored = [layer_signal(f"own_out{q}_stored_") for q in range(2)]

                frees_from = [(hid_ready, lambda e: hid_ready.start + FT * (e + 1)), (hid_ready, lambda e: hid_ready.start + FT * (e + 1)),
                              (y_done, lambda e: y_done.start + e + 1)]
                base = {j: landed_at[c0 + j] for j in range(RING)}
                for j in range(3 * EXPERTS):
                    s, n = frees_from[j % 3]
                    freed[c0 + j] = (s.sem, n(j // 3))
                with nc.Block() as block:
                    @block.sync
                    def _(sp):
                        fill_ring(sp, c0 - 1)
                        with sp.Fori(0, PAIRS - 1) as i:
                            for j in range(RING):
                                q, part = j // 3, j % 3
                                e = 2 * i + q
                                s, n = frees_from[part]
                                sp.wait_ge(s.sem, n(e))
                                name = ("exp_w1", "exp_w3", "exp_w2")[part]
                                src = A[name][layer].rearrange("e r n -> (e r) n")
                                nrow = A[name].shape[2]
                                src = src[bass.ds((e + 2) * nrow, nrow), :].rearrange("(k p) n -> p k n", p=P)
                                sp.dma_start(slot(c0 + j), src).then_inc(landed[(c0 + j) % RING].sem, 16)
                        for j in range(RING):
                            landed[(c0 + j) % RING].n += 16 * (PAIRS - 1)
                        issued[0] = c0 + 3 * EXPERTS
                        fill_ring(sp, c0 + 3 * EXPERTS - 1)

                    @block.gpsimd
                    def _(pool):
                        fullest = pool.value_load(most[0:1, 0:1], min_val=0, max_val=T)
                        with pool.If(fullest > CAP):
                            for q in range(2):
                                pool.dma_start(gate_b[:, q, :], gate_rows[layer, q].partition_broadcast(P)).then_inc(gate_in[q].up(16), 16)
                            flat_rows = gate_rows[layer].rearrange("e t -> (e t)")
                            with pool.Fori(0, PAIRS - 1) as i:
                                for q in range(2):
                                    e = 2 * i + q
                                    pool.wait_ge(hid_free.sem, hid_free.start + 2 + FT * (e + 1))
                                    pool.dma_start(gate_b[:, q, :], flat_rows[bass.ds((e + 2) * T, T)].partition_broadcast(P))\
                                        .then_inc(gate_in[q].sem, 16)
                        with pool.Else():
                            for q in range(2):
                                pool.wait_ge(y_stored[q].sem, 2 * 16 * PAIRS)
                            for t in range(TT):
                                for n in range(2):
                                    pool.indirect_dma_start(taken[:, t, n, :], None, expert_out[layer],
                                                            bass.IndirectOffsetOnAxis(ap=row[:, t, n:n + 1], axis=0)).then_inc(taken_in.sem, 16)

                    @block.tensor
                    def _(pe):
                        fullest = pe.value_load(most[0:1, 0:1], min_val=0, max_val=T)
                        with pe.If(fullest > CAP):
                            pe.wait_ge(zeroed.sem, 1)
                            for t in range(TT):
                                for half in range(2):
                                    nc.tensor.matmul(y[t][half][:, :], zero[:, 0:P], zero[:, :], start=True, stop=False)
                            with pe.Fori(0, PAIRS) as i:
                                for q in range(2):
                                    e = 2 * i + q
                                    w1, w3, w2 = (slot(c0 + 3 * q + part) for part in range(3))
                                    for part in range(2):
                                        pe.wait_ge(landed[(c0 + 3 * q + part) % RING].sem, base[3 * q + part] + 16 * i)
                                    for f in range(FT):
                                        pe.wait_ge(hid_free.sem, hid_free.start + FT * e + f + 1)
                                        for w, b in ((w1, f % 2), (w3, 2 + f % 2)):
                                            for k in range(KD):
                                                last = nc.tensor.matmul(bank[b][:, 0:T], w[:, k, f * P:(f + 1) * P], hT[:, k, :],
                                                                        start=(k == 0), stop=(k == KD - 1))
                                        last.then_inc(hid_ready.sem, 1)
                                    pe.wait_ge(landed[(c0 + 3 * q + 2) % RING].sem, base[3 * q + 2] + 16 * i)
                                    for f in range(FT):
                                        pe.wait_ge(hid_free.sem, hid_free.start + 2 + FT * e + f + 1)
                                        for t in range(TT):
                                            for half in range(2):
                                                last = nc.tensor.matmul(y[t][half][:, :], hid[:, f, t * P:(t + 1) * P],
                                                                        w2[:, f, half * 512:(half + 1) * 512], start=False, stop=False,
                                                                        skip_group_check=True)
                                    last.then_inc(y_done.sem, 1)
                            for t in range(TT):
                                for half in range(2):
                                    last = nc.tensor.matmul(y[t][half][:, :], zero[:, 0:P], zero[:, :], start=False, stop=True)
                            last.then_inc(summed.sem, 1)
                        with pe.Else():
                            halves = [slice(0, CAP), slice(CAP, 2 * CAP)]

                            def sort_tokens(e, q):
                                pe.wait_ge(member_ready.sem, e + 1)
                                for t in range(TT):
                                    for half in range(2):
                                        last = nc.tensor.matmul(bank[0][halves[half], :], member[:, q, t, :],
                                                                xn[:, t, half * 512:(half + 1) * 512], start=(t == 0), stop=(t == TT - 1))
                                last.then_inc(sorted_out.sem, 1)

                            def turn_tokens(e):
                                pe.wait_ge(rows_copied.sem, e + 1)
                                for c in range(KD // 2):
                                    last = nc.tensor.transpose(bank[1][:, c * P:(c + 1) * P], own_rows[:, c * P:(c + 1) * P], ident)
                                last.then_inc(rows_turned.sem, 1)

                            def two_experts(i, peeled):
                                for q in range(2):
                                    e = 2 * i + q
                                    w1, w3, w2 = (slot(c0 + 3 * q + part) for part in range(3))
                                    pe.wait_ge(own_ready.sem, e + 1)
                                    for part, w in enumerate((w1, w3)):
                                        pe.wait_ge(landed[(c0 + 3 * q + part) % RING].sem, base[3 * q + part] + 16 * i)
                                        for k in range(KD):
                                            for half in range(2):
                                                cols = slice(half * FE // 2, (half + 1) * FE // 2)
                                                last = nc.tensor.matmul(bank[2 + q][halves[half], part * FE // 2:(part + 1) * FE // 2],
                                                                        own[:, q, k % 4, k // 4, :], w[:, k, cols],
                                                                        start=(k == 0), stop=(k == KD - 1))
                                    last.then_inc(hid_ready.sem, FT)
                                    sort_tokens(e + 1, 1 - q)
                                    pe.wait_ge(own_hid_done.sem, e + 1)
                                    for c in range(FT // 2):
                                        last = nc.tensor.transpose(bank[4][:, c * P:(c + 1) * P], own_hid[:, c * P:(c + 1) * P], ident)
                                    last.then_inc(hid_turned.sem, 1)
                                    turn_tokens(e + 1)
                                    pe.wait_ge(landed[(c0 + 3 * q + 2) % RING].sem, base[3 * q + 2] + 16 * i)
                                    pe.wait_ge(hidT_ready.sem, e + 1)
                                    if not peeled:
                                        pe.wait_ge(y_copied.sem, e - 1)
                                    for f in range(FT):
                                        for half in range(2):
                                            last = nc.tensor.matmul(bank[5 + q][halves[half], :], own_hidT[:, q, f % 2, f // 2, :],
                                                                    w2[:, f, half * 512:(half + 1) * 512], start=(f == 0), stop=(f == FT - 1))
                                    last.then_inc(y_done.sem, 1)

                            sort_tokens(0, 0)
                            turn_tokens(0)
                            two_experts(0, True)
                            with pe.Fori(1, PAIRS) as i:
                                two_experts(i, False)
                        hid_ready.n += FT * EXPERTS
                        y_done.n += EXPERTS

                    @block.scalar
                    def _(act):
                        fullest = act.value_load(most[0:1, 0:1], min_val=0, max_val=T)
                        with act.If(fullest > CAP):
                            with act.Fori(0, PAIRS) as i:
                                for q in range(2):
                                    for f in range(FT):
                                        u = FT * (2 * i + q) + f
                                        act.wait_ge(hid_ready.sem, hid_ready.start + u + 1)
                                        act.wait_ge(hid_free.sem, hid_free.start + u + 1)
                                        nc.scalar.activation(act_h[:, f % 2, :], bank[f % 2][:, 0:T], ACT.Silu).then_inc(silu_done.sem, 1)
                        with act.Else():
                            def copy_rows(e):
                                act.wait_ge(sorted_out.sem, e + 1)
                                nc.scalar.copy(own_rows[:, :], bank[0][:, :]).then_inc(rows_copied.sem, 1)

                            copy_rows(0)
                            with act.Fori(0, PAIRS) as i:
                                for q in range(2):
                                    e = 2 * i + q
                                    act.wait_ge(hid_ready.sem, FT * (e + 1))
                                    nc.scalar.activation(own_silu[:, q, :], bank[2 + q][:, 0:FE // 2], ACT.Silu).then_inc(own_silu_done.sem, 1)
                                    copy_rows(e + 1)
                                    act.wait_ge(y_copied.sem, e + 1)
                                    for half in range(2):
                                        act.dma_start(expert_out[layer][bass.ds(e * CAP, CAP), half * 512:(half + 1) * 512],
                                                      own_y[half * CAP:(half + 1) * CAP, q, :]).then_inc(y_stored[q].sem, 16)

                    @block.vector
                    def _(dve):
                        fullest = dve.value_load(most[0:1, 0:1], min_val=0, max_val=T)
                        with dve.If(fullest > CAP):
                            nc.vector.memset(zero[:, :], 0.0).then_inc(zeroed.sem, 1)
                            with dve.Fori(0, PAIRS) as i:
                                for q in range(2):
                                    dve.wait_ge(gate_in[q].sem, 16 * (i + 1))
                                    for f in range(FT):
                                        u = FT * (2 * i + q) + f
                                        dve.wait_ge(hid_ready.sem, hid_ready.start + u + 1)
                                        nc.vector.tensor_tensor(gated[:, f % 2, :], bank[2 + f % 2][:, 0:T], gate_b[:, q, :], ALU.mult)\
                                            .then_inc(gated_done.sem, 1)
                                        dve.wait_ge(gated_done.sem, u + 1)
                                        dve.wait_ge(silu_done.sem, u + 1)
                                        nc.vector.tensor_tensor(hid[:, f, :], gated[:, f % 2, :], act_h[:, f % 2, :], ALU.mult).then_inc(hid_free.sem, 1)
                            dve.wait_ge(summed.sem, 1)
                            for t in range(TT):
                                for half in range(2):
                                    cols = slice(half * 512, (half + 1) * 512)
                                    nc.vector.tensor_tensor(zero[:, :], y[t][half][:, :], gates[:, 1, cols], ALU.mult).then_inc(sum_steps.up(), 1)
                                    dve.wait_ge(sum_steps.sem, sum_steps.n)
                                    nc.vector.tensor_tensor(x[:, t, cols], x[:, t, cols], zero[:, :], ALU.add).then_inc(sum_steps.up(), 1)
                                    dve.wait_ge(sum_steps.sem, sum_steps.n)
                        with dve.Else():
                            def find_members(e, q):
                                shape = [P, TT, CAP]
                                nc.vector.tensor_tensor(member[:, q], slots[:, :, bass.ds(e, 1)].to_broadcast(shape),
                                                        slot_number.unsqueeze(1).to_broadcast(shape), ALU.is_equal).then_inc(member_ready.sem, 1)

                            def own_tokens(e, q):
                                tiles = [P, KD // 2, 2, CAP]

                                def tile_columns(a):
                                    return a.rearrange("p (h c) -> p c h", h=2).unsqueeze(3).to_broadcast(tiles)
                                dve.wait_ge(rows_turned.sem, e + 1)
                                nc.vector.tensor_tensor(own[:, q], bank[1][:, :].rearrange("p (c h s) -> p c h s", c=KD // 2, h=2),
                                                        tile_columns(gain), ALU.mult).then_inc(own_scaled.sem, 1)
                                dve.wait_ge(own_scaled.sem, e + 1)
                                nc.vector.tensor_tensor(own[:, q], own[:, q], tile_columns(shift), ALU.add).then_inc(own_ready.sem, 1)

                            def two_experts(i, peeled):
                                for q in range(2):
                                    e = 2 * i + q
                                    dve.wait_ge(own_silu_done.sem, e + 1)
                                    nc.vector.tensor_tensor(own_hid[:, :], bank[2 + q][:, FE // 2:], own_silu[:, q, :],
                                                            ALU.mult).then_inc(own_hid_done.sem, 1)
                                    dve.wait_ge(hid_turned.sem, e + 1)
                                    nc.vector.tensor_copy(own_hidT[:, q].rearrange("p c h s -> p (c h s)"),
                                                          bank[4][:, 0:FE // 2]).then_inc(hidT_ready.sem, 1)
                                    own_tokens(e + 1, 1 - q)
                                    dve.wait_ge(y_done.sem, e + 1)
                                    if not peeled:
                                        dve.wait_ge(y_stored[q].sem, 2 * 16 * i)
                                    nc.vector.tensor_copy(own_y[:, q, :], bank[5 + q][:, :]).then_inc(y_copied.sem, 1)
                                    find_members(e + 2, q)

                            find_members(0, 0)
                            find_members(1, 1)
                            own_tokens(0, 0)
                            two_experts(0, True)
                            with dve.Fori(1, PAIRS) as i:
                                two_experts(i, False)
                            for t in range(TT):
                                dve.wait_ge(taken_in.sem, 16 * 2 * TT)
                                nc.vector.tensor_scalar(taken[:, t, 0, :], taken[:, t, 0, :], gains[:, t, 0:1], None, ALU.mult).then_inc(merge_steps.up(), 1)
                                dve.wait_ge(merge_steps.sem, merge_steps.n)
                                nc.vector.scalar_tensor_tensor(taken[:, t, 0, :], taken[:, t, 1, :], gains[:, t, 1:2], taken[:, t, 0, :],
                                                               ALU.mult, ALU.add).then_inc(merge_steps.up(), 1)
                                dve.wait_ge(merge_steps.sem, merge_steps.n)
                                nc.vector.tensor_tensor(taken[:, t, 0, :], taken[:, t, 0, :], gates[:, 1, :], ALU.mult).then_inc(merge_steps.up(), 1)
                                dve.wait_ge(merge_steps.sem, merge_steps.n)
                                nc.vector.tensor_tensor(x[:, t, :], x[:, t, :], taken[:, t, 0, :], ALU.add).then_inc(merge_steps.up(), 1)
                                dve.wait_ge(merge_steps.sem, merge_steps.n)


        def gla_mixer(mixed):
            DV = D // H
            with ExitStack() as st:
                qT = sb(st, "gla_qT", [P, H, T])
                kT = sb(st, "gla_kT", [P, H, T])
                v = sb(st, "gla_v", [P, TT, D])
                r = sb(st, "gla_r", [P, TT, D])
                lowT = sb(st, "gla_lowT", [16, T])
                project_stage(first["gla_in"], [("channel", to_channels(qT, 0, float(P) ** -0.5)), ("channel", to_channels(kT, 0)),
                                                ("token", to_tokens(v, 0)), ("token", to_tokens(v, 512)),
                                                ("token", to_tokens(r, 0)), ("token", to_tokens(r, 512)),
                                                ("channel", lambda pair: [(lowT[:, :], pair[0][0:16, 0:T], 1.0)])], hT)
                wg = sb(st, "gla_wg", [16, H * P])
                z = sb(st, "gla_z", [P, H, T])
                cum = sb(st, "gla_cum", [P, H, T])
                e = sb(st, "gla_decay", [P, H, T])
                qs = sb(st, "gla_qs", [P, H, T])
                ks = sb(st, "gla_ks", [P, H, T])
                part = sb(st, "gla_part", [P, 2 * H, P])
                attT = sb(st, "gla_attT", [P, 3 * H, P])
                ones_t = sb(st, "ones_t", [P, T])
                norm_row = sb(st, "gla_norm_row", [P, DV])
                stat = sb(st, "gla_stat", [P, 2, 2 * H])
                wg_in, low_ready, az_ready, ln_ready = signal("operands_in"), signal("gla_z_ready"), signal("gla_abs_ready"), signal("gla_ln_ready")
                dist, decayed, scaled, scored = signal("gla_dist_ready"), signal("gla_decay_ready"), signal("gla_scaled"), signal("gla_scored")
                att_ready, o_ready, ms_ready, root = signal("gla_att_ready"), signal("heads_out_ready"), signal("mean_square_ready"), signal("root_ready")
                gate_ready, row_in = signal("silu_gate_ready"), signal("gain_row_in")
                LAST = LEVELS
                with nc.Block() as block:
                    @block.scalar
                    def _(act):
                        act.dma_start(wg[:, :], A["gla_w_gate2"][0]).then_inc(wg_in.up(16), 16)
                        act.dma_start(norm_row[:, :], A["gla_out_norm"][0].partition_broadcast(P)).then_inc(row_in.up(16), 16)
                        act.wait_ge(az_ready.sem, az_ready.at(1))
                        nc.scalar.activation(e[:, :, :], e[:, :, :], ACT.Exp, scale=-1.0).then_inc(scalar_steps.up(), 1)
                        act.wait_ge(scalar_steps.sem, scalar_steps.n)
                        nc.scalar.activation(e[:, :, :], e[:, :, :], ACT.Ln, bias=1.0).then_inc(ln_ready.up(), 1)
                        for n in range(LEVELS + 1):
                            act.wait_ge(dist.sem, dist.at(n + 1))
                            nc.scalar.activation(e[:, :, :], e[:, :, :], ACT.Exp, scale=-1.0).then_inc(decayed.up(), 1)
                        nc.scalar.activation(r[:, :, :], r[:, :, :], ACT.Silu).then_inc(gate_ready.up(), 1)
                        act.wait_ge(ms_ready.sem, ms_ready.at(1))
                        nc.scalar.activation(stat[:, 1, :], stat[:, 0, :], ACT.Sqrt).then_inc(root.up(), 1)

                    @block.tensor
                    def _(pe):
                        pe.wait_ge(wg_in.sem, wg_in.at(16))
                        for h in range(H):
                            last = nc.tensor.matmul(bank[h // 2][:, (h % 2) * T:(h % 2 + 1) * T], wg[:, h * P:(h + 1) * P], lowT[:, :],
                                                    start=True, stop=True)
                        last.then_inc(low_ready.up(), 1)
                        for u in range(2 * H):
                            cols = slice((u // H) * P, (u // H + 1) * P)
                            last = nc.tensor.matmul(bank[4 + u // H][:, (u % H) * P:(u % H + 1) * P], kT[:, u % H, cols], qT[:, u % H, cols],
                                                    start=True, stop=True)
                        last.then_inc(scored.up(), 1)
                        for n in range(LEVELS):
                            b0 = (6, 4)[n % 2]
                            pe.wait_ge(scaled.sem, scaled.at(n + 1))
                            for u in range(2 * H):
                                cols = slice((u // H) * P, (u // H + 1) * P)
                                last = nc.tensor.matmul(bank[b0 + u // H][:, (u % H) * P:(u % H + 1) * P], ks[:, u % H, cols], qs[:, u % H, cols],
                                                        start=True, stop=True)
                            last.then_inc(scored.up(), 1)
                        pe.wait_ge(scaled.sem, scaled.at(LAST + 1))
                        for h in range(H):
                            last = nc.tensor.matmul(bank[4][:, h * P:(h + 1) * P], ks[:, h, 0:P], qs[:, h, P:2 * P], start=True, stop=True)
                        last.then_inc(scored.up(), 1)
                        pe.wait_ge(att_ready.sem, att_ready.at(1))
                        for t in range(TT):
                            for h in range(H):
                                acc = bank[2 * t + h // 2][:, (h % 2) * DV:(h % 2 + 1) * DV]
                                if t:
                                    nc.tensor.matmul(acc, attT[:, 2 * H + h, :], v[:, 0, h * DV:(h + 1) * DV], start=True, stop=False)
                                last = nc.tensor.matmul(acc, attT[:, t * H + h, :], v[:, t, h * DV:(h + 1) * DV], start=(t == 0), stop=True)
                        last.then_inc(o_ready.up(), 1)

                    @block.vector
                    def _(dve):
                        nc.vector.memset(ones_t[:, :], 1.0).then_inc(vector_steps.up(), 1)
                        dve.wait_ge(vector_steps.sem, vector_steps.n)
                        dve.wait_ge(low_ready.sem, low_ready.at(1))
                        for h in range(H):
                            ins = nc.vector.tensor_scalar(z[:, h, :], bank[h // 2][:, (h % 2) * T:(h % 2 + 1) * T], col("gla_b_gate2", h, 1), None, ALU.add)
                        ins.then_inc(vector_steps.up(), 1)
                        dve.wait_ge(vector_steps.sem, vector_steps.n)
                        nc.vector.scalar_tensor_tensor(e[:, :, :], z[:, :, :], -1.0, z[:, :, :], ALU.mult, ALU.max).then_inc(az_ready.up(), 1)
                        nc.vector.tensor_scalar(z[:, :, :], z[:, :, :], -1.0, 0.0, ALU.mult, ALU.max).then_inc(vector_steps.up(), 1)
                        dve.wait_ge(vector_steps.sem, vector_steps.n)
                        dve.wait_ge(ln_ready.sem, ln_ready.at(1))
                        nc.vector.tensor_tensor(z[:, :, :], z[:, :, :], e[:, :, :], ALU.add).then_inc(vector_steps.up(), 1)
                        dve.wait_ge(vector_steps.sem, vector_steps.n)
                        nc.vector.tensor_scalar(z[:, :, :], z[:, :, :], -1.0 / GLA_TAU, None, ALU.mult).then_inc(vector_steps.up(), 1)
                        dve.wait_ge(vector_steps.sem, vector_steps.n)
                        for h in range(H):
                            ins = nc.vector.tensor_tensor_scan(cum[:, h, :], ones_t[:, :], z[:, h, :], 0.0, ALU.mult, ALU.add)
                        ins.then_inc(vector_steps.up(), 1)
                        dve.wait_ge(vector_steps.sem, vector_steps.n)
                        units = [slice(0, H), slice(H, 2 * H)]

                        def psum3(b):
                            return bank[b][:, :].rearrange("p (u i) -> p u i", u=H)

                        def distance(n):
                            s = 1 << n
                            blocks = cum[:, :, :].rearrange("p h (m s) -> p (h m) s", s=2 * s)
                            m = H * T // (2 * s)
                            eb = e[:, :, :].rearrange("p h (m s) -> p (h m) s", s=2 * s)
                            edge = blocks[:, :, s - 1:s].to_broadcast([P, m, 2 * s])
                            nc.vector.tensor_tensor(eb, blocks, edge, ALU.subtract).then_inc(vector_steps.up(), 1)
                            dve.wait_ge(vector_steps.sem, vector_steps.n)
                            nc.vector.scalar_tensor_tensor(e[:, :, :], e[:, :, :], -1.0, e[:, :, :], ALU.mult, ALU.max).then_inc(dist.up(), 1)

                        distance(0)
                        dve.wait_ge(scored.sem, scored.at(1))
                        for t in range(TT):
                            nc.vector.tensor_tensor(attT[:, units[t], :], psum3(4 + t), ident.unsqueeze(1).to_broadcast([P, H, P]), ALU.mult).then_inc(vector_steps.up(), 1)
                            dve.wait_ge(vector_steps.sem, vector_steps.n)
                        for n in range(LEVELS + 1):
                            dve.wait_ge(decayed.sem, decayed.at(n + 1))
                            if n:
                                dve.wait_ge(scored.sem, scored.at(n + 1))
                            nc.vector.tensor_tensor(qs[:, :, :], qT[:, :, :], e[:, :, :], ALU.mult).then_inc(vector_steps.up(), 1)
                            dve.wait_ge(vector_steps.sem, vector_steps.n)
                            nc.vector.tensor_tensor(ks[:, :, :], kT[:, :, :], e[:, :, :], ALU.mult).then_inc(scaled.up(), 1)
                            dve.wait_ge(scaled.sem, scaled.n)
                            if n < LEVELS:
                                distance(n + 1)
                            if n:
                                b0 = (6, 4)[(n - 1) % 2]
                                for t in range(TT):
                                    nc.vector.tensor_tensor(part[:, units[t], :], psum3(b0 + t), level(n - 1).unsqueeze(1).to_broadcast([P, H, P]),
                                                                     ALU.mult).then_inc(vector_steps.up(), 1)
                                    dve.wait_ge(vector_steps.sem, vector_steps.n)
                                nc.vector.tensor_tensor(attT[:, 0:2 * H, :], attT[:, 0:2 * H, :], part[:, :, :], ALU.add).then_inc(vector_steps.up(), 1)
                                dve.wait_ge(vector_steps.sem, vector_steps.n)
                        dve.wait_ge(scored.sem, scored.at(LAST + 2))
                        nc.vector.tensor_copy(attT[:, 2 * H:3 * H, :], psum3(4)).then_inc(att_ready.up(), 1)
                        dve.wait_ge(o_ready.sem, o_ready.at(1))
                        for t in range(TT):
                            for b in range(2):
                                om = mixed[:, t, 512 * b:512 * (b + 1)].rearrange("p (h d) -> p h d", h=2)
                                sq = qs[:, 2 * b:2 * b + 2, :]
                                nc.vector.tensor_copy(om, bank[2 * t + b][:, :].rearrange("p (h d) -> p h d", h=2)).then_inc(vector_steps.up(), 1)
                                dve.wait_ge(vector_steps.sem, vector_steps.n)
                                nc.vector.tensor_tensor(sq, om, om, ALU.mult).then_inc(vector_steps.up(), 1)
                                dve.wait_ge(vector_steps.sem, vector_steps.n)
                            nc.vector.tensor_reduce(stat[:, 0, t * H:(t + 1) * H], qs[:, :, :], AX.X, ALU.add).then_inc(vector_steps.up(), 1)
                            dve.wait_ge(vector_steps.sem, vector_steps.n)
                        nc.vector.tensor_scalar(stat[:, 0, :], stat[:, 0, :], 1.0 / DV, EPS, ALU.mult, ALU.add).then_inc(ms_ready.up(), 1)
                        dve.wait_ge(root.sem, root.at(1))
                        dve.wait_ge(gate_ready.sem, gate_ready.at(1))
                        dve.wait_ge(row_in.sem, row_in.at(16))
                        nc.vector.reciprocal(stat[:, 1, :], stat[:, 1, :]).then_inc(vector_steps.up(), 1)
                        dve.wait_ge(vector_steps.sem, vector_steps.n)
                        for t in range(TT):
                            om = mixed[:, t, :].rearrange("p (h d) -> p h d", h=H)
                            nc.vector.tensor_tensor(om, om, stat[:, 1, t * H:(t + 1) * H].unsqueeze(2).to_broadcast([P, H, DV]), ALU.mult).then_inc(vector_steps.up(), 1)
                            dve.wait_ge(vector_steps.sem, vector_steps.n)
                            nc.vector.tensor_tensor(om, om, norm_row[:, :].unsqueeze(1).to_broadcast([P, H, DV]), ALU.mult).then_inc(vector_steps.up(), 1)
                            dve.wait_ge(vector_steps.sem, vector_steps.n)
                            nc.vector.tensor_tensor(mixed[:, t, :], mixed[:, t, :], r[:, t, :], ALU.mult).then_inc(vector_steps.up(), 1)
                            dve.wait_ge(vector_steps.sem, vector_steps.n)

        def final_norm_stage(name, dst):
            with ExitStack() as st:
                row = sb(st, "final_row", [P, D])
                sq = sb(st, "final_sq", [P, D])
                stat = sb(st, "final_stat", [P, 2, TT])
                row_in, ms_ready, root = signal("gain_row_in"), signal("mean_square_ready"), signal("root_ready")
                with nc.Block() as block:
                    @block.scalar
                    def _(act):
                        act.dma_start(row[:, :], A[name].partition_broadcast(P)).then_inc(row_in.up(16), 16)
                        act.wait_ge(ms_ready.sem, ms_ready.at(1))
                        nc.scalar.activation(stat[:, 1, :], stat[:, 0, :], ACT.Sqrt).then_inc(root.up(), 1)

                    @block.vector
                    def _(dve):
                        for t in range(TT):
                            nc.vector.tensor_tensor_reduce(sq[:, :], x[:, t, :], x[:, t, :], 1.0, 0.0, ALU.mult, ALU.add, stat[:, 0, t:t + 1]).then_inc(vector_steps.up(), 1)
                            dve.wait_ge(vector_steps.sem, vector_steps.n)
                        nc.vector.tensor_scalar(stat[:, 0, :], stat[:, 0, :], 1.0 / D, EPS, ALU.mult, ALU.add).then_inc(ms_ready.up(), 1)
                        dve.wait_ge(root.sem, root.at(1))
                        dve.wait_ge(row_in.sem, row_in.at(16))
                        nc.vector.reciprocal(stat[:, 1, :], stat[:, 1, :]).then_inc(vector_steps.up(), 1)
                        dve.wait_ge(vector_steps.sem, vector_steps.n)
                        for t in range(TT):
                            nc.vector.scalar_tensor_tensor(dst[:, t, :], x[:, t, :], stat[:, 1, t:t + 1], row[:, :], ALU.mult, ALU.mult).then_inc(vector_steps.up(), 1)
                            dve.wait_ge(vector_steps.sem, vector_steps.n)

        def attention_stage(units, branch_gate=None):
            n = len(units)
            with ExitStack() as st:
                probs = sb(st, "seg_probs", [P, 3, 3, T])
                probsT = sb(st, "seg_probsT", [P, 2, 6, P])
                stat = sb(st, "seg_stat", [P, 3, 3, 4])
                scored, shifted, exped, normal = signal("att_logits_ready"), signal("att_max_ready"), signal("att_exp_ready"), signal("att_probs_ready")
                turned, turned_in, summed, done = signal("att_probs_turned"), signal("att_probsT_ready"), signal("att_out_ready"), signal("att_tile_done")

                def score_bank(u, s):
                    return bank[2 * (u % 2) + s // 2][:, (s % 2) * T:(s % 2 + 1) * T]

                def groups(unit):
                    segs = unit["segs"]
                    return [(0, len(segs))] if unit["joint"] else [(s, s + 1) for s in range(len(segs))]

                def blocks(unit):
                    out = []
                    for s, (_, _, _, _, values) in enumerate(unit["segs"]):
                        k0 = 0
                        for v, keys in values:
                            out.append((s, k0, keys, v))
                            k0 += keys
                    return out

                with nc.Block() as block:
                    @block.tensor
                    def _(pe):
                        for u in range(n + 3):
                            if u < n:
                                if u >= 2:
                                    pe.wait_ge(shifted.sem, shifted.at(u - 1))
                                for s, (q, k, nk, _, _) in enumerate(units[u]["segs"]):
                                    last = nc.tensor.matmul(score_bank(u, s)[:, 0:nk], q, k, start=True, stop=True)
                                last.then_inc(scored.up(), 1)
                            if u >= 3:
                                w = u - 3
                                pe.wait_ge(turned_in.sem, turned_in.at(w + 1))
                                if w >= 2:
                                    pe.wait_ge(done.sem, done.at(w - 1))
                                lo, rows = units[w]["rows"]
                                bl = blocks(units[w])
                                for i, (s, k0, keys, v) in enumerate(bl):
                                    last = nc.tensor.matmul(bank[6 + w % 2][lo:lo + rows, 0:P], v, probsT[0:keys, w % 2, i, :],
                                                            start=(i == 0), stop=(i == len(bl) - 1))
                                last.then_inc(summed.up(), 1)
                            if 2 <= u < n + 2:
                                w = u - 2
                                pe.wait_ge(normal.sem, normal.at(w + 1))
                                for i, (s, k0, keys, _) in enumerate(blocks(units[w])):
                                    last = nc.tensor.transpose(bank[4 + i // 4][0:keys, (i % 4) * P:(i % 4 + 1) * P],
                                                               probs[:, w % 3, s, k0:k0 + keys], ident)
                                last.then_inc(turned.up(), 1)

                    @block.vector
                    def _(dve):
                        for u in range(n + 4):
                            if u < n:
                                dve.wait_ge(scored.sem, scored.at(u + 1))
                                for s, (_, _, nk, bias, _) in enumerate(units[u]["segs"]):
                                    d = probs[:, u % 3, s, 0:nk]
                                    if bias is None:
                                        ins = nc.vector.tensor_copy(d, score_bank(u, s)[:, 0:nk])
                                    else:
                                        ins = nc.vector.scalar_tensor_tensor(d, bias[0][:, 0:nk], -float(bias[1]), score_bank(u, s)[:, 0:nk],
                                                                             ALU.mult, ALU.add)
                                ins.then_inc(vector_steps.up(), 1)
                                dve.wait_ge(vector_steps.sem, vector_steps.n)
                                for a, b in groups(units[u]):
                                    nk = units[u]["segs"][a][2]
                                    ins = nc.vector.tensor_reduce(stat[:, u % 3, a, 0:1], probs[:, u % 3, a:b, 0:nk], AX.XY, ALU.max, negate=True)
                                ins.then_inc(shifted.up(), 1)
                            if 1 <= u < n + 1:
                                w = u - 1
                                dve.wait_ge(exped.sem, exped.at(w + 1))
                                m = len(groups(units[w]))
                                nc.vector.reciprocal(stat[:, w % 3, 0:m, 2], stat[:, w % 3, 0:m, 1]).then_inc(vector_steps.up(), 1)
                                dve.wait_ge(vector_steps.sem, vector_steps.n)
                                if units[w]["gates"] is not None:
                                    nc.vector.tensor_tensor(stat[:, w % 3, 0:m, 2], stat[:, w % 3, 0:m, 2], units[w]["gates"],
                                                            ALU.mult).then_inc(vector_steps.up(), 1)
                                    dve.wait_ge(vector_steps.sem, vector_steps.n)
                                for a, b in groups(units[w]):
                                    nk = units[w]["segs"][a][2]
                                    d = probs[:, w % 3, a:b, 0:nk]
                                    ins = nc.vector.tensor_scalar(d, d, stat[:, w % 3, a, 2:3], None, ALU.mult)
                                ins.then_inc(normal.up(), 1)
                            if u >= 4:
                                w = u - 4
                                dve.wait_ge(summed.sem, summed.at(w + 1))
                                lo, rows = units[w]["rows"]
                                dst, gate = units[w]["out"]
                                nc.vector.tensor_tensor(dst, bank[6 + w % 2][lo:lo + rows, 0:P], gate, ALU.mult).then_inc(done.up(), 1)

                    @block.scalar
                    def _(act):
                        for u in range(n + 2):
                            if u < n:
                                act.wait_ge(shifted.sem, shifted.at(u + 1))
                                for a, b in groups(units[u]):
                                    nk = units[u]["segs"][a][2]
                                    d = probs[:, u % 3, a:b, 0:nk]
                                    ins = nc.scalar.activation(d, d, ACT.Exp, bias=stat[:, u % 3, a, 0:1], accum_out=stat[:, u % 3, a, 1:2])
                                ins.then_inc(exped.up(), 1)
                            if u >= 2:
                                w = u - 2
                                act.wait_ge(turned.sem, turned.at(w + 1))
                                bl = blocks(units[w])
                                for i0 in range(0, len(bl), 4):
                                    whole = [x for x in bl[i0:i0 + 4] if x[2] == P]
                                    if whole:
                                        ins = nc.scalar.copy(probsT[:, w % 2, i0:i0 + len(whole), :].rearrange("p b s -> p (b s)"),
                                                             bank[4 + i0 // 4][:, 0:len(whole) * P])
                                    for i in range(i0 + len(whole), min(i0 + 4, len(bl))):
                                        keys = bl[i][2]
                                        ins = nc.scalar.copy(probsT[0:keys, w % 2, i, :], bank[4 + i // 4][0:keys, (i % 4) * P:(i % 4 + 1) * P])
                                ins.then_inc(turned_in.up(), 1)

        def memory_units(qT, kT, v, yT, gate, tile0):
            units = []
            for t in range(TT):
                for h in range(H):
                    lo = (h % 2) * HD
                    rows = slice(lo, lo + HD)
                    units.append({
                        "segs": [(qT[rows, h // 2, t * P:(t + 1) * P], kT[rows, h // 2, :], T, None,
                                  [(v[:, b, h * HD:(h + 1) * HD], P) for b in range(TT)])],
                        "joint": True, "gates": None, "rows": (lo, HD),
                        "out": (yT[rows, tile0 + h // 2, t * P:(t + 1) * P], gate[rows, h // 2, t * P:(t + 1) * P])})
            return units

        def memory_keys(prefix, c0, kT, v):
            with ExitStack() as st:
                mem = sb(st, "mem", [P, TT, D])
                norm_stage(mem, col(prefix + "_mem_norm_2"), None, hT, load=A["mem_2"][0].rearrange("(t p) d -> p t d", p=P))

                def evacuate(pair):
                    return [(kT[:, :, :], pair[0][:, :].rearrange("p (m t) -> p m t", m=2), 1.0),
                            (v[:, :, :], pair[1][:, :].rearrange("p (t d) -> p t d", t=TT), 1.0)]
                project_stage(c0, [("keys_values", evacuate)], hT)

        def recurrence(yT):
            with ExitStack() as st:
                xc = sb(st, "lru_x", [P, KD, T])
                za = sb(st, "lru_za", [P, KD, T])
                with ExitStack() as st_raw:
                    raw = sb(st_raw, "lru_raw", [P, KD, T + CONV - 1])

                    def to_raw(m0):
                        return lambda pair: [(raw[:, m0 + 2 * b:m0 + 2 * b + 2, CONV - 1:], pair[b][:, :].rearrange("p (m t) -> p m t", m=2), 1.0)
                                             for b in range(2)]
                    project_stage(first["hawk_in"], [("channel", to_raw(0)), ("channel", to_raw(4)),
                                                     ("channel", to_channels(za, 0)), ("channel", to_channels(za, 4))], hT)
                    convolve(raw, xc, KD, "hawk_conv_w_2", "hawk_conv_b_2")
                wgate = sb(st, "lru_gate_w", [P, 2, KD, P])
                rg = sb(st, "lru_r", [P, KD, T])
                ig = sb(st, "lru_i", [P, KD, T])
                den = sb(st, "lru_den", [P, KD, T])
                vec = sb(st, "lru_vec", [P, 4, KD])
                cleared, w_in, gated = signal("lru_w_cleared"), signal("operands_in"), signal("lru_gate_dots")
                soft_in, soft, r_ready, i_ready, log_ready = (signal(s) for s in ("lru_soft_in", "lru_soft_exp", "lru_r_ready", "lru_i_ready", "lru_log_ready"))
                a_ready, t_ready, m_in, m_ready, z_ready = (signal(s) for s in ("lru_a_ready", "lru_tanh_ready", "lru_mult_in", "lru_mult_ready", "lru_z_ready"))
                with nc.Block() as block:
                    @block.gpsimd
                    def _(pool):
                        nc.gpsimd.memset(wgate[:, :, :, :], 0.0).then_inc(cleared.up(), 1)

                    @block.scalar
                    def _(act):
                        act.wait_ge(cleared.sem, cleared.at(1))
                        for n, name in enumerate(("hawk_gate_a_w_2", "hawk_gate_x_w_2")):
                            w = A[name][0].rearrange("(m two) i j -> two i m j", two=2)
                            for two in range(2):
                                rows = slice(two * HD, (two + 1) * HD)
                                act.dma_start(wgate[rows, n, :, rows], w[two]).then_inc(w_in.up(16), 16)
                        act.wait_ge(soft_in.sem, soft_in.at(1))
                        nc.scalar.activation(vec[:, 1, :], vec[:, 0, :], ACT.Exp, scale=-1.0).then_inc(soft.up(), 1)
                        act.wait_ge(gated.sem, gated.at(2))
                        for n, (dst, bias, ready) in enumerate(((rg, "hawk_gate_a_b_2", r_ready), (ig, "hawk_gate_x_b_2", i_ready))):
                            for m in range(KD):
                                ins = nc.scalar.activation(dst[:, m, :], bank[4 * n + m // 2][:, (m % 2) * T:(m % 2 + 1) * T], ACT.Sigmoid,
                                                           bias=col(bias, m, 1))
                            ins.then_inc(ready.up(), 1)
                        act.wait_ge(log_ready.sem, log_ready.at(1))
                        nc.scalar.activation(den[:, :, :], rg[:, :, :], ACT.Tanh).then_inc(t_ready.up(), 1)
                        act.wait_ge(t_ready.sem, t_ready.n)
                        nc.scalar.activation(rg[:, :, :], rg[:, :, :], ACT.Exp).then_inc(a_ready.up(), 1)
                        nc.scalar.activation(za[:, :, :], za[:, :, :], ACT.Silu).then_inc(z_ready.up(), 1)
                        act.wait_ge(m_in.sem, m_in.at(1))
                        nc.scalar.activation(den[:, :, :], den[:, :, :], ACT.Sqrt).then_inc(m_ready.up(), 1)

                    @block.tensor
                    def _(pe):
                        pe.wait_ge(w_in.sem, w_in.at(64))
                        for n in range(2):
                            for m in range(KD):
                                last = nc.tensor.matmul(bank[4 * n + m // 2][:, (m % 2) * T:(m % 2 + 1) * T], wgate[:, n, m, :], xc[:, m, :],
                                                        start=True, stop=True)
                            last.then_inc(gated.up(), 1)

                    @block.vector
                    def _(dve):
                        lam = col("hawk_lambda_2")
                        nc.vector.scalar_tensor_tensor(vec[:, 0, :], lam, -1.0, lam, ALU.mult, ALU.max).then_inc(soft_in.up(), 1)
                        dve.wait_ge(soft.sem, soft.at(1))
                        nc.vector.tensor_scalar(vec[:, 2, :], vec[:, 1, :], 2.0, None, ALU.add).then_inc(vector_steps.up(), 1)
                        dve.wait_ge(vector_steps.sem, vector_steps.n)
                        nc.vector.reciprocal(vec[:, 2, :], vec[:, 2, :]).then_inc(vector_steps.up(), 1)
                        dve.wait_ge(vector_steps.sem, vector_steps.n)
                        nc.vector.tensor_tensor(vec[:, 0, :], vec[:, 1, :], vec[:, 2, :], ALU.mult).then_inc(vector_steps.up(), 1)
                        dve.wait_ge(vector_steps.sem, vector_steps.n)
                        nc.vector.tensor_tensor(vec[:, 1, :], vec[:, 0, :], vec[:, 0, :], ALU.mult).then_inc(vector_steps.up(), 1)
                        dve.wait_ge(vector_steps.sem, vector_steps.n)
                        nc.vector.memset(vec[:, 2, :], 1.0 / 17).then_inc(vector_steps.up(), 1)
                        dve.wait_ge(vector_steps.sem, vector_steps.n)
                        for odd in range(15, 0, -2):
                            nc.vector.tensor_tensor(vec[:, 2, :], vec[:, 2, :], vec[:, 1, :], ALU.mult).then_inc(vector_steps.up(), 1)
                            dve.wait_ge(vector_steps.sem, vector_steps.n)
                            nc.vector.tensor_scalar(vec[:, 2, :], vec[:, 2, :], 1.0 / odd, None, ALU.add).then_inc(vector_steps.up(), 1)
                            dve.wait_ge(vector_steps.sem, vector_steps.n)
                        nc.vector.tensor_tensor(vec[:, 2, :], vec[:, 2, :], vec[:, 0, :], ALU.mult).then_inc(vector_steps.up(), 1)
                        dve.wait_ge(vector_steps.sem, vector_steps.n)
                        nc.vector.tensor_scalar(vec[:, 1, :], lam, -1.0, 0.0, ALU.mult, ALU.max).then_inc(vector_steps.up(), 1)
                        dve.wait_ge(vector_steps.sem, vector_steps.n)
                        nc.vector.scalar_tensor_tensor(vec[:, 2, :], vec[:, 2, :], 2.0, vec[:, 1, :], ALU.mult, ALU.add).then_inc(vector_steps.up(), 1)
                        dve.wait_ge(vector_steps.sem, vector_steps.n)
                        nc.vector.tensor_scalar(vec[:, 3, :], vec[:, 2, :], -LRU_C, None, ALU.mult).then_inc(vector_steps.up(), 1)
                        dve.wait_ge(vector_steps.sem, vector_steps.n)
                        dve.wait_ge(r_ready.sem, r_ready.at(1))
                        nc.vector.tensor_tensor(rg[:, :, :], rg[:, :, :], vec[:, 3, :].unsqueeze(2).to_broadcast([P, KD, T]), ALU.mult).then_inc(log_ready.up(), 1)
                        dve.wait_ge(i_ready.sem, i_ready.at(1))
                        nc.vector.tensor_tensor(xc[:, :, :], xc[:, :, :], ig[:, :, :], ALU.mult).then_inc(vector_steps.up(), 1)
                        dve.wait_ge(vector_steps.sem, vector_steps.n)
                        dve.wait_ge(t_ready.sem, t_ready.at(1))
                        nc.vector.tensor_scalar(ig[:, :, :], den[:, :, :], -1.0, 1.0, ALU.mult, ALU.add).then_inc(vector_steps.up(), 1)
                        dve.wait_ge(vector_steps.sem, vector_steps.n)
                        nc.vector.reciprocal(ig[:, :, :], ig[:, :, :]).then_inc(vector_steps.up(), 1)
                        dve.wait_ge(vector_steps.sem, vector_steps.n)
                        nc.vector.scalar_tensor_tensor(den[:, :, :], den[:, :, :], -2.0, ig[:, :, :], ALU.mult, ALU.mult).then_inc(m_in.up(), 1)
                        dve.wait_ge(m_ready.sem, m_ready.at(1))
                        nc.vector.memset(den[:, :, 0:1], 1.0).then_inc(vector_steps.up(), 1)
                        dve.wait_ge(vector_steps.sem, vector_steps.n)
                        nc.vector.tensor_tensor(xc[:, :, :], xc[:, :, :], den[:, :, :], ALU.mult).then_inc(vector_steps.up(), 1)
                        dve.wait_ge(vector_steps.sem, vector_steps.n)
                        dve.wait_ge(a_ready.sem, a_ready.at(1))
                        for m in range(KD):
                            ins = nc.vector.tensor_tensor_scan(ig[:, m, :], rg[:, m, :], xc[:, m, :], 0.0, ALU.mult, ALU.add)
                        ins.then_inc(vector_steps.up(), 1)
                        dve.wait_ge(vector_steps.sem, vector_steps.n)
                        dve.wait_ge(z_ready.sem, z_ready.at(1))
                        nc.vector.tensor_tensor(yT[:, 0:KD, :], ig[:, :, :], za[:, :, :], ALU.mult).then_inc(vector_steps.up(), 1)
                        dve.wait_ge(vector_steps.sem, vector_steps.n)

        def hawk_layer():
            G = len(DIL)
            with ExitStack() as st:
                yT = sb(st, "hawk_yT", [P, 14, T])
                mem_kT = sb(st, "mem_kT", [P, 2, T])
                mem_v = sb(st, "mem_v", [P, TT, T])
                memory_keys("hawk", first["hawk_mem"], mem_kT, mem_v)
                norm_stage(x, col("hawk_norm_2"), None, hT)
                recurrence(yT)
                with ExitStack() as st_a:
                    qT = sb(st_a, "dil_qT", [P, G * H, T])
                    kT = sb(st_a, "dil_kT", [P, G * H, T])
                    v = sb(st_a, "dil_v", [P, TT, G * 512])
                    zb = sb(st_a, "dil_zb", [P, H, T])
                    mq = sb(st_a, "mem_q_gate", [P, 4, T])

                    def memory_query(pair):
                        return [(mq[:, 0:2, :], pair[0][:, :].rearrange("p (m t) -> p m t", m=2), HD ** -0.5),
                                (mq[:, 2:4, :], pair[1][:, :].rearrange("p (m t) -> p m t", m=2), 1.0)]
                    plan = [("channel", to_channels(qT, 4 * g, float(P) ** -0.5)) for g in range(G)]
                    plan += [("channel", to_channels(kT, 4 * g)) for g in range(G)]
                    plan += [("token", to_tokens(v, 512 * g)) for g in range(G)]
                    plan += [("channel", to_channels(zb, 0)), ("channel", memory_query)]
                    project_stage(first["hawk_in"] + 4, plan, hT)
                    silu_stage(zb)
                    silu_stage(mq[:, 2:4, :])
                    dist = sb(st_a, "dist", [P, 3, TT, T])
                    load_stage(dist, dists.rearrange("p (n t s) -> p n t s", n=4, t=TT)[:, 1:4])
                    units = []
                    for t in range(TT):
                        for h in range(H):
                            segs = [(qT[:, g * H + h, t * P:(t + 1) * P], kT[:, g * H + h, 0:(t + 1) * P], (t + 1) * P,
                                     (dist[:, g, t, :], SLOPES_DIL[g * H + h]),
                                     [(v[:, b, g * 512 + h * P:g * 512 + (h + 1) * P], P) for b in range(t + 1)]) for g in range(G)]
                            units.append({"segs": segs, "joint": True, "gates": None, "rows": (0, P),
                                          "out": (yT[:, KD + h, t * P:(t + 1) * P], zb[:, h, t * P:(t + 1) * P])})
                    units += memory_units(mq[:, 0:2, :], mem_kT, mem_v, yT, mq[:, 2:4, :], KD + H)
                    attention_stage(units)
                out_stage(first["hawk_out"], [(0, 8), (8, 6)], yT, None)

        def load_stage(dst, src):
            loaded = signal("operands_in")
            with nc.Block() as block:
                @block.scalar
                def _(act):
                    act.dma_start(dst[:, :, :, :] if len(dst.shape) == 4 else dst, src).then_inc(loaded.up(16), 16)
                    act.wait_ge(loaded.sem, loaded.n)

        def nsa_layer():
            G = 2
            KV = 2 * G
            with ExitStack() as st:
                yT = sb(st, "nsa_yT", [P, 10, T])
                mem_kT = sb(st, "mem_kT", [P, 2, T])
                mem_v = sb(st, "mem_v", [P, TT, T])
                memory_keys("nsa", first["nsa_mem"], mem_kT, mem_v)
                norm_stage(x, col("nsa_norm_2"), None, hT)
                qT = sb(st, "nsa_qT", [P, 8, T])
                pairT = sb(st, "cmp_pairT", [P, KV, T])
                kT = sb(st, "nsa_kT", [P, KV, T])
                vg = sb(st, "nsa_v_gates", [P, TT, 304])
                zT = sb(st, "nsa_zT", [P, 8, T])
                mq = sb(st, "nsa_mem_q_gate", [P, 4, T])

                def to_pairs(pair):
                    copies = []
                    for b in range(2):
                        src = pair[b][:, :].rearrange("p (m t) -> p m t", m=2)
                        copies.append((pairT[0:HD, 2 * b:2 * b + 2, :], src[0:HD], 1.0))
                        copies.append((pairT[HD:P, 2 * b:2 * b + 2, 0:T - 1], src[HD:P, :, 1:T], 1.0))
                    return copies

                def memory_query(pair):
                    return [(mq[:, 0:2, :], pair[0][:, :].rearrange("p (m t) -> p m t", m=2), HD ** -0.5),
                            (mq[:, 2:4, :], pair[1][:, :].rearrange("p (m t) -> p m t", m=2), 1.0)]

                project_stage(first["nsa_in"], [("channel", to_channels(qT, 0, HD ** -0.5)), ("channel", to_channels(qT, 4, HD ** -0.5)),
                                                ("channel", to_pairs), ("channel", to_channels(kT, 0)), ("token", to_tokens(vg, 0, 304)),
                                                ("channel", to_channels(zT, 0)), ("channel", to_channels(zT, 4)), ("channel", memory_query)], hT)
                silu_stage(zT)
                silu_stage(mq[:, 2:4, :])
                gates = sb(st, "nsa_gates", [P, TT, 3 * NSA_H])
                cmp_kT = sb(st, "cmp_kT", [P, G * NCMP])
                cmp_v = sb(st, "cmp_v", [16, G, HD])
                compress(pairT, vg, gates, cmp_kT, cmp_v)
                dist = sb(st, "nsa_dist", [P, 1, TT, T])
                load_stage(dist, dists.rearrange("p (n t s) -> p n t s", n=4, t=TT)[:, 0:1])
                units = []
                for t in range(TT):
                    for h in range(NSA_H):
                        g, lo = h // 8, (h % 2) * HD
                        rows = slice(lo, lo + HD)
                        q = qT[rows, h // 2, t * P:(t + 1) * P]
                        slope = SLOPES_NSA[h]
                        keys = (t + 1) * P
                        segs = [(q, cmp_kT[rows, g * NCMP:(g + 1) * NCMP], NCMP, (cmp_dist[:, t, :], slope), [(cmp_v[0:NCMP, g, :], NCMP)])]
                        for branch in range(2):
                            at = branch * P + g * HD
                            segs.append((q, kT[rows, branch * 2 + g, 0:keys], keys, (dist[:, 0, t, :], slope),
                                         [(vg[:, b, at:at + HD], P) for b in range(t + 1)]))
                        segs = [segs[1], segs[2], segs[0]]
                        units.append({"segs": segs, "joint": False, "gates": gates[:, t, 3 * h:3 * h + 3], "rows": (lo, HD),
                                      "out": (yT[rows, h // 2, t * P:(t + 1) * P], zT[rows, h // 2, t * P:(t + 1) * P])})
                units += memory_units(mq[:, 0:2, :], mem_kT, mem_v, yT, mq[:, 2:4, :], 8)
                attention_stage(units)
                out_stage(first["nsa_out"], [(0, 8), (8, 2)], yT, None)

        def compress(pairT, vg, gates, cmp_kT, cmp_v):
            c0 = first["nsa_phi"]
            frees(c0, 2)
            used0 = chunk_used.n
            G, STEPS = 2, CMP_BLOCK // 2
            n = G * NCMP
            with ExitStack() as st:
                rows = sb(st, "cmp_rows", [P, 2, STEPS, n])
                hid = sb(st, "cmp_hid", [P, 2, 2, n])
                w2k = sb(st, "cmp_w2k", [P, 2, P])
                w2v = sb(st, "cmp_w2v", [P, 2, HD])
                sig = sb(st, "nsa_sig", [P, TT, 3 * NSA_H])
                w_in, rows_ready, hid_ready, out_ready, sig_ready = (signal(s) for s in ("cmp_w2_in", "cmp_rows_ready", "cmp_hid_ready", "cmp_out_ready", "nsa_sig_ready"))
                with nc.Block() as block:
                    @block.sync
                    def _(sp):
                        fill_ring(sp, c0 + 1)

                    @block.scalar
                    def _(act):
                        for two in range(2):
                            act.dma_start(w2k[:, :, two * HD:(two + 1) * HD], A["nsa_phi_k_w2_2"][0].rearrange("(k p) d -> p k d", p=P)).then_inc(w_in.up(16), 16)
                        act.dma_start(w2v[:, :, :], A["nsa_phi_v_w2_2"][0].rearrange("(k p) d -> p k d", p=P)).then_inc(w_in.up(16), 16)
                        nc.scalar.activation(sig[:, :, :], vg[:, :, 256:304], ACT.Sigmoid).then_inc(sig_ready.up(), 1)
                        for i in range(2):
                            act.wait_ge(chunk_used.sem, used0 + i + 1)
                            nc.scalar.activation(hid[:, i, :, :], bank[i][:, 0:2 * n].rearrange("p (m n) -> p m n", m=2), ACT.Silu).then_inc(hid_ready.up(), 1)

                    @block.vector
                    def _(dve):
                        for i, name in enumerate(("nsa_pe_k_2", "nsa_pe_v_2")):
                            for g in range(G):
                                src = pairT[:, 2 * i + g, :]
                                for m in range(STEPS):
                                    ins = nc.vector.tensor_scalar(rows[:, i, m, g * NCMP:(g + 1) * NCMP],
                                                                  src[:, 2 * m:2 * m + CMP_STRIDE * (NCMP - 1) + 1:CMP_STRIDE],
                                                                  col(name, m, 1), None, ALU.add)
                            ins.then_inc(rows_ready.up(), 1)
                        dve.wait_ge(sig_ready.sem, sig_ready.at(1))
                        g3 = gates[:, :, :].rearrange("p t (h b) -> p t h b", b=3)
                        s3 = sig[:, :, :].rearrange("p t (h b) -> p t h b", b=3)
                        nc.vector.tensor_copy(g3[:, :, :, 0:2], s3[:, :, :, 1:3]).then_inc(vector_steps.up(), 1)
                        dve.wait_ge(vector_steps.sem, vector_steps.n)
                        for t in range(TT):
                            nc.vector.tensor_scalar(g3[:, t, :, 2], s3[:, t, :, 0], kc[:, C_ANY + t:C_ANY + t + 1], None, ALU.mult).then_inc(vector_steps.up(), 1)
                            dve.wait_ge(vector_steps.sem, vector_steps.n)
                        dve.wait_ge(out_ready.sem, out_ready.at(1))
                        nc.vector.tensor_copy(cmp_kT[:, :], bank[2][:, 0:n]).then_inc(vector_steps.up(), 1)
                        dve.wait_ge(vector_steps.sem, vector_steps.n)
                        nc.vector.tensor_copy(cmp_v[0:NCMP, :, :], bank[3][0:NCMP, 0:G * HD].rearrange("p (g d) -> p g d", g=G)).then_inc(vector_steps.up(), 1)
                        dve.wait_ge(vector_steps.sem, vector_steps.n)

                    @block.tensor
                    def _(pe):
                        for i in range(2):
                            arrived(pe, c0 + i)
                            pe.wait_ge(rows_ready.sem, rows_ready.at(i + 1))
                            w = slot(c0 + i)
                            for m in range(2):
                                for s in range(STEPS):
                                    last = nc.tensor.matmul(bank[i][:, m * n:(m + 1) * n], w[:, s, m * P:(m + 1) * P], rows[:, i, s, :],
                                                            start=(s == 0), stop=(s == STEPS - 1))
                            last.then_inc(chunk_used.up(), 1)
                        pe.wait_ge(w_in.sem, w_in.at(48))
                        pe.wait_ge(hid_ready.sem, hid_ready.at(2))
                        for m in range(2):
                            nc.tensor.matmul(bank[2][:, 0:n], w2k[:, m, :], hid[:, 0, m, :], start=(m == 0), stop=(m == 1))
                        for g in range(G):
                            for m in range(2):
                                last = nc.tensor.matmul(bank[3][0:NCMP, g * HD:(g + 1) * HD], hid[:, 1, m, g * NCMP:(g + 1) * NCMP], w2v[:, m, :],
                                                        start=(m == 0), stop=(m == 1))
                        last.then_inc(out_ready.up(), 1)

        def store_stage():
            stored = signal("output_stored")
            with nc.Block() as block:
                @block.sync
                def _(sp):
                    sp.dma_start(out[0].rearrange("(t p) d -> p t d", p=P), x[:, :, :]).then_inc(stored.up(16), 16)
                    sp.wait_ge(stored.sem, stored.n)

        for layer in range(2):
            with ExitStack() as st:
                gates = sb(st, "gates", [P, 2, D])
                mod = sb(st, "mod", [P, 4, KD])
                modulation_stage(layer, gates, mod)
                norm_stage(x, mod[:, 0, :], mod[:, 1, :], hT)
                with ExitStack() as st_m:
                    mixed = sb(st_m, "mixed", [P, TT, D])
                    (even_mixer, gla_mixer)[layer](mixed)
                    turn_stage(mixed, hT)
                out_stage(first[("even_out", "gla_out")[layer]], [(0, KD)], hT, gates[:, 0, :])
                if last_stage == ("mix", layer):
                    store_stage()
                    return
                xn = sb(st, "xn_kept", [P, TT, D])
                norm_stage(x, mod[:, 2, :], mod[:, 3, :], hT, xn=xn)
                experts_stage(layer, gates, xn, mod[:, 2, :], mod[:, 3, :])
            if last_stage == ("moe", layer):
                store_stage()
                return
        final_norm_stage("final_norm", x)
        hawk_layer()
        if last_stage == "hawk":
            store_stage()
            return
        nsa_layer()
        final_norm_stage("final_norm_2", x)
        store_stage()


_INS = ['x', 'c', 'positions', 'ada_w', 'ada_b', 'norm_mix', 'norm_ffn', 'even_w_in', 'gdn_conv_w', 'gdn_a_log', 'gdn_dt_bias', 'gdn_out_norm',
        'even_w_out', 'gla_w_in', 'gla_w_gate2', 'gla_b_gate2', 'gla_out_norm', 'gla_w_out', 'router_group_w', 'router_group_b', 'router_exp_w',
        'router_exp_b', 'exp_w1', 'exp_w3', 'exp_w2', 'final_norm', 'mem_2', 'hawk_norm_2', 'hawk_w_in_2', 'hawk_conv_w_2', 'hawk_conv_b_2',
        'hawk_gate_a_w_2', 'hawk_gate_a_b_2', 'hawk_gate_x_w_2', 'hawk_gate_x_b_2', 'hawk_lambda_2', 'hawk_mem_norm_2', 'hawk_w_mem_kv_2',
        'hawk_w_out_2', 'nsa_norm_2', 'nsa_w_in_2', 'nsa_pe_k_2', 'nsa_pe_v_2', 'nsa_phi_k_w1_2', 'nsa_phi_k_w2_2', 'nsa_phi_v_w1_2',
        'nsa_phi_v_w2_2', 'nsa_mem_norm_2', 'nsa_w_mem_kv_2', 'nsa_w_out_2', 'final_norm_2']


LAST_STAGE = None


def kernel(**inputs):
    import concourse.bacc as _bacc
    from concourse.bass_utils import run_bass_kernel_spmd as _run

    nc = _bacc.Bacc("TRN2", target_bir_lowering=False, num_devices=1)
    arrays, args = {}, {}
    table, distances = constants()
    given = {name: inputs[name] for name in _INS}
    given["consts"], given["dists"] = table, distances
    for name, value in given.items():
        a = np.ascontiguousarray(value)
        arrays[f"in_{name}_dram"] = a
        args[name] = nc.dram_tensor(f"in_{name}_dram", a.shape, mybir.dt.from_np(a.dtype), kind="ExternalInput").ap()
    result = nc.dram_tensor("out_0_dram", (1, T, D), F32, kind="ExternalOutput").ap()
    program(nc, args, args["consts"], args["dists"], result, LAST_STAGE)
    r = _run(nc, [arrays], core_ids=[0])
    return r.results[0]["out_0_dram"]
```

```python
from contextlib import ExitStack

import numpy as np
import concourse.bass as bass
from concourse import mybir

F32 = mybir.dt.float32
I32 = mybir.dt.int32
U32 = mybir.dt.uint32
ALU = mybir.AluOpType
ACT = mybir.ActivationFunctionType
AX = mybir.AxisListType

P = 128
T = 256
TT = T // P
D = 1024
KD = D // P
EPS = 1e-6
NEG = -1e30
TAKEN = -3e30
FAR = 1e32

SLOT = 4096
RING = 6

H = 4
CONV = 4
TOPK = 64
IDX_DH = 64
EXPERTS = 32
GROUPS = 4
PER_GROUP = EXPERTS // GROUPS
FE = 512
FT = FE // P
LEVELS = 7
CAP = 64
GLA_TAU = 16.0
ROPE_THETA = 10000.0

SLOPES_DIL = np.exp2(-8.0 * np.arange(1, 13) / 12).astype(np.float32)
SLOPES_NSA = np.exp2(-8.0 * np.arange(1, 17) / 16).astype(np.float32)
DIL = ((128, 1), (512, 4), (2048, 16))
NSA_H = 16
HD = 64
CMP_BLOCK = 32
CMP_STRIDE = 16
NCMP = (T - CMP_BLOCK) // CMP_STRIDE + 1
PHI = 256
LRU_C = 8.0

C_IDENT = 0
C_ONES = C_IDENT + P
C_TRIU = C_ONES + P
C_LEVEL = C_TRIU + P
C_CAUSAL = C_LEVEL + LEVELS * P
C_IOTA = C_CAUSAL + TT * T
C_INV = C_IOTA + EXPERTS
C_GRP = C_INV + 64 + 32
C_CDIST = C_GRP + EXPERTS
C_ANY = C_CDIST + TT * 16
C_SLOT = C_ANY + TT
C_PICK = C_SLOT + CAP
C_END = C_PICK + P
CD_END = 4 * TT * T


def constants():
    a = np.zeros((P, C_END), np.float32)
    r, c = np.arange(P)[:, None], np.arange(P)[None, :]
    a[:, C_IDENT:C_IDENT + P] = r == c
    a[:, C_ONES:C_ONES + P] = 1.0
    a[:, C_TRIU:C_TRIU + P] = r <= c
    for n in range(LEVELS):
        s = 1 << n
        a[:, C_LEVEL + n * P:C_LEVEL + (n + 1) * P] = (
            (r // (2 * s) == c // (2 * s)) & (r % (2 * s) < s) & (c % (2 * s) >= s))
    d = np.zeros((P, CD_END), np.float32)
    for t in range(TT):
        i = t * P + np.arange(P)[:, None]
        j = np.arange(T)[None, :]
        dist = (i - j).astype(np.float32)
        a[:, C_CAUSAL + t * T:C_CAUSAL + (t + 1) * T] = np.where(dist >= 0, 0.0, NEG)
        kinds = [dist >= 0] + [(dist >= 0) & (dist % dil == 0) & (dist <= w) for w, dil in DIL]
        for n, ok in enumerate(kinds):
            d[:, (n * TT + t) * T:(n * TT + t + 1) * T] = np.where(ok, dist, FAR)
        end = np.arange(NCMP)[None, :] * CMP_STRIDE + CMP_BLOCK - 1
        cd = (i - end).astype(np.float32)
        a[:, C_CDIST + t * 16:C_CDIST + t * 16 + NCMP] = np.where(cd >= 0, cd, FAR)
        a[:, C_ANY + t] = (cd >= 0).any(axis=1)
    a[::32, C_PICK:C_PICK + P] = 1.0
    a[:, C_SLOT:C_SLOT + CAP] = 1 + np.arange(CAP)
    a[:, C_IOTA:C_IOTA + EXPERTS] = np.arange(EXPERTS)
    a[:, C_GRP:C_GRP + EXPERTS] = np.arange(EXPERTS) // PER_GROUP
    for at, dim in ((C_INV, 128), (C_INV + 64, IDX_DH)):
        a[:, at:at + dim // 2] = 1.0 / (np.float32(ROPE_THETA) ** (np.arange(0, dim, 2, dtype=np.float32) / np.float32(dim)))
    return a, d


class Signal:

    def __init__(self, sem):
        self.sem, self.n, self.start = sem, 0, 0

    def up(self, k=1):
        self.n += k
        return self.sem

    def at(self, k):
        return self.start + k


COL_A = {}
for _name, _rows in (("norm_mix", 16), ("norm_ffn", 16), ("hawk_norm_2", 8), ("nsa_norm_2", 8), ("hawk_mem_norm_2", 8),
                     ("nsa_mem_norm_2", 8), ("hawk_conv_b_2", 8), ("hawk_gate_a_b_2", 8), ("hawk_gate_x_b_2", 8),
                     ("hawk_lambda_2", 8), ("gla_b_gate2", 4), ("c", 8)):
    COL_A[_name] = (sum(n for _, n in COL_A.values()), _rows)
ROWS_A = sum(n for _, n in COL_A.values())
COL_B = {}
for _name, _rows in (("gdn_conv_w", 48), ("hawk_conv_w_2", 32), ("nsa_pe_k_2", 16), ("nsa_pe_v_2", 16)):
    COL_B[_name] = (sum(n for _, n in COL_B.values()), _rows)
ROWS_B = sum(n for _, n in COL_B.values())


def flat(ap):
    names = " ".join(f"d{i}" for i in range(len(ap.shape)))
    return ap.rearrange(f"{names} -> ({names})")


def program(nc, A, consts, dists, out, last_stage=None):
    with ExitStack() as ctx:
        names = {}

        def sb(stack, name, shape, dt=F32):
            names[name] = names.get(name, 0) + 1
            return stack.enter_context(nc.sbuf_tensor(name if names[name] == 1 else f"{name}_{names[name]}", shape, dt))

        def sem(name):
            return ctx.enter_context(nc.semaphore(name))

        ctx.enter_context(nc.allow_non_contiguous_dma(reason="vectors, position columns and narrow weights"))

        ring = sb(ctx, "ring", [P, RING, SLOT])
        x = sb(ctx, "x", [P, TT, D])
        hT = sb(ctx, "hT", [P, KD, T])
        kc = sb(ctx, "kc", [P, C_END])
        ada_bias = sb(ctx, "ada_bias", [2 * 12, 512])
        colA = sb(ctx, "colA", [P, ROWS_A])
        colB = sb(ctx, "colB", [P, ROWS_B])
        bank = [ctx.enter_context(nc.psum_tensor(f"bank{i}", [P, 512], F32)) for i in range(8)]
        expert_out = [nc.dram_tensor(f"expert_out{i}", (EXPERTS * CAP, D), F32, kind="Internal").ap() for i in range(2)]
        gate_rows = nc.dram_tensor("gate_rows", (2, EXPERTS, T), F32, kind="Internal").ap()

        ident = kc[:, C_IDENT:C_IDENT + P]
        ones = kc[:, C_ONES:C_ONES + P]
        triu = kc[:, C_TRIU:C_TRIU + P]

        def level(n):
            return kc[:, C_LEVEL + n * P:C_LEVEL + (n + 1) * P]

        causal = kc[:, C_CAUSAL:C_CAUSAL + TT * T].rearrange("p (t s) -> p t s", t=TT)
        iota = kc[:, C_IOTA:C_IOTA + EXPERTS]
        group_of = kc[:, C_GRP:C_GRP + EXPERTS]
        pick = kc[:, C_PICK:C_PICK + P]
        slot_number = kc[:, C_SLOT:C_SLOT + CAP]
        cmp_dist = kc[:, C_CDIST:C_CDIST + TT * 16].rearrange("p (t n) -> p t n", t=TT)

        def col(name, k0=0, n=None):
            table, where = (colA, COL_A) if name in COL_A else (colB, COL_B)
            at, rows = where[name]
            return table[:, at + k0:at + (rows if n is None else k0 + n)]

        vector_steps = Signal(sem("vector_steps"))
        scalar_steps = Signal(sem("scalar_steps"))
        landed = [Signal(sem(f"slot{i}_landed")) for i in range(RING)]
        chunk_used = Signal(sem("chunk_used"))

        chunks = []

        def cols_of(w, k0, nk, parts):
            width = sum(n for _, n in parts)
            dmas, at = [], 0
            for c0, n in parts:
                src = w[k0 * P:(k0 + nk) * P, c0:c0 + n].rearrange("(k p) n -> p k n", p=P)
                dmas.append((at, n, src))
                at += n
            chunks.append((nk, width, dmas))

        def experts(layer):
            for e in range(EXPERTS):
                chunks.append((KD, FE, [(0, FE, A["exp_w1"][layer, e].rearrange("(k p) n -> p k n", p=P))]))
                chunks.append((KD, FE, [(0, FE, A["exp_w3"][layer, e].rearrange("(k p) n -> p k n", p=P))]))
                chunks.append((FT, D, [(0, D, A["exp_w2"][layer, e].rearrange("(k p) n -> p k n", p=P))]))

        first = {}

        def group(name):
            first[name] = len(chunks)

        for layer in range(2):
            group(f"ada{layer}")
            for j in range(12):
                cols_of(A["ada_w"][layer], 0, KD, [(512 * j, 512)])
            if layer == 0:
                group("even_in")
                w = A["even_w_in"][0]
                for c0 in (0, 512, 1024, 1536, 2056, 2568, 3080):
                    cols_of(w, 0, KD, [(c0, 512)])
                cols_of(w, 0, KD, [(2048, 8), (3592, 324)])
                group("even_out")
                for half in range(2):
                    cols_of(A["even_w_out"][0], 0, KD, [(512 * half, 512)])
            else:
                group("gla_in")
                for j in range(6):
                    cols_of(A["gla_w_in"][0], 0, KD, [(512 * j, 512)])
                cols_of(A["gla_w_in"][0], 0, KD, [(3072, 16)])
                group("gla_out")
                for half in range(2):
                    cols_of(A["gla_w_out"][0], 0, KD, [(512 * half, 512)])
            group(f"experts{layer}")
            experts(layer)
        group("hawk_mem")
        cols_of(A["hawk_w_mem_kv_2"][0], 0, KD, [(0, 512)])
        group("nsa_mem")
        cols_of(A["nsa_w_mem_kv_2"][0], 0, KD, [(0, 512)])
        group("hawk_in")
        for j in [*range(10), 14, 13, 10, 11, 12]:
            cols_of(A["hawk_w_in_2"][0], 0, KD, [(512 * j, 512)])
        group("hawk_out")
        for half in range(2):
            cols_of(A["hawk_w_out_2"][0], 0, 8, [(512 * half, 512)])
            cols_of(A["hawk_w_out_2"][0], 8, 6, [(512 * half, 512)])
        group("nsa_in")
        w = A["nsa_w_in_2"][0]
        for j in range(2):
            cols_of(w, 0, KD, [(512 * j, 512)])
        cols_of(w, 0, KD, [(1024, 64)] * 2 + [(1088, 64)] * 2 + [(1152, 64)] * 2 + [(1216, 64)] * 2)
        cols_of(w, 0, KD, [(1280, 64)] * 2 + [(1344, 64)] * 2 + [(1536, 64)] * 2 + [(1600, 64)] * 2)
        cols_of(w, 0, KD, [(1408, 128), (1664, 128), (1792, 48)])
        for j in range(3):
            cols_of(w, 0, KD, [(1840 + 512 * j, 512)])
        group("nsa_phi")
        for name in ("nsa_phi_k_w1_2", "nsa_phi_v_w1_2"):
            cols_of(A[name][0], 0, 16, [(0, PHI)])
        group("nsa_out")
        for half in range(2):
            cols_of(A["nsa_w_out_2"][0], 0, 8, [(512 * half, 512)])
            cols_of(A["nsa_w_out_2"][0], 8, 2, [(512 * half, 512)])

        landed_at = {}
        freed = {}
        issued = [0]

        def slot(c):
            nk, width, _ = chunks[c]
            return ring[:, c % RING, 0:nk * width].rearrange("p (k n) -> p k n", k=nk)

        def load_chunk(sp, c):
            for at, n, src in chunks[c][2]:
                sp.dma_start(slot(c)[:, :, at:at + n], src).then_inc(landed[c % RING].up(16), 16)
            landed_at[c] = landed[c % RING].n

        for c in range(len(chunks)):
            before = landed_at.get(c - RING, 0)
            landed_at[c] = before + 16 * len(chunks[c][2])

        def fill_ring(sp, last):
            while issued[0] < min(len(chunks), last + 1 + RING):
                c = issued[0]
                if c >= RING:
                    s, n = freed[c - RING]
                    sp.wait_ge(s, n)
                load_chunk(sp, c)
                issued[0] += 1

        def arrived(pe, c):
            pe.wait_ge(landed[c % RING].sem, landed_at[c])

        def frees(c0, n):
            for j in range(n):
                freed[c0 + j] = (chunk_used.sem, chunk_used.n + j + 1)

        signals = {}

        def signal(name):
            s = signals.setdefault(name, None) or Signal(sem(name))
            signals[name] = s
            s.start = s.n
            return s

        st_first = ctx.enter_context(ExitStack())
        router_w = sb(st_first, "router_w", [P, 2, KD, GROUPS + EXPERTS])
        router_b = sb(st_first, "router_b", [1, 2, GROUPS + EXPERTS])
        router_in = signal("router_in")
        with ExitStack() as st:
            rowsA = sb(st, "rowsA", [ROWS_A, P])
            rowsB = sb(st, "rowsB", [ROWS_B, P])
            consts_in, vectors_in, turned = signal("consts_in"), signal("vectors_in"), signal("tiles_turned")
            n_vec = len(COL_A) + len(COL_B) + 1
            with nc.Block() as block:
                @block.sync
                def _(sp):
                    sp.dma_start(kc[:, :], consts).then_inc(consts_in.up(16), 16)
                    for c in range(RING // 2):
                        load_chunk(sp, c)
                        issued[0] += 1
                    sp.wait_ge(consts_in.sem, consts_in.at(16))
                    sp.wait_ge(vectors_in.sem, 16 * (n_vec + 1))
                    fill_ring(sp, -1)

                @block.scalar
                def _(act):
                    for stage_rows, table in ((rowsA, COL_A), (rowsB, COL_B)):
                        for name, (at, n) in table.items():
                            act.dma_start(stage_rows[at:at + n, :],
                                                        flat(A[name]).rearrange("(r p) -> r p", p=P)).then_inc(vectors_in.up(16), 16)
                    act.dma_start(ada_bias[:, :], A["ada_b"].rearrange("l (r n) -> (l r) n", n=512)).then_inc(vectors_in.up(16), 16)
                    act.dma_start(x[:, :, :], A["x"][0].rearrange("(t p) d -> p t d", p=P)).then_inc(vectors_in.up(16), 16)
                    for layer in range(2):
                        act.dma_start(router_w[:, layer, :, 0:GROUPS], A["router_group_w"][layer].rearrange("(k p) g -> p k g", p=P))\
                            .then_inc(router_in.up(16), 16)
                        for g in range(GROUPS):
                            at = GROUPS + PER_GROUP * g
                            act.dma_start(router_w[:, layer, :, at:at + PER_GROUP], A["router_exp_w"][layer, g].rearrange("(k p) e -> p k e", p=P))\
                                .then_inc(router_in.up(16), 16)
                    act.dma_start(router_b[:, :, 0:GROUPS], A["router_group_b"].unsqueeze(0)).then_inc(router_in.up(16), 16)
                    act.dma_start(router_b[:, :, GROUPS:], A["router_exp_b"].rearrange("l g e -> l (g e)").unsqueeze(0)).then_inc(router_in.up(16), 16)

                @block.tensor
                def _(pe):
                    pe.wait_ge(consts_in.sem, consts_in.at(16))
                    pe.wait_ge(vectors_in.sem, vectors_in.at(16 * (n_vec + 1)))
                    nc.tensor.transpose(bank[0][:, 0:ROWS_A], rowsA[:, :], ident[0:ROWS_A, 0:ROWS_A])
                    nc.tensor.transpose(bank[1][:, 0:ROWS_B], rowsB[:, :], ident[0:ROWS_B, 0:ROWS_B]).then_inc(turned.up(), 1)

                @block.vector
                def _(dve):
                    dve.wait_ge(turned.sem, turned.at(1))
                    nc.vector.tensor_copy(colA[:, :], bank[0][:, 0:ROWS_A]).then_inc(vector_steps.up(), 1)
                    dve.wait_ge(vector_steps.sem, vector_steps.n)
                    nc.vector.tensor_copy(colB[:, :], bank[1][:, 0:ROWS_B]).then_inc(vector_steps.up(), 1)
                    dve.wait_ge(vector_steps.sem, vector_steps.n)

        def turn_tiles(pe, src, per_bank):
            for b in range(4):
                for k in (2 * b, 2 * b + 1):
                    for t in range(TT):
                        at = (k % 2) * T + t * P
                        last = nc.tensor.transpose(bank[b][:, at:at + P], src[:, t, k * P:(k + 1) * P], ident)
                last.then_inc(per_bank.up(), 1)

        def norm_stage(src, gain, shift, dst, load=None, xn=None):
            with ExitStack() as st:
                if xn is None:
                    xn = sb(st, "xn", [P, TT, D])
                stat = sb(st, "stat", [P, 3, TT])
                squares, root = signal("mean_square_ready"), signal("root_ready")
                normed, turned, squared, inverse = signal("normed"), signal("tiles_turned"), signal("heads_squared"), signal("norm_inverse_ready")
                src_in = signal("operands_in")
                with nc.Block() as block:
                    @block.vector
                    def _(dve):
                        if load is not None:
                            dve.wait_ge(src_in.sem, src_in.at(16))
                        nc.vector.tensor_tensor_reduce(xn[:, 0, :], src[:, 0, :], src[:, 0, :], 1.0, 0.0, ALU.mult,
                                                       ALU.add, stat[:, 0, 0:1]).then_inc(vector_steps.up(), 1)
                        dve.wait_ge(vector_steps.sem, vector_steps.n)
                        dve.wait_ge(squared.sem, squared.at(1))
                        nc.vector.tensor_scalar(stat[:, 1, :], stat[:, 0, :], 1.0 / D, EPS, ALU.mult, ALU.add).then_inc(squares.up(), 1)
                        dve.wait_ge(root.sem, root.at(1))
                        nc.vector.reciprocal(stat[:, 0, :], stat[:, 2, :]).then_inc(inverse.up(), 1)
                        dve.wait_ge(inverse.sem, inverse.n)
                        nc.vector.tensor_scalar(xn[:, 0, :], src[:, 0, :], stat[:, 0, 0:1], None, ALU.mult).then_inc(normed.up(), 1)
                        for k in (0, 1, 4, 5):
                            dve.wait_ge(turned.sem, turned.at(k // 2 + 1))
                            if gain is None:
                                nc.vector.tensor_copy(dst[:, k, :], bank[k // 2][:, (k % 2) * T:(k % 2 + 1) * T])
                            elif shift is None:
                                nc.vector.tensor_scalar(dst[:, k, :], bank[k // 2][:, (k % 2) * T:(k % 2 + 1) * T], gain[:, k:k + 1], None, ALU.mult)
                            else:
                                nc.vector.tensor_scalar(dst[:, k, :], bank[k // 2][:, (k % 2) * T:(k % 2 + 1) * T], gain[:, k:k + 1],
                                                        shift[:, k:k + 1], ALU.mult, ALU.add)

                    @block.scalar
                    def _(act):
                        if load is not None:
                            act.dma_start(src[:, :, :], load).then_inc(src_in.up(16), 16)
                            act.wait_ge(src_in.sem, src_in.at(16))
                        nc.scalar.activation(xn[:, 1, :], src[:, 1, :], ACT.Square, accum_out=stat[:, 0, 1:2]).then_inc(squared.up(), 1)
                        act.wait_ge(squares.sem, squares.at(1))
                        nc.scalar.activation(stat[:, 2, :], stat[:, 1, :], ACT.Sqrt).then_inc(root.up(), 1)
                        act.wait_ge(inverse.sem, inverse.at(1))
                        nc.scalar.activation(xn[:, 1, :], src[:, 1, :], ACT.Identity, scale=stat[:, 0, 1:2]).then_inc(normed.up(), 1)
                        for k in (2, 3, 6, 7):
                            act.wait_ge(turned.sem, turned.at(k // 2 + 1))
                            if gain is None:
                                nc.scalar.copy(dst[:, k, :], bank[k // 2][:, (k % 2) * T:(k % 2 + 1) * T])
                            elif shift is None:
                                nc.scalar.activation(dst[:, k, :], bank[k // 2][:, (k % 2) * T:(k % 2 + 1) * T], ACT.Identity, scale=gain[:, k:k + 1])
                            else:
                                nc.scalar.activation(dst[:, k, :], bank[k // 2][:, (k % 2) * T:(k % 2 + 1) * T], ACT.Identity, bias=shift[:, k:k + 1],
                                                     scale=gain[:, k:k + 1])

                    @block.tensor
                    def _(pe):
                        pe.wait_ge(normed.sem, normed.at(TT))
                        turn_tiles(pe, xn, turned)

        def turn_stage(src, dst):
            turned = signal("tiles_turned")
            with nc.Block() as block:
                @block.tensor
                def _(pe):
                    turn_tiles(pe, src, turned)

                @block.vector
                def _(dve):
                    for b in range(4):
                        dve.wait_ge(turned.sem, turned.at(b + 1))
                        ins = nc.vector.tensor_copy(dst[:, 2 * b:2 * b + 2, :],
                                                    bank[b][:, :].rearrange("p (k t) -> p k t", k=2))
                    ins.then_inc(vector_steps.up(), 1)
                    dve.wait_ge(vector_steps.sem, vector_steps.n)

        def project_tokens(pe, c, pair, src):
            w = slot(c)
            n = chunks[c][1]
            for t in range(TT):
                for k in range(KD):
                    last = nc.tensor.matmul(pair[t][:, 0:n], src[:, k, t * P:(t + 1) * P], w[:, k, :],
                                            start=(k == 0), stop=(k == KD - 1))
            return last

        def project_channels(pe, c, pair, src):
            w = slot(c)
            n = chunks[c][1]
            for m in range(-(-n // P)):
                rows = min(P, n - m * P)
                for k in range(KD):
                    last = nc.tensor.matmul(pair[m // 2][0:rows, (m % 2) * T:(m % 2 + 1) * T], w[:, k, m * P:m * P + rows],
                                            src[:, k, :], start=(k == 0), stop=(k == KD - 1))
            return last

        def project_keys_values(pe, c, pair, src):
            w = slot(c)
            for m in range(2):
                for k in range(KD):
                    nc.tensor.matmul(pair[0][:, m * T:(m + 1) * T], w[:, k, m * P:(m + 1) * P], src[:, k, :],
                                     start=(k == 0), stop=(k == KD - 1))
            for t in range(TT):
                for k in range(KD):
                    last = nc.tensor.matmul(pair[1][:, t * T:(t + 1) * T], src[:, k, t * P:(t + 1) * P], w[:, k, 256:512],
                                            start=(k == 0), stop=(k == KD - 1))
            return last

        def project_stage(c0, plan, src, pairs=4, tensor_work=None, scalar_work=None, vector_work=None):
            frees(c0, len(plan))
            used0 = chunk_used.n
            evacuated = signal("chunk_evacuated")
            project = {"token": project_tokens, "channel": project_channels, "keys_values": project_keys_values}
            pair = [(bank[2 * i], bank[2 * i + 1]) for i in range(pairs)]
            with nc.Block() as block:
                @block.sync
                def _(sp):
                    fill_ring(sp, c0 + len(plan) - 1)

                @block.tensor
                def _(pe):
                    for j, (kind, _) in enumerate(plan):
                        arrived(pe, c0 + j)
                        if j >= pairs:
                            pe.wait_ge(evacuated.sem, evacuated.at(j - pairs + 1))
                        project[kind](pe, c0 + j, pair[j % pairs], src).then_inc(chunk_used.up(), 1)
                        if tensor_work and j in tensor_work:
                            tensor_work[j](pe)

                @block.scalar
                def _(act):
                    for j, (_, evacuate) in enumerate(plan):
                        act.wait_ge(chunk_used.sem, used0 + j + 1)
                        for d, s, scale in evacuate(pair[j % pairs]):
                            ins = nc.scalar.activation(d, s, ACT.Copy, scale=scale)
                        ins.then_inc(evacuated.up(), 1)
                        if scalar_work and j in scalar_work:
                            scalar_work[j](act)

                @block.vector
                def _(dve):
                    if vector_work:
                        vector_work(dve, evacuated)

        def to_tokens(dst, at=0, n=512, scale=1.0, src_at=0):
            return lambda pair: [(dst[:, t, at:at + n], pair[t][:, src_at:src_at + n], scale) for t in range(TT)]

        def to_channels(dst, m0, scale=1.0):
            return lambda pair: [(dst[:, m0 + 2 * b:m0 + 2 * b + 2, :], pair[b][:, :].rearrange("p (m t) -> p m t", m=2), scale)
                                 for b in range(2)]

        def out_stage(c0, parts, src, gate):
            n = 2 * len(parts)
            frees(c0, n)
            used0 = chunk_used.n
            last_k = parts[-1][0] + parts[-1][1] - 1
            with ExitStack() as st:
                gated = sb(st, "gated", [P, 512])
                with nc.Block() as block:
                    @block.sync
                    def _(sp):
                        fill_ring(sp, c0 + n - 1)

                    @block.tensor
                    def _(pe):
                        for half in range(2):
                            for i, (k0, nk) in enumerate(parts):
                                c = c0 + half * len(parts) + i
                                arrived(pe, c)
                                w = slot(c)
                                for t in range(TT):
                                    for k in range(nk):
                                        last = nc.tensor.matmul(bank[2 * half + t][:, :], src[:, k0 + k, t * P:(t + 1) * P],
                                                                w[:, k, :], start=(k0 + k == 0), stop=(k0 + k == last_k))
                                last.then_inc(chunk_used.up(), 1)

                    @block.vector
                    def _(dve):
                        for half in range(2):
                            dve.wait_ge(chunk_used.sem, used0 + (half + 1) * len(parts))
                            for t in range(TT):
                                part = bank[2 * half + t][:, :]
                                if gate is not None:
                                    nc.vector.tensor_tensor(gated[:, :], part, gate[:, half * 512:(half + 1) * 512], ALU.mult).then_inc(vector_steps.up(), 1)
                                    dve.wait_ge(vector_steps.sem, vector_steps.n)
                                    part = gated[:, :]
                                xs = x[:, t, half * 512:(half + 1) * 512]
                                nc.vector.tensor_tensor(xs, xs, part, ALU.add).then_inc(vector_steps.up(), 1)
                                dve.wait_ge(vector_steps.sem, vector_steps.n)

        def modulation_work(layer, st, gates, mod):
            c0 = first[f"ada{layer}"]
            frees(c0, 12)
            used0 = chunk_used.n
            cond = sb(st, "cond", [P, KD, 32])
            silu_c = sb(st, "silu_c", [P, KD])
            parts = sb(st, "mod_parts", [P, 2, 512])
            cols = sb(st, "mod_cols", [P, 4, KD])
            silu_ready, cond_ready = signal("silu_c_ready"), signal("cond_ready")
            parts_copied, picked = signal("mod_parts_copied"), signal("mod_parts_summed")
            kinds = [0, 1, None, 2, 3, None]

            def silu_condition(act):
                nc.scalar.activation(silu_c[:, :], col("c"), ACT.Silu).then_inc(silu_ready.up(), 1)

            def spread_condition(dve):
                dve.wait_ge(silu_ready.sem, silu_ready.at(1))
                nc.vector.tensor_copy(cond[:, :, :], silu_c[:, :].unsqueeze(2).to_broadcast([P, KD, 32])).then_inc(cond_ready.up(), 1)

            def products(pe):
                def sum_parts(j):
                    pe.wait_ge(parts_copied.sem, parts_copied.at(j + 1))
                    kind = kinds[j // 2]
                    if kind is None:
                        last = nc.tensor.matmul(bank[2 + 2 * (j // 6) + j % 2][:, :], pick, parts[:, j % 2, :], start=True, stop=True)
                    else:
                        for m in range(4):
                            at = kind * KD + (j % 2) * 4 + m
                            last = nc.tensor.matmul(bank[7][:, at:at + 1], parts[:, j % 2, m * P:(m + 1) * P], pick[:, 0:1],
                                                    start=True, stop=True)
                    last.then_inc(picked.up(), 1)

                pe.wait_ge(cond_ready.sem, cond_ready.at(1))
                for j in range(12):
                    arrived(pe, c0 + j)
                    for k in range(KD):
                        g = k % 4
                        last = nc.tensor.matmul(bank[j % 2][32 * g:32 * g + 32, :], cond[:, k, :], slot(c0 + j)[:, k, :],
                                                start=(k < 4), stop=(4 < k))
                    row = 12 * layer + j
                    last = nc.tensor.matmul(bank[j % 2][0:32, :], ident[0:24, row:row + 1].to_broadcast([24, 32]), ada_bias[:, :],
                                            start=False, stop=True)
                    last.then_inc(chunk_used.up(), 1)
                    if j:
                        sum_parts(j - 1)
                sum_parts(11)

            def copy_parts(act):
                for j in range(12):
                    act.wait_ge(chunk_used.sem, used0 + j + 1)
                    nc.scalar.copy(parts[:, j % 2, :], bank[j % 2][:, :]).then_inc(parts_copied.up(), 1)

            def rows_and_columns(dve):
                for n, j in enumerate((4, 5, 10, 11)):
                    dve.wait_ge(picked.sem, picked.at(j + 1))
                    ins = nc.vector.tensor_copy(gates[:, n // 2, (n % 2) * 512:(n % 2 + 1) * 512], bank[2 + n][:, :])
                nc.vector.tensor_copy(cols[:, :, :], bank[7][:, 0:4 * KD].rearrange("p (q k) -> p q k", q=4)).then_inc(vector_steps.up(), 1)
                dve.wait_ge(vector_steps.sem, vector_steps.n)
                for half, name in ((0, "norm_mix"), (1, "norm_ffn")):
                    nc.vector.tensor_copy(mod[:, 2 * half + 1, :], cols[:, 2 * half, :])
                    nc.vector.scalar_tensor_tensor(mod[:, 2 * half, :], cols[:, 2 * half + 1, :], 1.0,
                                                   col(name, 8 * layer, KD), ALU.add, ALU.mult).then_inc(vector_steps.up(), 1)
                dve.wait_ge(vector_steps.sem, vector_steps.n)

            return silu_condition, spread_condition, products, copy_parts, rows_and_columns, c0 + 11

        def modulation_stage(layer, gates, mod):
            with ExitStack() as st:
                silu_condition, spread_condition, products, copy_parts, rows_and_columns, last = modulation_work(layer, st, gates, mod)
                with nc.Block() as block:
                    @block.sync
                    def _(sp):
                        fill_ring(sp, last)

                    @block.scalar
                    def _(act):
                        silu_condition(act)
                        copy_parts(act)

                    @block.vector
                    def _(dve):
                        spread_condition(dve)
                        rows_and_columns(dve)

                    @block.tensor
                    def _(pe):
                        products(pe)


        def even_mixer(mixed):
            with ExitStack() as st:
                conv = sb(st, "conv", [P, 12, T])
                za = sb(st, "za", [P, TT, 512])
                small = sb(st, "small", [P, TT, 332])
                with ExitStack() as st_att:
                    qb = sb(st_att, "qb", [P, TT, 512])
                    kb = sb(st_att, "kb", [P, TT, 512])
                    vb = sb(st_att, "vb", [P, TT, 512])
                    qr, kr = (mixed[:, :, n * 512:(n + 1) * 512].rearrange("p t (h d) -> p t h d", h=H) for n in range(2))
                    ir = sb(st_att, "ir", [P, TT, 6, IDX_DH])
                    with ExitStack() as st_raw:
                        raw = sb(st_raw, "raw", [P, 12, T + CONV - 1])
                        pos_i = sb(st_raw, "pos_i", [P, TT], I32)
                        angle, turns, sin, cos = (sb(st_raw, name, [P, TT, 96]) for name in ("angle", "turns", "sin", "cos"))
                        t1 = sb(st_raw, "rope_t1", [P, TT, 5 * 64])
                        t2 = sb(st_raw, "rope_t2", [P, TT, 5 * 64])
                        pos_in, convolved = signal("positions_in"), signal("convolved")
                        reduced, folded, sin_ready = signal("angle_reduced"), signal("angle_folded"), signal("sin_cos_ready")

                        def to_raw(m0):
                            return lambda pair: [(raw[:, m0 + 2 * b:m0 + 2 * b + 2, CONV - 1:], pair[b][:, :].rearrange("p (m t) -> p m t", m=2), 1.0)
                                                 for b in range(2)]

                        def load_positions(act):
                            act.dma_start(pos_i[:, :], A["positions"].rearrange("a (t p) -> p (a t)", p=P)).then_inc(pos_in.up(16), 16)

                        def sines(act):
                            act.wait_ge(reduced.sem, reduced.at(1))
                            nc.scalar.activation(sin[:, :, :], angle[:, :, :], ACT.Sin)
                            act.wait_ge(folded.sem, folded.at(1))
                            nc.scalar.activation(cos[:, :, :], turns[:, :, :], ACT.Sin).then_inc(sin_ready.up(), 1)

                        def silu_conv(act):
                            act.wait_ge(convolved.sem, convolved.at(1))
                            nc.scalar.activation(conv[:, :, :], conv[:, :, :], ACT.Silu).then_inc(scalar_steps.up(), 1)

                        def convolve_and_rotate(dve, evacuated):
                            dve.wait_ge(pos_in.sem, pos_in.at(16))
                            reduce_angles(dve, pos_i, angle, turns, reduced, folded)
                            dve.wait_ge(evacuated.sem, evacuated.at(3))
                            convolve(dve, raw, conv, 12, "gdn_conv_w", None, convolved)
                            dve.wait_ge(sin_ready.sem, sin_ready.at(1))
                            for n, (src, dst) in enumerate(((qb, qr), (kb, kr))):
                                dve.wait_ge(evacuated.sem, evacuated.at(5 + n))
                                rotate(dve, dst, src[:, :, :].rearrange("p t (h d) -> p t h d", h=H), H, 64,
                                       cos[:, :, 0:64], sin[:, :, 0:64], t1, t2)
                            dve.wait_ge(evacuated.sem, evacuated.at(8))
                            rotate(dve, ir[:, :, 0:5, :], small[:, :, 8:328].rearrange("p t (h d) -> p t h d", h=5), 5, 32,
                                   cos[:, :, 64:96], sin[:, :, 64:96], t1, t2)
                            nc.vector.tensor_copy(ir[:, :, 5, :], ir[:, :, 4, :])

                        project_stage(first["even_in"], [("channel", to_raw(0)), ("channel", to_raw(4)), ("channel", to_raw(8)),
                                                         ("token", to_tokens(za)), ("token", to_tokens(qb)), ("token", to_tokens(kb)),
                                                         ("token", to_tokens(vb)), ("token", to_tokens(small, 0, 332))], hT,
                                      scalar_work={0: load_positions, 3: sines, 6: silu_conv}, vector_work=convolve_and_rotate)
                    sparse_attention(mixed, qr, kr, ir, vb, small, qb, kb)
                delta_rule(mixed, conv, za, small)

        def convolve(dve, raw, conv, tiles, weights, bias, convolved):
            nc.vector.memset(raw[:, :, 0:CONV - 1], 0.0).then_inc(vector_steps.up(), 1)
            dve.wait_ge(vector_steps.sem, vector_steps.n)
            for i in range(CONV):
                for m in range(tiles):
                    w = col(weights, i * tiles + m, 1)
                    if i == 0 and bias is not None:
                        ins = nc.vector.tensor_scalar(conv[:, m, :], raw[:, m, 0:T], w, col(bias, m, 1), ALU.mult, ALU.add)
                    elif i == 0:
                        ins = nc.vector.tensor_scalar(conv[:, m, :], raw[:, m, 0:T], w, None, ALU.mult)
                    else:
                        ins = nc.vector.scalar_tensor_tensor(conv[:, m, :], raw[:, m, i:i + T], w, conv[:, m, :], ALU.mult, ALU.add)
                ins.then_inc(convolved.sem if i == CONV - 1 else vector_steps.up(), 1)
                if i < CONV - 1:
                    dve.wait_ge(vector_steps.sem, vector_steps.n)
            convolved.n += 1

        def reduce_angles(dve, pos_i, angle, turns, reduced, folded):
            turn = 2.0 * np.pi
            c1 = 6.28125
            c2 = float(np.float32(np.floor((turn - c1) * 2.0 ** 20) / 2.0 ** 20))
            c3 = float(np.float32(turn - c1 - c2))
            magic = 1.5 * 2.0 ** 23
            pos = turns[:, :, 0]
            nc.vector.tensor_copy(pos, pos_i[:, :]).then_inc(vector_steps.up(), 1)
            dve.wait_ge(vector_steps.sem, vector_steps.n)
            for t in range(TT):
                ins = nc.vector.tensor_scalar(angle[:, t, :], kc[:, C_INV:C_INV + 96], turns[:, t, 0:1], None, ALU.mult)
            ins.then_inc(vector_steps.up(), 1)
            dve.wait_ge(vector_steps.sem, vector_steps.n)
            nc.vector.tensor_scalar(turns[:, :, :], angle[:, :, :], 1.0 / turn, magic, ALU.mult, ALU.add).then_inc(vector_steps.up(), 1)
            dve.wait_ge(vector_steps.sem, vector_steps.n)
            nc.vector.tensor_scalar(turns[:, :, :], turns[:, :, :], magic, None, ALU.subtract).then_inc(vector_steps.up(), 1)
            dve.wait_ge(vector_steps.sem, vector_steps.n)
            for part in (c1, c2, c3):
                nc.vector.scalar_tensor_tensor(angle[:, :, :], turns[:, :, :], -part, angle[:, :, :], ALU.mult, ALU.add).then_inc(vector_steps.up(), 1)
                dve.wait_ge(vector_steps.sem, vector_steps.n)
            nc.vector.tensor_scalar(angle[:, :, :], angle[:, :, :], 3.1415925, -3.1415925, ALU.min, ALU.max).then_inc(reduced.up(), 1)
            dve.wait_ge(reduced.sem, reduced.n)
            nc.vector.scalar_tensor_tensor(turns[:, :, :], angle[:, :, :], -1.0, angle[:, :, :], ALU.mult, ALU.min).then_inc(vector_steps.up(), 1)
            dve.wait_ge(vector_steps.sem, vector_steps.n)
            nc.vector.tensor_scalar(turns[:, :, :], turns[:, :, :], float(np.pi / 2), None, ALU.add).then_inc(folded.up(), 1)

        def rotate(dve, dst, src, heads, half, cos, sin, t1, t2):
            t1, t2 = (t[:, :, 0:heads * half].rearrange("p t (h d) -> p t h d", h=heads) for t in (t1, t2))

            def table(a):
                return a.unsqueeze(2).to_broadcast([P, TT, heads, half])
            a, b = src[:, :, :, 0:half], src[:, :, :, half:2 * half]
            nc.vector.tensor_tensor(t1, a, table(cos), ALU.mult)
            nc.vector.tensor_tensor(t2, b, table(sin), ALU.mult).then_inc(vector_steps.up(), 1)
            dve.wait_ge(vector_steps.sem, vector_steps.n)
            nc.vector.tensor_tensor(dst[:, :, :, 0:half], t1, t2, ALU.subtract).then_inc(vector_steps.up(), 1)
            dve.wait_ge(vector_steps.sem, vector_steps.n)
            nc.vector.tensor_tensor(t1, b, table(cos), ALU.mult)
            nc.vector.tensor_tensor(t2, a, table(sin), ALU.mult).then_inc(vector_steps.up(), 1)
            dve.wait_ge(vector_steps.sem, vector_steps.n)
            nc.vector.tensor_tensor(dst[:, :, :, half:2 * half], t1, t2, ALU.add).then_inc(vector_steps.up(), 1)
            dve.wait_ge(vector_steps.sem, vector_steps.n)

        def sparse_attention(mixed, qr, kr, ir, vb, small, qb, kb):
            scale = float(P) ** -0.5
            with ExitStack() as st:
                qT = sb(st, "qT", [P, H, T])
                kT = sb(st, "kT", [P, H, T])
                iT = sb(st, "iT", [P, 3, T])
                turned = signal("tiles_turned")
                with nc.Block() as block:
                    @block.vector
                    def _(dve):
                        for n, (dst, m0, m, s) in enumerate(((qT, 0, 2, scale), (qT, 2, 2, scale), (kT, 0, 2, 1.0), (kT, 2, 2, 1.0),
                                                             (iT, 0, 2, 1.0), (iT, 2, 1, 1.0))):
                            dve.wait_ge(turned.sem, turned.at(n + 1))
                            ins = nc.vector.tensor_scalar(dst[:, m0:m0 + m, :], bank[n][:, 0:m * T].rearrange("p (m t) -> p m t", m=m),
                                                          s, None, ALU.mult)

                    @block.tensor
                    def _(pe):
                        tiles = [qr[:, :, h, :] for h in range(H)] + [kr[:, :, h, :] for h in range(H)]
                        tiles += [ir[:, :, 2 * m:2 * m + 2, :] for m in range(3)]
                        for n, tile in enumerate(tiles):
                            for t in range(TT):
                                at = (n % 2) * T + t * P
                                src = tile[:, t] if n < 8 else tile[:, t].rearrange("p h d -> p (h d)")
                                last = nc.tensor.transpose(bank[n // 2][:, at:at + P], src, ident)
                            if n % 2 == 1 or n == 10:
                                last.then_inc(turned.up(), 1)

                wi = sb(st, "wi", [P, TT, H])
                rel = sb(st, "rel", [P, TT, H, T])
                probs = rel
                score = sb(st, "score", [P, TT, T])
                top8 = sb(st, "top8", [P, TT, 8])
                keep = sb(st, "keep", [P, TT, T])
                stat = sb(st, "att_stat", [P, TT, 3, H])
                probsT = [room[:, :, :].rearrange("p t (h s) -> p (t h) s", s=P).rearrange("p (h b) s -> p h b s", b=TT) for room in (qb, kb)]
                dots_ready, logits_ready = signal("index_dots_ready"), signal("att_logits_ready")
                shifted, exped, normal = signal("att_max_ready"), signal("att_exp_ready"), signal("att_probs_ready")
                turned, probsT_ready, out_ready = signal("att_probs_turned"), signal("att_probsT_ready"), signal("att_out_ready")
                with nc.Block() as block:
                    @block.tensor
                    def _(pe):
                        for t in range(TT):
                            for h in range(H):
                                lo = (h % 2) * IDX_DH
                                last = nc.tensor.matmul(bank[4 * t + h % 2][:, (h // 2) * T:(h // 2 + 1) * T],
                                                        iT[lo:lo + IDX_DH, h // 2, t * P:(t + 1) * P], iT[lo:lo + IDX_DH, 2, :],
                                                        start=True, stop=True)
                            last.then_inc(dots_ready.up(), 1)
                        for t in range(TT):
                            for h in range(H):
                                last = nc.tensor.matmul(bank[4 * t + 2 + h // 2][:, (h % 2) * T:(h % 2 + 1) * T],
                                                        qT[:, h, t * P:(t + 1) * P], kT[:, h, :], start=True, stop=True)
                            last.then_inc(logits_ready.up(), 1)
                        for t in range(TT):
                            pe.wait_ge(normal.sem, normal.at(t + 1))
                            for h in range(H):
                                for b in range(TT):
                                    at = ((h % 2) * TT + b) * P
                                    last = nc.tensor.transpose(bank[4 * t + h // 2][:, at:at + P], probs[:, t, h, b * P:(b + 1) * P], ident)
                            last.then_inc(turned.up(), 1)
                        for t in range(TT):
                            pe.wait_ge(probsT_ready.sem, probsT_ready.at(t + 1))
                            for h in range(H):
                                for b in range(TT):
                                    last = nc.tensor.matmul(bank[4 * t + 2][:, h * P:(h + 1) * P], probsT[t][:, h, b, :], vb[:, b, h * P:(h + 1) * P],
                                                            start=(b == 0), stop=(b == TT - 1))
                            last.then_inc(out_ready.up(), 1)

                    @block.vector
                    def _(dve):
                        def step(ins):
                            ins.then_inc(vector_steps.up(), 1)
                            dve.wait_ge(vector_steps.sem, vector_steps.n)

                        step(nc.vector.tensor_scalar(wi[:, :, :], small[:, :, 328:332], (H * IDX_DH) ** -0.5, None, ALU.mult))
                        for t in range(TT):
                            dve.wait_ge(dots_ready.sem, dots_ready.at(t + 1))
                            for h in range(H):
                                ins = nc.vector.tensor_scalar(rel[:, t, h, :], bank[4 * t + h % 2][:, (h // 2) * T:(h // 2 + 1) * T], 0.0,
                                                              wi[:, t, h:h + 1], ALU.max, ALU.mult)
                        step(ins)
                        step(nc.vector.tensor_tensor(score[:, :, :], rel[:, :, 0, :], rel[:, :, 1, :], ALU.add))
                        step(nc.vector.tensor_tensor(score[:, :, :], score[:, :, :], rel[:, :, 2, :], ALU.add))
                        step(nc.vector.tensor_tensor(score[:, :, :], score[:, :, :], rel[:, :, 3, :], ALU.add))
                        step(nc.vector.tensor_tensor(score[:, :, :], score[:, :, :], causal, ALU.add))
                        for _ in range(TOPK // 8):
                            for t in range(TT):
                                ins = nc.vector.max(top8[:, t, :], score[:, t, :])
                            step(ins)
                            for t in range(TT):
                                ins = nc.vector.match_replace(score[:, t, :], top8[:, t, :], score[:, t, :], TAKEN)
                            step(ins)
                        step(nc.vector.tensor_scalar(keep[:, :, :], score[:, :, :], TAKEN, -NEG, ALU.is_equal, ALU.mult))
                        step(nc.vector.scalar_tensor_tensor(keep[:, :, :], keep[:, :, :], NEG, causal, ALU.add, ALU.add))
                        for t in range(TT):
                            dve.wait_ge(logits_ready.sem, logits_ready.at(t + 1))
                            for b in range(2):
                                ins = nc.vector.tensor_tensor(probs[:, t, 2 * b:2 * b + 2, :],
                                                              bank[4 * t + 2 + b][:, :].rearrange("p (h s) -> p h s", h=2),
                                                              keep[:, t, :].unsqueeze(1).to_broadcast([P, 2, T]), ALU.add)
                            step(ins)
                            nc.vector.tensor_reduce(stat[:, t, 0, :], probs[:, t, :, :], AX.X, ALU.max, negate=True).then_inc(shifted.up(), 1)
                        for t in range(TT):
                            dve.wait_ge(exped.sem, exped.at(t + 1))
                            step(nc.vector.reciprocal(stat[:, t, 2, :], stat[:, t, 1, :]))
                            nc.vector.tensor_tensor(probs[:, t, :, :], probs[:, t, :, :], stat[:, t, 2, :].unsqueeze(2).to_broadcast([P, H, T]),
                                                    ALU.mult).then_inc(normal.up(), 1)
                        for t in range(TT):
                            dve.wait_ge(out_ready.sem, out_ready.at(t + 1))
                            nc.vector.tensor_copy(mixed[:, t, 512:1024], bank[4 * t + 2][:, :])

                    @block.scalar
                    def _(act):
                        for t in range(TT):
                            act.wait_ge(shifted.sem, shifted.at(t + 1))
                            for h in range(H):
                                ins = nc.scalar.activation(probs[:, t, h, :], probs[:, t, h, :], ACT.Exp, bias=stat[:, t, 0, h:h + 1],
                                                           accum_out=stat[:, t, 1, h:h + 1])
                            ins.then_inc(exped.up(), 1)
                        for t in range(TT):
                            act.wait_ge(turned.sem, turned.at(t + 1))
                            for b in range(2):
                                ins = nc.scalar.copy(probsT[t][:, 2 * b:2 * b + 2, :, :].rearrange("p h b s -> p (h b s)"), bank[4 * t + b][:, :])
                            ins.then_inc(probsT_ready.up(), 1)

        def delta_rule(mixed, conv, za, small):
            U = TT * H
            with ExitStack() as st:
                gates = sb(st, "gdn_gates", [P, 8, U])
                beta, g, gc, egc, kscale, tmp, tmp2 = (gates[:, i, :] for i in range(7))
                invT = sb(st, "invT", [P, U, P])
                aqk = sb(st, "aqk", [P, U, P])
                qg = sb(st, "qg", [P, H, P])
                with ExitStack() as st_n:
                    sq = sb(st_n, "qk_sq", [P, 8, T])
                    rn = sb(st_n, "qk_rn", [P, 2, 8 * TT])
                    vec = sb(st_n, "gdn_vec", [P, 2, H])
                    squared, summed, rooted = signal("qk_squared"), signal("qk_summed"), signal("root_ready")
                    inverse, spread = signal("norm_inverse_ready"), signal("qk_norms_spread")
                    vec_in, softened, exp1 = signal("operands_in"), signal("gdn_gate_in"), signal("gdn_exp1")
                    with nc.Block() as block:
                        @block.vector
                        def _(dve):
                            nc.vector.tensor_tensor(sq[:, :, :], conv[:, 0:8, :], conv[:, 0:8, :], ALU.mult).then_inc(squared.up(), 1)
                            for t in range(TT):
                                nc.vector.tensor_copy(beta[:, t * H:(t + 1) * H], small[:, t, 0:H]).then_inc(vector_steps.up(), 1)
                                dve.wait_ge(vector_steps.sem, vector_steps.n)
                            dve.wait_ge(vec_in.sem, vec_in.at(32))
                            for t in range(TT):
                                nc.vector.tensor_tensor(g[:, t * H:(t + 1) * H], small[:, t, H:2 * H], vec[:, 1, :], ALU.add).then_inc(vector_steps.up(), 1)
                                dve.wait_ge(vector_steps.sem, vector_steps.n)
                            nc.vector.scalar_tensor_tensor(gates[:, 5, :], g, -1.0, g, ALU.mult, ALU.max).then_inc(softened.up(), 1)
                            dve.wait_ge(rooted.sem, rooted.at(1))
                            nc.vector.reciprocal(rn[:, 1, :], rn[:, 0, :]).then_inc(inverse.up(), 1)
                            dve.wait_ge(exp1.sem, exp1.at(1))
                            nc.vector.tensor_scalar(beta, beta, 1.0, None, ALU.add).then_inc(vector_steps.up(), 1)
                            dve.wait_ge(vector_steps.sem, vector_steps.n)
                            nc.vector.reciprocal(beta, beta).then_inc(vector_steps.up(), 1)
                            dve.wait_ge(vector_steps.sem, vector_steps.n)
                            nc.vector.scalar_tensor_tensor(g, g, 0.0, gates[:, 5, :], ALU.max, ALU.add).then_inc(vector_steps.up(), 1)
                            dve.wait_ge(vector_steps.sem, vector_steps.n)
                            for t in range(TT):
                                nc.vector.scalar_tensor_tensor(g[:, t * H:(t + 1) * H], g[:, t * H:(t + 1) * H], -1.0, vec[:, 0, :],
                                                                        ALU.mult, ALU.mult).then_inc(vector_steps.up(), 1)
                                dve.wait_ge(vector_steps.sem, vector_steps.n)
                            for b in range(4):
                                s = slice(2 * b, 2 * b + 2)
                                dve.wait_ge(spread.sem, spread.at(b + 1))
                                nc.vector.scalar_tensor_tensor(conv[:, s, :], conv[:, s, :], float(P) ** -0.5 if b < 2 else 1.0,
                                                               bank[1 + b][:, :].rearrange("p (h t) -> p h t", h=2), ALU.mult, ALU.mult)

                        @block.tensor
                        def _(pe):
                            pe.wait_ge(squared.sem, squared.at(1))
                            for j in range(8 * TT):
                                last = nc.tensor.matmul(bank[0][:, j:j + 1], sq[:, j // TT, (j % TT) * P:(j % TT + 1) * P], ones[:, 0:1],
                                                        start=True, stop=True)
                            last.then_inc(summed.up(), 1)
                            pe.wait_ge(inverse.sem, inverse.at(1))
                            for b in range(4):
                                for i in range(2 * TT):
                                    j = 2 * TT * b + i
                                    last = nc.tensor.matmul(bank[1 + b][:, i * P:(i + 1) * P], rn[:, 1, j:j + 1].to_broadcast([P, P]), ident,
                                                            start=True, stop=True)
                                last.then_inc(spread.up(), 1)

                        @block.scalar
                        def _(act):
                            act.dma_start(vec[:, 0, :], A["gdn_a_log"][0].partition_broadcast(P)).then_inc(vec_in.up(16), 16)
                            act.dma_start(vec[:, 1, :], A["gdn_dt_bias"][0].partition_broadcast(P)).then_inc(vec_in.up(16), 16)
                            act.wait_ge(summed.sem, summed.at(1))
                            nc.scalar.activation(rn[:, 0, :], bank[0][:, 0:8 * TT], ACT.Sqrt, bias=EPS).then_inc(rooted.up(), 1)
                            act.wait_ge(softened.sem, softened.at(1))
                            nc.scalar.activation(gates[:, 5, :], gates[:, 5, :], ACT.Exp, scale=-1.0)
                            nc.scalar.activation(vec[:, 0, :], vec[:, 0, :], ACT.Exp)
                            nc.scalar.activation(beta, beta, ACT.Exp, scale=-1.0).then_inc(scalar_steps.up(), 1)
                            act.wait_ge(scalar_steps.sem, scalar_steps.n)
                            nc.scalar.activation(gates[:, 5, :], gates[:, 5, :], ACT.Ln, bias=1.0).then_inc(exp1.up(), 1)

                def qT(u):
                    return conv[:, u % H, (u // H) * P:(u // H + 1) * P]

                def kT(u):
                    return conv[:, H + u % H, (u // H) * P:(u // H + 1) * P]

                with ExitStack() as st_d:
                    decay = sb(st_d, "decay", [P, U, P])
                    wide = sb(st_d, "wide", [P, U, P])
                    inv = sb(st_d, "inv", [P, U, P])
                    step = sb(st_d, "inv_step", [P, U, P])
                    lower = sb(st_d, "lower", [P, U, P])
                    g_ready, cum, diff, decayed = signal("gdn_g_ready"), signal("gdn_cum_ready"), signal("gdn_diff_ready"), signal("gdn_decay_ready")
                    products, masked, turned0 = signal("gdn_products_ready"), signal("gdn_masked"), signal("gdn_first_turned")
                    level_in, x_ready, x_copied, x2_ready = signal("level_in"), signal("level_x_ready"), signal("level_x_copied"), signal("level_terms_ready")
                    inv_ready = signal("level_inverse_ready")
                    masks = (wide, decay)

                    def halves(t):
                        return [t[:, 4 * b:4 * b + 4, :].rearrange("p u i -> p (u i)") for b in range(2)]

                    with nc.Block() as block:
                        @block.scalar
                        def _(act):
                            act.wait_ge(diff.sem, diff.at(1))
                            nc.scalar.activation(decay[:, :, :], decay[:, :, :], ACT.Exp)
                            nc.scalar.activation(egc, gc, ACT.Exp)
                            nc.scalar.activation(kscale, kscale, ACT.Exp)
                            nc.scalar.activation(qg[:, :, :], qg[:, :, :], ACT.Exp).then_inc(decayed.up(), 1)
                            for n in range(1, LEVELS):
                                for b in range(2):
                                    act.wait_ge(x_ready.sem, x_ready.at(2 * (n - 1) + b + 1))
                                    nc.scalar.copy(halves(step)[b], bank[1 + b][:, :]).then_inc(x_copied.up(), 1)

                        @block.vector
                        def _(dve):
                            nc.vector.tensor_copy(step[:, :, :], beta.unsqueeze(2).to_broadcast([P, U, P]))
                            nc.vector.tensor_copy(wide[:, :, :], g.unsqueeze(2).to_broadcast([P, U, P])).then_inc(g_ready.up(), 1)
                            dve.wait_ge(cum.sem, cum.at(1))
                            nc.vector.tensor_copy(gc, bank[0][:, 0:U]).then_inc(vector_steps.up(), 1)
                            dve.wait_ge(vector_steps.sem, vector_steps.n)
                            for u in range(U):
                                row = bank[1 + u // H][:, (u % H) * P:(u % H + 1) * P]
                                nc.vector.tensor_scalar(decay[:, u, :], row, gc[:, u:u + 1], 0.0, ALU.subtract, ALU.min)
                            for h in range(H):
                                ins = nc.vector.tensor_scalar(kscale[:, h:h + 1], bank[1][:, h * P + P - 1:h * P + P], gc[:, h:h + 1], None, ALU.subtract)
                            for h in range(H):
                                nc.vector.tensor_copy(kscale[:, H + h:H + h + 1], gc[:, H + h:H + h + 1])
                            nc.vector.tensor_copy(qg[:, :, :], bank[2][:, :].rearrange("p (h i) -> p h i", h=H)).then_inc(diff.up(), 1)
                            dve.wait_ge(decayed.sem, decayed.at(1))
                            dve.wait_ge(products.sem, products.at(1))
                            nc.vector.tensor_tensor(wide[:, :, :], decay[:, :, :], triu.unsqueeze(1).to_broadcast([P, U, P]), ALU.mult).then_inc(vector_steps.up(), 1)
                            dve.wait_ge(vector_steps.sem, vector_steps.n)
                            for b in range(2):
                                nc.vector.tensor_tensor(halves(aqk)[b], bank[5 + b][:, :], halves(wide)[b], ALU.mult).then_inc(vector_steps.up(), 1)
                                dve.wait_ge(vector_steps.sem, vector_steps.n)
                                nc.vector.tensor_tensor(halves(lower)[b], bank[3 + b][:, :], halves(decay)[b], ALU.mult).then_inc(vector_steps.up(), 1)
                                dve.wait_ge(vector_steps.sem, vector_steps.n)
                                nc.vector.tensor_tensor(halves(lower)[b], halves(lower)[b], bank[(7, 0)[b]][:, :], ALU.mult).then_inc(vector_steps.up(), 1)
                                dve.wait_ge(vector_steps.sem, vector_steps.n)
                            wideI = ident.unsqueeze(1).to_broadcast([P, U, P])
                            nc.vector.tensor_tensor(wide[:, :, :], lower[:, :, :], level(0).unsqueeze(1).to_broadcast([P, U, P]), ALU.mult).then_inc(vector_steps.up(), 1)
                            dve.wait_ge(vector_steps.sem, vector_steps.n)
                            nc.vector.tensor_tensor(invT[:, :, :], wideI, wide[:, :, :], ALU.subtract).then_inc(masked.up(), 1)
                            dve.wait_ge(turned0.sem, turned0.at(1))
                            for b in range(2):
                                nc.vector.tensor_copy(halves(inv)[b], bank[1 + b][:, :]).then_inc(vector_steps.up(), 1)
                                dve.wait_ge(vector_steps.sem, vector_steps.n)
                            def mask_level(n):
                                nc.vector.tensor_tensor(masks[n % 2][:, :, :], lower[:, :, :], level(n).unsqueeze(1).to_broadcast([P, U, P]),
                                                        ALU.mult).then_inc(level_in.up(), 1)

                            mask_level(1)
                            for n in range(1, LEVELS):
                                if n < LEVELS - 1:
                                    mask_level(n + 1)
                                for b in range(2):
                                    dve.wait_ge(x2_ready.sem, x2_ready.at(2 * (n - 1) + b + 1))
                                    ins = nc.vector.tensor_tensor(halves(invT)[b], halves(invT)[b], bank[3 + b][:, :], ALU.subtract)
                                    if n < LEVELS - 1:
                                        ins = nc.vector.tensor_tensor(halves(inv)[b], halves(inv)[b], bank[5 + b][:, :], ALU.subtract)
                                    ins.then_inc(inv_ready.up(), 1)

                        @block.tensor
                        def _(pe):
                            pe.wait_ge(g_ready.sem, g_ready.at(1))
                            for t in range(TT):
                                nc.tensor.matmul(bank[0][:, t * H:(t + 1) * H], triu, g[:, t * H:(t + 1) * H], start=True, stop=True)
                            for u in range(U):
                                last = nc.tensor.matmul(bank[1 + u // H][:, (u % H) * P:(u % H + 1) * P], wide[:, u, :], triu, start=True, stop=True)
                            last.then_inc(cum.up(), 1)
                            for u in range(U):
                                nc.tensor.matmul(bank[3 + u // H][:, (u % H) * P:(u % H + 1) * P], kT(u), kT(u), start=True, stop=True)
                                nc.tensor.matmul(bank[5 + u // H][:, (u % H) * P:(u % H + 1) * P], kT(u), qT(u), start=True, stop=True)
                            pe.wait_ge(decayed.sem, decayed.at(1))
                            for u in range(U):
                                last = nc.tensor.matmul(bank[(7, 0)[u // H]][:, (u % H) * P:(u % H + 1) * P], step[:, u, :], ident, start=True, stop=True)
                            last.then_inc(products.up(), 1)
                            pe.wait_ge(masked.sem, masked.at(1))
                            for u in range(U):
                                last = nc.tensor.transpose(bank[1 + u // H][:, (u % H) * P:(u % H + 1) * P], invT[:, u, :], ident)
                            last.then_inc(turned0.up(), 1)
                            for n in range(1, LEVELS):
                                pe.wait_ge(level_in.sem, level_in.at(n))
                                for b in range(2):
                                    if n > 1:
                                        pe.wait_ge(inv_ready.sem, inv_ready.at(2 * (n - 2) + b + 1))
                                    for u in range(4 * b, 4 * b + 4):
                                        last = nc.tensor.matmul(bank[1 + b][:, (u % H) * P:(u % H + 1) * P], masks[n % 2][:, u, :], inv[:, u, :],
                                                                start=True, stop=True)
                                    last.then_inc(x_ready.up(), 1)
                                for b in range(2):
                                    pe.wait_ge(x_copied.sem, x_copied.at(2 * (n - 1) + b + 1))
                                    for u in range(4 * b, 4 * b + 4):
                                        cols = slice((u % H) * P, (u % H + 1) * P)
                                        last = nc.tensor.matmul(bank[3 + b][:, cols], step[:, u, :], invT[:, u, :], start=True, stop=True)
                                        if n < LEVELS - 1:
                                            last = nc.tensor.matmul(bank[5 + b][:, cols], invT[:, u, :], step[:, u, :], start=True, stop=True)
                                    last.then_inc(x2_ready.up(), 1)

                with ExitStack() as st_o:
                    ktok = sb(st_o, "ktok", [P, U, P])
                    vtok = sb(st_o, "vtok", [P, U, P])
                    kd = sb(st_o, "kd", [P, H, P])
                    wT = sb(st_o, "wT", [P, H, P])
                    state = sb(st_o, "state", [P, H, P])
                    vnew = sb(st_o, "vnew", [P, U, P])
                    norm_row = sb(st_o, "gdn_norm_row", [P, P])
                    turned, scaled = signal("gdn_kv_turned"), signal("gdn_kv_scaled")
                    u_ready, v0_ready, s_ready, s_copied = signal("gdn_u_ready"), signal("gdn_v0_ready"), signal("gdn_state_ready"), signal("gdn_state_copied")
                    ws_ready, v1_ready, o_ready, squared = (signal(s) for s in ("gdn_ws_ready", "gdn_v1_ready", "heads_out_ready", "heads_squared"))
                    ms_ready, root, row_in, z_ready = signal("mean_square_ready"), signal("root_ready"), signal("gain_row_in"), signal("silu_gate_ready")

                    def unit_cols(b0, u):
                        return bank[b0 + u // H][:, (u % H) * P:(u % H + 1) * P]

                    def half(t, b):
                        return t[:, 4 * b:4 * b + 4, :]

                    def psum3(b):
                        return bank[b][:, :].rearrange("p (u i) -> p u i", u=4)

                    with nc.Block() as block:
                        @block.tensor
                        def _(pe):
                            for u in range(U):
                                nc.tensor.transpose(unit_cols(0, u), kT(u), ident)
                                vT = conv[:, 2 * H + u % H, (u // H) * P:(u // H + 1) * P]
                                last = nc.tensor.transpose(unit_cols(2, u), vT, ident)
                            last.then_inc(turned.up(), 1)
                            pe.wait_ge(scaled.sem, scaled.at(1))
                            for u in range(U):
                                nc.tensor.matmul(unit_cols(4, u), invT[:, u, :], vtok[:, u, :], start=True, stop=True)
                            for h in range(H):
                                last = nc.tensor.matmul(unit_cols(6, h), ktok[:, H + h, :], invT[:, H + h, :], start=True, stop=True)
                            last.then_inc(u_ready.up(), 1)
                            pe.wait_ge(v0_ready.sem, v0_ready.at(1))
                            for h in range(H):
                                last = nc.tensor.matmul(unit_cols(7, h), kd[:, h, :], vnew[:, h, :], start=True, stop=True)
                            last.then_inc(s_ready.up(), 1)
                            for h in range(H):
                                nc.tensor.matmul(unit_cols(0, h), aqk[:, h, :], vnew[:, h, :], start=True, stop=True)
                            pe.wait_ge(s_copied.sem, s_copied.at(1))
                            for h in range(H):
                                last = nc.tensor.matmul(unit_cols(2, h), wT[:, h, :], state[:, h, :], start=True, stop=True)
                            last.then_inc(ws_ready.up(), 1)
                            pe.wait_ge(v1_ready.sem, v1_ready.at(1))
                            for h in range(H):
                                nc.tensor.matmul(unit_cols(1, h), qg[:, h, :], state[:, h, :], start=True, stop=False)
                                last = nc.tensor.matmul(unit_cols(1, h), aqk[:, H + h, :], vnew[:, H + h, :], start=False, stop=True)
                            last.then_inc(o_ready.up(), 1)

                        @block.vector
                        def _(dve):
                            nc.vector.tensor_tensor(qg[:, :, :], qg[:, :, :], conv[:, 0:H, P:2 * P], ALU.mult).then_inc(vector_steps.up(), 1)
                            dve.wait_ge(vector_steps.sem, vector_steps.n)
                            dve.wait_ge(turned.sem, turned.at(1))
                            nc.vector.tensor_tensor(tmp, beta, egc, ALU.mult).then_inc(vector_steps.up(), 1)
                            dve.wait_ge(vector_steps.sem, vector_steps.n)
                            nc.vector.tensor_tensor(kd[:, :, :], psum3(0), kscale[:, 0:H].unsqueeze(2).to_broadcast([P, H, P]), ALU.mult).then_inc(vector_steps.up(), 1)
                            dve.wait_ge(vector_steps.sem, vector_steps.n)
                            for b in range(2):
                                nc.vector.tensor_tensor(half(ktok, b), psum3(b), tmp[:, 4 * b:4 * b + 4].unsqueeze(2).to_broadcast([P, H, P]), ALU.mult).then_inc(vector_steps.up(), 1)
                                dve.wait_ge(vector_steps.sem, vector_steps.n)
                                ins = nc.vector.tensor_tensor(half(vtok, b), psum3(2 + b), beta[:, 4 * b:4 * b + 4].unsqueeze(2).to_broadcast([P, H, P]), ALU.mult)
                            ins.then_inc(scaled.up(), 1)
                            dve.wait_ge(u_ready.sem, u_ready.at(1))
                            nc.vector.tensor_copy(wT[:, :, :], psum3(6)).then_inc(vector_steps.up(), 1)
                            dve.wait_ge(vector_steps.sem, vector_steps.n)
                            nc.vector.tensor_copy(half(vnew, 0), psum3(4)).then_inc(v0_ready.up(), 1)
                            nc.vector.tensor_copy(half(vnew, 1), psum3(5)).then_inc(vector_steps.up(), 1)
                            dve.wait_ge(vector_steps.sem, vector_steps.n)
                            dve.wait_ge(s_ready.sem, s_ready.at(1))
                            nc.vector.tensor_copy(state[:, :, :], psum3(7)).then_inc(s_copied.up(), 1)
                            dve.wait_ge(ws_ready.sem, ws_ready.at(1))
                            nc.vector.tensor_tensor(half(vnew, 1), half(vnew, 1), psum3(2), ALU.subtract).then_inc(v1_ready.up(), 1)
                            dve.wait_ge(z_ready.sem, z_ready.at(1))
                            dve.wait_ge(row_in.sem, row_in.at(16))
                            for t in range(TT):
                                rows = za[:, t, :].rearrange("p (h d) -> p h d", h=H)
                                nc.vector.tensor_tensor(rows, rows, norm_row[:, :].unsqueeze(1).to_broadcast([P, H, P]), ALU.mult)
                            dve.wait_ge(squared.sem, squared.at(1))
                            nc.vector.tensor_scalar(tmp, tmp, 1.0 / P, EPS, ALU.mult, ALU.add).then_inc(ms_ready.up(), 1)
                            dve.wait_ge(root.sem, root.at(1))
                            nc.vector.reciprocal(tmp2, tmp2).then_inc(vector_steps.up(), 1)
                            dve.wait_ge(vector_steps.sem, vector_steps.n)
                            for u in range(U):
                                cols = slice((u % H) * P, (u % H + 1) * P)
                                nc.vector.scalar_tensor_tensor(mixed[:, u // H, cols], unit_cols(0, u), tmp2[:, u:u + 1], za[:, u // H, cols],
                                                               ALU.mult, ALU.mult)

                        @block.scalar
                        def _(act):
                            act.dma_start(norm_row[:, :], A["gdn_out_norm"][0].partition_broadcast(P)).then_inc(row_in.up(16), 16)
                            nc.scalar.activation(za[:, :, :], za[:, :, :], ACT.Silu).then_inc(z_ready.up(), 1)
                            act.wait_ge(o_ready.sem, o_ready.at(1))
                            for u in range(U):
                                ins = nc.scalar.activation(vtok[:, u, :], unit_cols(0, u), ACT.Square, accum_out=tmp[:, u:u + 1])
                            ins.then_inc(squared.up(), 1)
                            act.wait_ge(ms_ready.sem, ms_ready.at(1))
                            nc.scalar.activation(tmp2, tmp, ACT.Sqrt).then_inc(root.up(), 1)

        def routing_stage(layer, st, gate_free, routes):
            gains, slots, row, most = routes
            wr, br = router_w[:, layer], router_b[:, layer]
            g8 = sb(st, "group_logits", [P, TT, 8])
            el = sb(st, "expert_logits", [P, TT, EXPERTS])
            best = sb(st, "best", [P, TT, 2, 8])
            index = sb(st, "index", [P, TT, 2, 8], U32)
            indexf = sb(st, "indexf", [P, TT, 2, 8])
            stat = sb(st, "route_stat", [P, TT, 8])
            gexp = sb(st, "group_exp", [P, TT, GROUPS])
            weight = sb(st, "expert_weight", [P, TT, 2, EXPERTS])
            choice = sb(st, "expert_choice", [P, TT, 3, EXPERTS])
            place = sb(st, "expert_place", [P, TT, EXPERTS])
            rowf = sb(st, "expert_row", [P, TT, 2])
            mostf = sb(st, "expert_most", [P, 1])
            rows = sb(st, "weight_rows", [EXPERTS, T])
            logits, shifted, exped = signal("router_logits"), signal("route_max_ready"), signal("route_exp_ready")
            chosen, ranked = signal("experts_chosen"), signal("tokens_ranked")
            weighed, turned, rows_ready, stored = signal("route_weighed"), signal("route_turned"), signal("gate_rows_ready"), signal("gate_rows_stored")
            with nc.Block() as block:
                @block.scalar
                def _(act):
                    act.wait_ge(shifted.sem, shifted.at(1))
                    for t in range(TT):
                        nc.scalar.activation(gexp[:, t, :], g8[:, t, 0:GROUPS], ACT.Exp, bias=stat[:, t, 0:1], accum_out=stat[:, t, 1:2])
                        ins = nc.scalar.activation(stat[:, t, 3:4], stat[:, t, 2:3], ACT.Exp)
                    ins.then_inc(exped.up(), 1)
                    act.wait_ge(rows_ready.sem, rows_ready.at(1))
                    act.dma_start(gate_rows[layer], rows[:, :]).then_inc(stored.up(16), 16)

                @block.tensor
                def _(pe):
                    pe.wait_ge(router_in.sem, router_in.n)
                    for t in range(TT):
                        acc = bank[0][:, t * (GROUPS + EXPERTS):(t + 1) * (GROUPS + EXPERTS)]
                        nc.tensor.matmul(acc, ones[0:1, :], br, start=True, stop=False)
                        for k in range(KD):
                            last = nc.tensor.matmul(acc, hT[:, k, t * P:(t + 1) * P], wr[:, k, :], start=False, stop=(k == KD - 1))
                    last.then_inc(logits.up(), 1)
                    pe.wait_ge(chosen.sem, chosen.at(1))
                    for t in range(TT):
                        for b in range(t + 1):
                            nc.tensor.matmul(bank[3][:, t * EXPERTS:(t + 1) * EXPERTS], triu if b == t else ones, choice[:, b, 2, :],
                                             start=(b == 0), stop=(b == t))
                    for b in range(TT):
                        last = nc.tensor.matmul(bank[3][:, TT * EXPERTS:(TT + 1) * EXPERTS], ones, choice[:, b, 2, :],
                                                start=(b == 0), stop=(b == TT - 1))
                    last.then_inc(ranked.up(), 1)
                    pe.wait_ge(weighed.sem, weighed.at(1))
                    for t in range(TT):
                        last = nc.tensor.transpose(bank[2][0:EXPERTS, t * P:(t + 1) * P], weight[:, t, 0, :], ident)
                    last.then_inc(turned.up(), 1)

                @block.vector
                def _(dve):
                    def step(ins):
                        ins.then_inc(vector_steps.up(), 1)
                        dve.wait_ge(vector_steps.sem, vector_steps.n)

                    step(nc.vector.memset(g8[:, :, :], NEG))
                    dve.wait_ge(logits.sem, logits.at(1))
                    both = bank[0][:, 0:TT * (GROUPS + EXPERTS)].rearrange("p (t n) -> p t n", t=TT)
                    step(nc.vector.tensor_copy(g8[:, :, 0:GROUPS], both[:, :, 0:GROUPS]))
                    for t in range(TT):
                        ins = nc.vector.max(best[:, t, 0, :], g8[:, t, :])
                    step(ins)
                    for t in range(TT):
                        ins = nc.vector.max_index(index[:, t, 0, :], best[:, t, 0, :], g8[:, t, :])
                    step(ins)
                    step(nc.vector.tensor_copy(indexf[:, :, 0, :], index[:, :, 0, :]))
                    for t in range(TT):
                        ins = nc.vector.tensor_scalar(el[:, t, :], group_of, indexf[:, t, 0, 0:1], NEG, ALU.not_equal, ALU.mult)
                    step(ins)
                    step(nc.vector.tensor_tensor(el[:, :, :], el[:, :, :], both[:, :, GROUPS:], ALU.add))
                    for t in range(TT):
                        ins = nc.vector.max(best[:, t, 1, :], el[:, t, :])
                    step(ins)
                    nc.vector.tensor_scalar(stat[:, :, 0], best[:, :, 0, 0], -1.0, None, ALU.mult)
                    nc.vector.tensor_tensor(stat[:, :, 2], best[:, :, 1, 1], best[:, :, 1, 0], ALU.subtract).then_inc(shifted.up(), 1)
                    for t in range(TT):
                        ins = nc.vector.max_index(index[:, t, 1, :], best[:, t, 1, :], el[:, t, :])
                    step(ins)
                    step(nc.vector.tensor_copy(indexf[:, :, 1, :], index[:, :, 1, :]))
                    for t in range(TT):
                        for n in range(2):
                            ins = nc.vector.tensor_scalar(choice[:, t, n, :], iota, indexf[:, t, 1, n:n + 1], None, ALU.is_equal)
                    ins.then_inc(vector_steps.up(), 1)
                    dve.wait_ge(vector_steps.sem, vector_steps.n)
                    nc.vector.tensor_tensor(choice[:, :, 2, :], choice[:, :, 0, :], choice[:, :, 1, :], ALU.add).then_inc(chosen.up(), 1)
                    dve.wait_ge(ranked.sem, ranked.at(1))
                    dve.wait_ge(chosen.sem, chosen.n)
                    placed = bank[3][:, 0:TT * EXPERTS].rearrange("p (t e) -> p t e", t=TT)
                    nc.vector.memset(slots[:, :, EXPERTS:], 0.0)
                    nc.vector.tensor_tensor(slots[:, :, 0:EXPERTS], placed, choice[:, :, 2, :], ALU.mult)
                    nc.vector.tensor_reduce(mostf[:, :], bank[3][:, TT * EXPERTS:(TT + 1) * EXPERTS], AX.X, ALU.max)
                    nc.vector.scalar_tensor_tensor(place[:, :, :], iota.unsqueeze(1).to_broadcast([P, TT, EXPERTS]), float(CAP), placed,
                                                   ALU.mult, ALU.add).then_inc(vector_steps.up(), 1)
                    dve.wait_ge(vector_steps.sem, vector_steps.n)
                    nc.vector.tensor_copy(most[:, :], mostf[:, :])
                    nc.vector.tensor_tensor(choice[:, :, 0:2, :], choice[:, :, 0:2, :], place[:, :, :].unsqueeze(2).to_broadcast([P, TT, 2, EXPERTS]),
                                            ALU.mult).then_inc(vector_steps.up(), 1)
                    dve.wait_ge(vector_steps.sem, vector_steps.n)
                    nc.vector.tensor_reduce(rowf[:, :, :], choice[:, :, 0:2, :], AX.X, ALU.add).then_inc(vector_steps.up(), 1)
                    dve.wait_ge(vector_steps.sem, vector_steps.n)
                    nc.vector.tensor_scalar(rowf[:, :, :], rowf[:, :, :], -1.0, None, ALU.add).then_inc(vector_steps.up(), 1)
                    dve.wait_ge(vector_steps.sem, vector_steps.n)
                    nc.vector.tensor_copy(row[:, :, :], rowf[:, :, :]).then_inc(vector_steps.up(), 1)
                    dve.wait_ge(vector_steps.sem, vector_steps.n)
                    dve.wait_ge(exped.sem, exped.at(1))
                    step(nc.vector.scalar_tensor_tensor(stat[:, :, 4], stat[:, :, 3], 1.0, stat[:, :, 1], ALU.add, ALU.mult))
                    step(nc.vector.reciprocal(stat[:, :, 5], stat[:, :, 4]))
                    step(nc.vector.tensor_tensor(stat[:, :, 6], stat[:, :, 5], stat[:, :, 3], ALU.mult))
                    for t in range(TT):
                        for n in range(2):
                            ins = nc.vector.tensor_scalar(weight[:, t, n, :], iota, indexf[:, t, 1, n:n + 1], stat[:, t, 5 + n:6 + n],
                                                          ALU.is_equal, ALU.mult)
                    step(ins)
                    nc.vector.tensor_tensor(weight[:, :, 0, :], weight[:, :, 0, :], weight[:, :, 1, :], ALU.add).then_inc(weighed.up(), 1)
                    nc.vector.tensor_copy(gains[:, :, :], stat[:, :, 5:7]).then_inc(vector_steps.up(), 1)
                    dve.wait_ge(vector_steps.sem, vector_steps.n)
                    dve.wait_ge(turned.sem, turned.at(1))
                    nc.vector.memset(stat[:, :, 7], 0.0).then_inc(gate_free.up(), 1)
                    nc.vector.memset(best[:, 0, 0, 0:1], 0.0).then_inc(gate_free.up(), 1)
                    nc.vector.tensor_copy(rows[:, :], bank[2][0:EXPERTS, 0:T]).then_inc(rows_ready.up(), 1)

                @block.gpsimd
                def _(pool):
                    pool.wait_ge(stored.sem, stored.at(16))

        def experts_stage(layer, gates, xn, gain, shift, following):
            c0 = first[f"experts{layer}"]
            PAIRS = EXPERTS // 2

            def layer_signal(name):
                return signal(f"{name}{layer}")

            with ExitStack() as st:
                gains = sb(st, "route_gains", [P, TT, 2])
                slots = sb(st, "route_slots", [P, TT, EXPERTS + 2])
                row = sb(st, "route_rows", [P, TT, 2], I32)
                most = sb(st, "route_most", [P, 1], I32)
                hid_free = layer_signal("hidden_free")
                with ExitStack() as st_r:
                    routing_stage(layer, st_r, hid_free, (gains, slots, row, most))
                hid_ready, y_done = layer_signal("hidden_ready"), layer_signal("expert_out_ready")
                gate_b = sb(st, "gate_b", [P, 2, T])
                act_h = sb(st, "silu_h", [P, 2, T])
                gated = sb(st, "gated_h", [P, 2, T])
                hid = sb(st, "hidden", [P, FT, T])
                zero = sb(st, "zero", [P, 512])
                gate_in = [layer_signal(f"gate{q}_in_") for q in range(2)]
                silu_done, gated_done = layer_signal("silu_done"), layer_signal("gated_done")
                zeroed, summed, sum_steps = layer_signal("zero_ready"), layer_signal("experts_summed"), layer_signal("sum_steps")
                y = [[bank[4 + 2 * t + half] for half in range(2)] for t in range(TT)]
                member = sb(st, "member", [P, 2, TT, CAP])
                own_rows = sb(st, "own_rows", [P, 512])
                own = sb(st, "own_tokens", [P, 2, KD // 2, 2, CAP])
                own_silu = sb(st, "own_silu", [P, 2, FE // 2])
                own_hid = sb(st, "own_hidden", [P, FE // 2])
                own_hidT = sb(st, "own_hiddenT", [P, 2, FT // 2, 2, CAP])
                own_y = sb(st, "own_out", [P, 2, 512])
                taken = sb(st, "taken_rows", [P, TT, 2, D])
                member_ready, sorted_out, rows_copied = layer_signal("member_ready"), layer_signal("tokens_sorted"), layer_signal("own_rows_copied")
                rows_turned, own_scaled, own_ready = layer_signal("own_rows_turned"), layer_signal("own_tokens_scaled"), layer_signal("own_tokens_ready")
                own_silu_done, own_hid_done = layer_signal("own_silu_done"), layer_signal("own_hidden_done")
                hid_turned, hidT_ready = layer_signal("own_hidden_turned"), layer_signal("own_hiddenT_ready")
                y_copied, merge_steps = layer_signal("own_out_copied"), layer_signal("merge_steps")
                taken_in = [layer_signal(f"rows{t}_taken_") for t in range(TT)]
                y_stored = [layer_signal(f"own_out{q}_stored_") for q in range(2)]

                frees_from = [(hid_ready, lambda e: hid_ready.start + FT * (e + 1)), (hid_ready, lambda e: hid_ready.start + FT * (e + 1)),
                              (y_done, lambda e: y_done.start + e + 1)]
                base = {j: landed_at[c0 + j] for j in range(RING)}
                for j in range(3 * EXPERTS):
                    s, n = frees_from[j % 3]
                    freed[c0 + j] = (s.sem, n(j // 3))
                with nc.Block() as block:
                    @block.sync
                    def _(sp):
                        fill_ring(sp, c0 - 1)
                        with sp.Fori(0, PAIRS - 1) as i:
                            for j in range(RING):
                                q, part = j // 3, j % 3
                                e = 2 * i + q
                                s, n = frees_from[part]
                                sp.wait_ge(s.sem, n(e))
                                name = ("exp_w1", "exp_w3", "exp_w2")[part]
                                src = A[name][layer].rearrange("e r n -> (e r) n")
                                nrow = A[name].shape[2]
                                src = src[bass.ds((e + 2) * nrow, nrow), :].rearrange("(k p) n -> p k n", p=P)
                                sp.dma_start(slot(c0 + j), src).then_inc(landed[(c0 + j) % RING].sem, 16)
                        for j in range(RING):
                            landed[(c0 + j) % RING].n += 16 * (PAIRS - 1)
                        issued[0] = c0 + 3 * EXPERTS
                        if following:
                            fill_ring(sp, following[5])
                        else:
                            fill_ring(sp, c0 + 3 * EXPERTS - 1 - RING)

                    @block.gpsimd
                    def _(pool):
                        fullest = pool.value_load(most[0:1, 0:1], min_val=0, max_val=T)
                        with pool.If(fullest > CAP):
                            for q in range(2):
                                pool.dma_start(gate_b[:, q, :], gate_rows[layer, q].partition_broadcast(P)).then_inc(gate_in[q].up(16), 16)
                            flat_rows = gate_rows[layer].rearrange("e t -> (e t)")
                            with pool.Fori(0, PAIRS - 1) as i:
                                for q in range(2):
                                    e = 2 * i + q
                                    pool.wait_ge(hid_free.sem, hid_free.start + 2 + FT * (e + 1))
                                    pool.dma_start(gate_b[:, q, :], flat_rows[bass.ds((e + 2) * T, T)].partition_broadcast(P))\
                                        .then_inc(gate_in[q].sem, 16)
                        with pool.Else():
                            for q in range(2):
                                pool.wait_ge(y_stored[q].sem, 2 * 16 * PAIRS)
                            for t in range(TT):
                                for n in range(2):
                                    pool.indirect_dma_start(taken[:, t, n, :], None, expert_out[layer],
                                                            bass.IndirectOffsetOnAxis(ap=row[:, t, n:n + 1], axis=0)).then_inc(taken_in[t].sem, 16)

                    @block.tensor
                    def _(pe):
                        fullest = pe.value_load(most[0:1, 0:1], min_val=0, max_val=T)
                        with pe.If(fullest > CAP):
                            pe.wait_ge(zeroed.sem, 1)
                            for t in range(TT):
                                for half in range(2):
                                    nc.tensor.matmul(y[t][half][:, :], zero[:, 0:P], zero[:, :], start=True, stop=False)
                            with pe.Fori(0, PAIRS) as i:
                                for q in range(2):
                                    e = 2 * i + q
                                    w1, w3, w2 = (slot(c0 + 3 * q + part) for part in range(3))
                                    for part in range(2):
                                        pe.wait_ge(landed[(c0 + 3 * q + part) % RING].sem, base[3 * q + part] + 16 * i)
                                    for f in range(FT):
                                        pe.wait_ge(hid_free.sem, hid_free.start + FT * e + f + 1)
                                        for w, b in ((w1, f % 2), (w3, 2 + f % 2)):
                                            for k in range(KD):
                                                last = nc.tensor.matmul(bank[b][:, 0:T], w[:, k, f * P:(f + 1) * P], hT[:, k, :],
                                                                        start=(k == 0), stop=(k == KD - 1))
                                        last.then_inc(hid_ready.sem, 1)
                                    pe.wait_ge(landed[(c0 + 3 * q + 2) % RING].sem, base[3 * q + 2] + 16 * i)
                                    for f in range(FT):
                                        pe.wait_ge(hid_free.sem, hid_free.start + 2 + FT * e + f + 1)
                                        for t in range(TT):
                                            for half in range(2):
                                                last = nc.tensor.matmul(y[t][half][:, :], hid[:, f, t * P:(t + 1) * P],
                                                                        w2[:, f, half * 512:(half + 1) * 512], start=False, stop=False,
                                                                        skip_group_check=True)
                                    last.then_inc(y_done.sem, 1)
                            for t in range(TT):
                                for half in range(2):
                                    last = nc.tensor.matmul(y[t][half][:, :], zero[:, 0:P], zero[:, :], start=False, stop=True)
                            last.then_inc(summed.sem, 1)
                            pe.wait_ge(sum_steps.sem, 2 * TT)
                        with pe.Else():
                            halves = [slice(0, CAP), slice(CAP, 2 * CAP)]

                            def sort_tokens(e, q):
                                pe.wait_ge(member_ready.sem, e + 1)
                                for t in range(TT):
                                    for half in range(2):
                                        last = nc.tensor.matmul(bank[0][halves[half], :], member[:, q, t, :],
                                                                xn[:, t, half * 512:(half + 1) * 512], start=(t == 0), stop=(t == TT - 1))
                                last.then_inc(sorted_out.sem, 1)

                            def turn_tokens(e):
                                pe.wait_ge(rows_copied.sem, e + 1)
                                for c in range(KD // 2):
                                    last = nc.tensor.transpose(bank[1][:, c * P:(c + 1) * P], own_rows[:, c * P:(c + 1) * P], ident)
                                last.then_inc(rows_turned.sem, 1)

                            def two_experts(i, peeled):
                                for q in range(2):
                                    e = 2 * i + q
                                    w1, w3, w2 = (slot(c0 + 3 * q + part) for part in range(3))
                                    pe.wait_ge(own_ready.sem, e + 1)
                                    for part, w in enumerate((w1, w3)):
                                        pe.wait_ge(landed[(c0 + 3 * q + part) % RING].sem, base[3 * q + part] + 16 * i)
                                        for k in range(KD):
                                            for half in range(2):
                                                cols = slice(half * FE // 2, (half + 1) * FE // 2)
                                                last = nc.tensor.matmul(bank[2 + q][halves[half], part * FE // 2:(part + 1) * FE // 2],
                                                                        own[:, q, k % 4, k // 4, :], w[:, k, cols],
                                                                        start=(k == 0), stop=(k == KD - 1))
                                    last.then_inc(hid_ready.sem, FT)
                                    sort_tokens(e + 1, 1 - q)
                                    pe.wait_ge(own_hid_done.sem, e + 1)
                                    for c in range(FT // 2):
                                        last = nc.tensor.transpose(bank[4][:, c * P:(c + 1) * P], own_hid[:, c * P:(c + 1) * P], ident)
                                    last.then_inc(hid_turned.sem, 1)
                                    turn_tokens(e + 1)
                                    pe.wait_ge(landed[(c0 + 3 * q + 2) % RING].sem, base[3 * q + 2] + 16 * i)
                                    pe.wait_ge(hidT_ready.sem, e + 1)
                                    if not peeled:
                                        pe.wait_ge(y_copied.sem, e - 1)
                                    for f in range(FT):
                                        for half in range(2):
                                            last = nc.tensor.matmul(bank[5 + q][halves[half], :], own_hidT[:, q, f % 2, f // 2, :],
                                                                    w2[:, f, half * 512:(half + 1) * 512], start=(f == 0), stop=(f == FT - 1))
                                    last.then_inc(y_done.sem, 1)

                            sort_tokens(0, 0)
                            turn_tokens(0)
                            two_experts(0, True)
                            with pe.Fori(1, PAIRS) as i:
                                two_experts(i, False)
                            pe.wait_ge(y_copied.sem, EXPERTS)
                        hid_ready.n += FT * EXPERTS
                        y_done.n += EXPERTS
                        if following:
                            following[2](pe)

                    @block.scalar
                    def _(act):
                        if following:
                            following[0](act)
                        fullest = act.value_load(most[0:1, 0:1], min_val=0, max_val=T)
                        with act.If(fullest > CAP):
                            with act.Fori(0, PAIRS) as i:
                                for q in range(2):
                                    for f in range(FT):
                                        u = FT * (2 * i + q) + f
                                        act.wait_ge(hid_ready.sem, hid_ready.start + u + 1)
                                        act.wait_ge(hid_free.sem, hid_free.start + u + 1)
                                        nc.scalar.activation(act_h[:, f % 2, :], bank[f % 2][:, 0:T], ACT.Silu).then_inc(silu_done.sem, 1)
                        with act.Else():
                            def copy_rows(e):
                                act.wait_ge(sorted_out.sem, e + 1)
                                nc.scalar.copy(own_rows[:, :], bank[0][:, :]).then_inc(rows_copied.sem, 1)

                            copy_rows(0)
                            with act.Fori(0, PAIRS) as i:
                                for q in range(2):
                                    e = 2 * i + q
                                    act.wait_ge(hid_ready.sem, FT * (e + 1))
                                    nc.scalar.activation(own_silu[:, q, :], bank[2 + q][:, 0:FE // 2], ACT.Silu).then_inc(own_silu_done.sem, 1)
                                    copy_rows(e + 1)
                                    act.wait_ge(y_copied.sem, e + 1)
                                    for half in range(2):
                                        act.dma_start(expert_out[layer][bass.ds(e * CAP, CAP), half * 512:(half + 1) * 512],
                                                      own_y[half * CAP:(half + 1) * CAP, q, :]).then_inc(y_stored[q].sem, 16)
                        if following:
                            following[3](act)

                    @block.vector
                    def _(dve):
                        if following:
                            following[1](dve)
                        fullest = dve.value_load(most[0:1, 0:1], min_val=0, max_val=T)
                        with dve.If(fullest > CAP):
                            nc.vector.memset(zero[:, :], 0.0).then_inc(zeroed.sem, 1)
                            with dve.Fori(0, PAIRS) as i:
                                for q in range(2):
                                    dve.wait_ge(gate_in[q].sem, 16 * (i + 1))
                                    for f in range(FT):
                                        u = FT * (2 * i + q) + f
                                        dve.wait_ge(hid_ready.sem, hid_ready.start + u + 1)
                                        nc.vector.tensor_tensor(gated[:, f % 2, :], bank[2 + f % 2][:, 0:T], gate_b[:, q, :], ALU.mult)\
                                            .then_inc(gated_done.sem, 1)
                                        dve.wait_ge(gated_done.sem, u + 1)
                                        dve.wait_ge(silu_done.sem, u + 1)
                                        nc.vector.tensor_tensor(hid[:, f, :], gated[:, f % 2, :], act_h[:, f % 2, :], ALU.mult).then_inc(hid_free.sem, 1)
                            dve.wait_ge(summed.sem, 1)
                            for t in range(TT):
                                for half in range(2):
                                    cols = slice(half * 512, (half + 1) * 512)
                                    nc.vector.tensor_tensor(taken[:, t, 0, cols], y[t][half][:, :], gates[:, 1, cols], ALU.mult).then_inc(sum_steps.up(), 1)
                            dve.wait_ge(sum_steps.sem, sum_steps.n)
                        with dve.Else():
                            def find_members(e, q):
                                shape = [P, TT, CAP]
                                nc.vector.tensor_tensor(member[:, q], slots[:, :, bass.ds(e, 1)].to_broadcast(shape),
                                                        slot_number.unsqueeze(1).to_broadcast(shape), ALU.is_equal).then_inc(member_ready.sem, 1)

                            def own_tokens(e, q):
                                tiles = [P, KD // 2, 2, CAP]

                                def tile_columns(a):
                                    return a.rearrange("p (h c) -> p c h", h=2).unsqueeze(3).to_broadcast(tiles)
                                dve.wait_ge(rows_turned.sem, e + 1)
                                nc.vector.tensor_tensor(own[:, q], bank[1][:, :].rearrange("p (c h s) -> p c h s", c=KD // 2, h=2),
                                                        tile_columns(gain), ALU.mult).then_inc(own_scaled.sem, 1)
                                dve.wait_ge(own_scaled.sem, e + 1)
                                nc.vector.tensor_tensor(own[:, q], own[:, q], tile_columns(shift), ALU.add).then_inc(own_ready.sem, 1)

                            def two_experts(i, peeled):
                                for q in range(2):
                                    e = 2 * i + q
                                    dve.wait_ge(own_silu_done.sem, e + 1)
                                    nc.vector.tensor_tensor(own_hid[:, :], bank[2 + q][:, FE // 2:], own_silu[:, q, :],
                                                            ALU.mult).then_inc(own_hid_done.sem, 1)
                                    dve.wait_ge(hid_turned.sem, e + 1)
                                    nc.vector.tensor_copy(own_hidT[:, q].rearrange("p c h s -> p (c h s)"),
                                                          bank[4][:, 0:FE // 2]).then_inc(hidT_ready.sem, 1)
                                    own_tokens(e + 1, 1 - q)
                                    dve.wait_ge(y_done.sem, e + 1)
                                    if not peeled:
                                        dve.wait_ge(y_stored[q].sem, 2 * 16 * i)
                                    nc.vector.tensor_copy(own_y[:, q, :], bank[5 + q][:, :]).then_inc(y_copied.sem, 1)
                                    find_members(e + 2, q)

                            find_members(0, 0)
                            find_members(1, 1)
                            own_tokens(0, 0)
                            two_experts(0, True)
                            with dve.Fori(1, PAIRS) as i:
                                two_experts(i, False)
                            for t in range(TT):
                                dve.wait_ge(taken_in[t].sem, 16 * 2)
                                nc.vector.tensor_scalar(taken[:, t, 0, :], taken[:, t, 0, :], gains[:, t, 0:1], None, ALU.mult).then_inc(merge_steps.up(), 1)
                                dve.wait_ge(merge_steps.sem, merge_steps.n)
                                nc.vector.scalar_tensor_tensor(taken[:, t, 0, :], taken[:, t, 1, :], gains[:, t, 1:2], taken[:, t, 0, :],
                                                               ALU.mult, ALU.add).then_inc(merge_steps.up(), 1)
                                dve.wait_ge(merge_steps.sem, merge_steps.n)
                                nc.vector.tensor_tensor(taken[:, t, 0, :], taken[:, t, 0, :], gates[:, 1, :], ALU.mult).then_inc(merge_steps.up(), 1)
                                dve.wait_ge(merge_steps.sem, merge_steps.n)
                        nc.vector.tensor_tensor(x[:, :, :], x[:, :, :], taken[:, :, 0, :], ALU.add)
                        if following:
                            following[4](dve)


        def gla_mixer(mixed):
            DV = D // H
            with ExitStack() as st:
                qT = sb(st, "gla_qT", [P, H, T])
                kT = sb(st, "gla_kT", [P, H, T])
                v = sb(st, "gla_v", [P, TT, D])
                r = sb(st, "gla_r", [P, TT, D])
                lowT = sb(st, "gla_lowT", [16, T])
                project_stage(first["gla_in"], [("channel", to_channels(qT, 0, float(P) ** -0.5)), ("channel", to_channels(kT, 0)),
                                                ("token", to_tokens(v, 0)), ("token", to_tokens(v, 512)),
                                                ("token", to_tokens(r, 0)), ("token", to_tokens(r, 512)),
                                                ("channel", lambda pair: [(lowT[:, :], pair[0][0:16, 0:T], 1.0)])], hT)
                wg = sb(st, "gla_wg", [16, H * P])
                z = sb(st, "gla_z", [P, H, T])
                cum = sb(st, "gla_cum", [P, H, T])
                e = sb(st, "gla_decay", [P, H, T])
                qs = sb(st, "gla_qs", [P, H, T])
                ks = sb(st, "gla_ks", [P, H, T])
                part = gates[0][:, 0, :].rearrange("p (u i) -> p u i", i=P)
                attT = sb(st, "gla_attT", [P, 3 * H, P])
                norm_row = sb(st, "gla_norm_row", [P, DV])
                stat = sb(st, "gla_stat", [P, 2, 2 * H])
                wg_in, low_ready, az_ready, ln_ready = signal("operands_in"), signal("gla_z_ready"), signal("gla_abs_ready"), signal("gla_ln_ready")
                dist, decayed, scaled, scored = signal("gla_dist_ready"), signal("gla_decay_ready"), signal("gla_scaled"), signal("gla_scored")
                att_ready, o_ready, ms_ready, root = signal("gla_att_ready"), signal("heads_out_ready"), signal("mean_square_ready"), signal("root_ready")
                gate_ready, row_in, squared = signal("silu_gate_ready"), signal("gain_row_in"), signal("heads_squared")
                LAST = LEVELS
                with nc.Block() as block:
                    @block.scalar
                    def _(act):
                        act.dma_start(wg[:, :], A["gla_w_gate2"][0]).then_inc(wg_in.up(16), 16)
                        act.dma_start(norm_row[:, :], A["gla_out_norm"][0].partition_broadcast(P)).then_inc(row_in.up(16), 16)
                        act.wait_ge(az_ready.sem, az_ready.at(1))
                        nc.scalar.activation(e[:, :, :], e[:, :, :], ACT.Exp, scale=-1.0).then_inc(scalar_steps.up(), 1)
                        act.wait_ge(scalar_steps.sem, scalar_steps.n)
                        nc.scalar.activation(e[:, :, :], e[:, :, :], ACT.Ln, bias=1.0).then_inc(ln_ready.up(), 1)
                        for n in range(LEVELS + 1):
                            act.wait_ge(dist.sem, dist.at(n + 1))
                            nc.scalar.activation(e[:, :, :], e[:, :, :], ACT.Exp).then_inc(decayed.up(), 1)
                        nc.scalar.activation(r[:, :, :], r[:, :, :], ACT.Silu).then_inc(gate_ready.up(), 1)
                        act.wait_ge(o_ready.sem, o_ready.at(1))
                        for u in range(2 * H):
                            ins = nc.scalar.activation((qs, ks)[u // H][:, u % H, :], bank[u // 2][:, (u % 2) * DV:(u % 2 + 1) * DV], ACT.Square,
                                                       accum_out=stat[:, 0, u:u + 1])
                        ins.then_inc(squared.up(), 1)
                        act.wait_ge(ms_ready.sem, ms_ready.at(1))
                        nc.scalar.activation(stat[:, 1, :], stat[:, 0, :], ACT.Sqrt).then_inc(root.up(), 1)

                    @block.tensor
                    def _(pe):
                        pe.wait_ge(wg_in.sem, wg_in.at(16))
                        for h in range(H):
                            last = nc.tensor.matmul(bank[h // 2][:, (h % 2) * T:(h % 2 + 1) * T], wg[:, h * P:(h + 1) * P], lowT[:, :],
                                                    start=True, stop=True)
                        last.then_inc(low_ready.up(), 1)
                        for u in range(2 * H):
                            cols = slice((u // H) * P, (u // H + 1) * P)
                            last = nc.tensor.matmul(bank[4 + u // H][:, (u % H) * P:(u % H + 1) * P], kT[:, u % H, cols], qT[:, u % H, cols],
                                                    start=True, stop=True)
                        last.then_inc(scored.up(), 1)
                        for n in range(LEVELS):
                            b0 = (6, 4)[n % 2]
                            pe.wait_ge(scaled.sem, scaled.at(n + 1))
                            for u in range(2 * H):
                                cols = slice((u // H) * P, (u // H + 1) * P)
                                last = nc.tensor.matmul(bank[b0 + u // H][:, (u % H) * P:(u % H + 1) * P], ks[:, u % H, cols], qs[:, u % H, cols],
                                                        start=True, stop=True)
                            last.then_inc(scored.up(), 1)
                        pe.wait_ge(scaled.sem, scaled.at(LAST + 1))
                        for h in range(H):
                            last = nc.tensor.matmul(bank[4][:, h * P:(h + 1) * P], ks[:, h, 0:P], qs[:, h, P:2 * P], start=True, stop=True)
                        last.then_inc(scored.up(), 1)
                        pe.wait_ge(att_ready.sem, att_ready.at(1))
                        for t in range(TT):
                            for h in range(H):
                                acc = bank[2 * t + h // 2][:, (h % 2) * DV:(h % 2 + 1) * DV]
                                if t:
                                    nc.tensor.matmul(acc, attT[:, 2 * H + h, :], v[:, 0, h * DV:(h + 1) * DV], start=True, stop=False)
                                last = nc.tensor.matmul(acc, attT[:, t * H + h, :], v[:, t, h * DV:(h + 1) * DV], start=(t == 0), stop=True)
                        last.then_inc(o_ready.up(), 1)

                    @block.vector
                    def _(dve):
                        dve.wait_ge(low_ready.sem, low_ready.at(1))
                        for h in range(H):
                            ins = nc.vector.tensor_scalar(z[:, h, :], bank[h // 2][:, (h % 2) * T:(h % 2 + 1) * T], col("gla_b_gate2", h, 1), None, ALU.add)
                        ins.then_inc(vector_steps.up(), 1)
                        dve.wait_ge(vector_steps.sem, vector_steps.n)
                        nc.vector.scalar_tensor_tensor(e[:, :, :], z[:, :, :], -1.0, z[:, :, :], ALU.mult, ALU.max).then_inc(az_ready.up(), 1)
                        nc.vector.tensor_scalar(z[:, :, :], z[:, :, :], -1.0, 0.0, ALU.mult, ALU.max).then_inc(vector_steps.up(), 1)
                        dve.wait_ge(vector_steps.sem, vector_steps.n)
                        dve.wait_ge(ln_ready.sem, ln_ready.at(1))
                        nc.vector.tensor_tensor(z[:, :, :], z[:, :, :], e[:, :, :], ALU.add).then_inc(vector_steps.up(), 1)
                        dve.wait_ge(vector_steps.sem, vector_steps.n)
                        nc.vector.tensor_scalar(z[:, :, :], z[:, :, :], -1.0 / GLA_TAU, None, ALU.mult).then_inc(vector_steps.up(), 1)
                        dve.wait_ge(vector_steps.sem, vector_steps.n)
                        for h in range(H):
                            ins = nc.vector.tensor_tensor_scan(cum[:, h, :], ones[:, 0:1].to_broadcast([P, T]), z[:, h, :], 0.0, ALU.mult, ALU.add)
                        ins.then_inc(vector_steps.up(), 1)
                        dve.wait_ge(vector_steps.sem, vector_steps.n)
                        units = [slice(0, H), slice(H, 2 * H)]

                        def psum3(b):
                            return bank[b][:, :].rearrange("p (u i) -> p u i", u=H)

                        def distance(n):
                            s = 1 << n
                            m = H * T // (2 * s)
                            sums = cum[:, :, :].rearrange("p h (m s) -> p (h m) s", s=2 * s)
                            eb = e[:, :, :].rearrange("p h (m s) -> p (h m) s", s=2 * s)
                            edge = sums[:, :, s - 1:s].to_broadcast([P, m, s])
                            nc.vector.tensor_tensor(eb[:, :, 0:s], edge, sums[:, :, 0:s], ALU.subtract)
                            nc.vector.tensor_tensor(eb[:, :, s:2 * s], sums[:, :, s:2 * s], edge, ALU.subtract).then_inc(dist.up(), 1)

                        distance(0)
                        dve.wait_ge(scored.sem, scored.at(1))
                        for t in range(TT):
                            nc.vector.tensor_tensor(attT[:, units[t], :], psum3(4 + t), ident.unsqueeze(1).to_broadcast([P, H, P]), ALU.mult).then_inc(vector_steps.up(), 1)
                            dve.wait_ge(vector_steps.sem, vector_steps.n)
                        for n in range(LEVELS + 1):
                            dve.wait_ge(decayed.sem, decayed.at(n + 1))
                            if n:
                                dve.wait_ge(scored.sem, scored.at(n + 1))
                            nc.vector.tensor_tensor(qs[:, :, :], qT[:, :, :], e[:, :, :], ALU.mult).then_inc(vector_steps.up(), 1)
                            dve.wait_ge(vector_steps.sem, vector_steps.n)
                            nc.vector.tensor_tensor(ks[:, :, :], kT[:, :, :], e[:, :, :], ALU.mult).then_inc(scaled.up(), 1)
                            dve.wait_ge(scaled.sem, scaled.n)
                            if n < LEVELS:
                                distance(n + 1)
                            if n:
                                b0 = (6, 4)[(n - 1) % 2]
                                for t in range(TT):
                                    nc.vector.tensor_tensor(part[:, units[t], :], psum3(b0 + t), level(n - 1).unsqueeze(1).to_broadcast([P, H, P]),
                                                                     ALU.mult).then_inc(vector_steps.up(), 1)
                                    dve.wait_ge(vector_steps.sem, vector_steps.n)
                                nc.vector.tensor_tensor(attT[:, 0:2 * H, :], attT[:, 0:2 * H, :], part, ALU.add).then_inc(vector_steps.up(), 1)
                                dve.wait_ge(vector_steps.sem, vector_steps.n)
                        dve.wait_ge(scored.sem, scored.at(LAST + 2))
                        nc.vector.tensor_copy(attT[:, 2 * H:3 * H, :], psum3(4)).then_inc(att_ready.up(), 1)
                        dve.wait_ge(gate_ready.sem, gate_ready.at(1))
                        dve.wait_ge(row_in.sem, row_in.at(16))
                        for t in range(TT):
                            rows = r[:, t, :].rearrange("p (h d) -> p h d", h=H)
                            nc.vector.tensor_tensor(rows, rows, norm_row[:, :].unsqueeze(1).to_broadcast([P, H, DV]), ALU.mult)
                        dve.wait_ge(squared.sem, squared.at(1))
                        nc.vector.tensor_scalar(stat[:, 0, :], stat[:, 0, :], 1.0 / DV, EPS, ALU.mult, ALU.add).then_inc(ms_ready.up(), 1)
                        dve.wait_ge(root.sem, root.at(1))
                        nc.vector.reciprocal(stat[:, 1, :], stat[:, 1, :]).then_inc(vector_steps.up(), 1)
                        dve.wait_ge(vector_steps.sem, vector_steps.n)
                        for u in range(2 * H):
                            cols = slice((u % H) * DV, (u % H + 1) * DV)
                            nc.vector.scalar_tensor_tensor(mixed[:, u // H, cols], bank[u // 2][:, (u % 2) * DV:(u % 2 + 1) * DV], stat[:, 1, u:u + 1],
                                                           r[:, u // H, cols], ALU.mult, ALU.mult)

        def final_norm_stage(name, dst, mem=None):
            with ExitStack() as st:
                row = sb(st, "final_row", [P, D])
                sq = sb(st, "final_sq", [P, D])
                stat = sb(st, "final_stat", [P, 2, TT])
                row_in, ms_ready, root, mem_in = (signal(s) for s in ("gain_row_in", "mean_square_ready", "root_ready", "operands_in"))
                with nc.Block() as block:
                    @block.sync
                    def _(sp):
                        if mem is not None:
                            sp.dma_start(mem[:, :, :], A["mem_2"][0].rearrange("(t p) d -> p t d", p=P)).then_inc(mem_in.up(16), 16)
                            sp.wait_ge(row_in.sem, row_in.start + 16)
                            sp.wait_ge(mem_in.sem, mem_in.n)
                            fill_ring(sp, first["hawk_mem"] - 1)

                    @block.scalar
                    def _(act):
                        act.dma_start(row[:, :], A[name].partition_broadcast(P)).then_inc(row_in.up(16), 16)
                        act.wait_ge(ms_ready.sem, ms_ready.at(1))
                        nc.scalar.activation(stat[:, 1, :], stat[:, 0, :], ACT.Sqrt).then_inc(root.up(), 1)

                    @block.vector
                    def _(dve):
                        for t in range(TT):
                            nc.vector.tensor_tensor_reduce(sq[:, :], x[:, t, :], x[:, t, :], 1.0, 0.0, ALU.mult, ALU.add, stat[:, 0, t:t + 1]).then_inc(vector_steps.up(), 1)
                            dve.wait_ge(vector_steps.sem, vector_steps.n)
                        nc.vector.tensor_scalar(stat[:, 0, :], stat[:, 0, :], 1.0 / D, EPS, ALU.mult, ALU.add).then_inc(ms_ready.up(), 1)
                        dve.wait_ge(root.sem, root.at(1))
                        dve.wait_ge(row_in.sem, row_in.at(16))
                        nc.vector.reciprocal(stat[:, 1, :], stat[:, 1, :]).then_inc(vector_steps.up(), 1)
                        dve.wait_ge(vector_steps.sem, vector_steps.n)
                        for t in range(TT):
                            nc.vector.scalar_tensor_tensor(dst[:, t, :], x[:, t, :], stat[:, 1, t:t + 1], row[:, :], ALU.mult, ALU.mult).then_inc(vector_steps.up(), 1)
                            dve.wait_ge(vector_steps.sem, vector_steps.n)

        def attention_stage(units, depth=2):
            n = len(units)
            with ExitStack() as st:
                probs = sb(st, "seg_probs", [P, 3, 3, T])
                probsT = sb(st, "seg_probsT", [P, depth, 6, P])
                stat = sb(st, "seg_stat", [P, 3, 3, 4])
                scored, shifted, exped, normal = signal("att_logits_ready"), signal("att_max_ready"), signal("att_exp_ready"), signal("att_probs_ready")
                turned, turned_in, summed, done = signal("att_probs_turned"), signal("att_probsT_ready"), signal("att_out_ready"), signal("att_tile_done")

                def score_bank(u, s):
                    return bank[2 * (u % 2) + s // 2][:, (s % 2) * T:(s % 2 + 1) * T]

                def groups(unit):
                    segs = unit["segs"]
                    return [(0, len(segs))] if unit["joint"] else [(s, s + 1) for s in range(len(segs))]

                def blocks(unit):
                    out = []
                    for s, (_, _, _, _, values) in enumerate(unit["segs"]):
                        k0 = 0
                        for v, keys in values:
                            out.append((s, k0, keys, v))
                            k0 += keys
                    return out

                with nc.Block() as block:
                    @block.tensor
                    def _(pe):
                        for u in range(n + 3):
                            if u < n:
                                if u >= 2:
                                    pe.wait_ge(shifted.sem, shifted.at(u - 1))
                                for s, (q, k, nk, _, _) in enumerate(units[u]["segs"]):
                                    last = nc.tensor.matmul(score_bank(u, s)[:, 0:nk], q, k, start=True, stop=True)
                                last.then_inc(scored.up(), 1)
                            if u >= 3:
                                w = u - 3
                                pe.wait_ge(turned_in.sem, turned_in.at(w + 1))
                                if w >= 2:
                                    pe.wait_ge(done.sem, done.at(w - 1))
                                lo, rows = units[w]["rows"]
                                bl = blocks(units[w])
                                for i, (s, k0, keys, v) in enumerate(bl):
                                    last = nc.tensor.matmul(bank[6 + w % 2][lo:lo + rows, 0:P], v, probsT[0:keys, w % depth, i, :],
                                                            start=(i == 0), stop=(i == len(bl) - 1))
                                last.then_inc(summed.up(), 1)
                            if 2 <= u < n + 2:
                                w = u - 2
                                pe.wait_ge(normal.sem, normal.at(w + 1))
                                for i, (s, k0, keys, _) in enumerate(blocks(units[w])):
                                    last = nc.tensor.transpose(bank[4 + i // 4][0:keys, (i % 4) * P:(i % 4 + 1) * P],
                                                               probs[:, w % 3, s, k0:k0 + keys], ident)
                                last.then_inc(turned.up(), 1)

                    @block.vector
                    def _(dve):
                        for u in range(n + 4):
                            if u < n:
                                dve.wait_ge(scored.sem, scored.at(u + 1))
                                for s, (_, _, nk, bias, _) in enumerate(units[u]["segs"]):
                                    d = probs[:, u % 3, s, 0:nk]
                                    if bias is None:
                                        ins = nc.vector.tensor_copy(d, score_bank(u, s)[:, 0:nk])
                                    else:
                                        ins = nc.vector.scalar_tensor_tensor(d, bias[0][:, 0:nk], -float(bias[1]), score_bank(u, s)[:, 0:nk],
                                                                             ALU.mult, ALU.add)
                                ins.then_inc(vector_steps.up(), 1)
                                dve.wait_ge(vector_steps.sem, vector_steps.n)
                                for a, b in groups(units[u]):
                                    nk = units[u]["segs"][a][2]
                                    ins = nc.vector.tensor_reduce(stat[:, u % 3, a, 0:1], probs[:, u % 3, a:b, 0:nk], AX.XY, ALU.max, negate=True)
                                ins.then_inc(shifted.up(), 1)
                            if 1 <= u < n + 1:
                                w = u - 1
                                dve.wait_ge(exped.sem, exped.at(w + 1))
                                m = len(groups(units[w]))
                                nc.vector.reciprocal(stat[:, w % 3, 0:m, 2], stat[:, w % 3, 0:m, 1]).then_inc(vector_steps.up(), 1)
                                dve.wait_ge(vector_steps.sem, vector_steps.n)
                                if units[w]["gates"] is not None:
                                    nc.vector.tensor_tensor(stat[:, w % 3, 0:m, 2], stat[:, w % 3, 0:m, 2], units[w]["gates"],
                                                            ALU.mult).then_inc(vector_steps.up(), 1)
                                    dve.wait_ge(vector_steps.sem, vector_steps.n)
                                for a, b in groups(units[w]):
                                    nk = units[w]["segs"][a][2]
                                    d = probs[:, w % 3, a:b, 0:nk]
                                    ins = nc.vector.tensor_scalar(d, d, stat[:, w % 3, a, 2:3], None, ALU.mult)
                                ins.then_inc(normal.up(), 1)
                            if u >= 4:
                                w = u - 4
                                dve.wait_ge(summed.sem, summed.at(w + 1))
                                lo, rows = units[w]["rows"]
                                dst, gate = units[w]["out"]
                                nc.vector.tensor_tensor(dst, bank[6 + w % 2][lo:lo + rows, 0:P], gate, ALU.mult).then_inc(done.up(), 1)

                    @block.scalar
                    def _(act):
                        for u in range(n + 2):
                            if u < n:
                                act.wait_ge(shifted.sem, shifted.at(u + 1))
                                for a, b in groups(units[u]):
                                    nk = units[u]["segs"][a][2]
                                    d = probs[:, u % 3, a:b, 0:nk]
                                    ins = nc.scalar.activation(d, d, ACT.Exp, bias=stat[:, u % 3, a, 0:1], accum_out=stat[:, u % 3, a, 1:2])
                                ins.then_inc(exped.up(), 1)
                            if u >= 2:
                                w = u - 2
                                act.wait_ge(turned.sem, turned.at(w + 1))
                                bl = blocks(units[w])
                                for i0 in range(0, len(bl), 4):
                                    whole = [x for x in bl[i0:i0 + 4] if x[2] == P]
                                    if whole:
                                        ins = nc.scalar.copy(probsT[:, w % depth, i0:i0 + len(whole), :].rearrange("p b s -> p (b s)"),
                                                             bank[4 + i0 // 4][:, 0:len(whole) * P])
                                    for i in range(i0 + len(whole), min(i0 + 4, len(bl))):
                                        keys = bl[i][2]
                                        ins = nc.scalar.copy(probsT[0:keys, w % depth, i, :], bank[4 + i // 4][0:keys, (i % 4) * P:(i % 4 + 1) * P])
                                ins.then_inc(turned_in.up(), 1)

        def memory_units(qT, kT, v, yT, gate, tile0):
            units = []
            for t in range(TT):
                for h in range(H):
                    lo = (h % 2) * HD
                    rows = slice(lo, lo + HD)
                    units.append({
                        "segs": [(qT[rows, h // 2, t * P:(t + 1) * P], kT[rows, h // 2, :], T, None,
                                  [(v[:, b, h * HD:(h + 1) * HD], P) for b in range(TT)])],
                        "joint": True, "gates": None, "rows": (lo, HD),
                        "out": (yT[rows, tile0 + h // 2, t * P:(t + 1) * P], gate[rows, h // 2, t * P:(t + 1) * P])})
            return units

        def memory_keys(mem, hawk_kT, hawk_v, nsa_kT, nsa_v):
            def copies(kT, v):
                return lambda pair: [(kT[:, :, :], pair[0][:, :].rearrange("p (m t) -> p m t", m=2), 1.0),
                                     (v[:, :, :], pair[1][:, :].rearrange("p (t d) -> p t d", t=TT), 1.0)]

            with ExitStack() as st:
                memT = mem[:, :, :].rearrange("p t d -> p (t d)").rearrange("p (k t) -> p k t", t=T)
                plainT = sb(st, "mem_plainT", [P, KD, T])
                norm_stage(mem, None, None, plainT)
                with nc.Block() as block:
                    @block.vector
                    def _(dve):
                        for dst, name in ((hT, "hawk_mem_norm_2"), (memT, "nsa_mem_norm_2")):
                            for k in range(KD):
                                nc.vector.tensor_scalar(dst[:, k, :], plainT[:, k, :], col(name, k, 1), None, ALU.mult)
                project_stage(first["hawk_mem"], [("keys_values", copies(hawk_kT, hawk_v))], hT)
                project_stage(first["nsa_mem"], [("keys_values", copies(nsa_kT, nsa_v))], memT)

        def recurrence_work(st, yT, za, raw, room):
            xc = yT[:, 0:KD, :]
            ig = raw[:, :, 0:T]
            wgate = room[:, 0:KD * T].rearrange("p (n m j) -> p n m j", n=2, m=KD)
            den = room[:, 0:KD * T].rearrange("p (m t) -> p m t", t=T)
            rg = room[:, KD * T:2 * KD * T].rearrange("p (m t) -> p m t", t=T)
            vec = sb(st, "lru_vec", [P, 4, KD])
            cleared, w_in, gated, convolved, done = (signal(s) for s in ("lru_w_cleared", "lru_w_in", "lru_gate_dots", "convolved", "lru_done"))
            soft_in, soft, sigmoids, log_ready = (signal(s) for s in ("lru_soft_in", "lru_soft_exp", "lru_sigmoids", "lru_log_ready"))
            a_ready, t_ready, m_in, m_ready, z_ready = (signal(s) for s in ("lru_a_ready", "lru_tanh_ready", "lru_mult_in", "lru_mult_ready", "lru_z_ready"))

            def load_gates(act):
                act.wait_ge(cleared.sem, cleared.at(1))
                for n, name in enumerate(("hawk_gate_a_w_2", "hawk_gate_x_w_2")):
                    w = A[name][0].rearrange("(m two) i j -> two i m j", two=2)
                    for two in range(2):
                        rows = slice(two * HD, (two + 1) * HD)
                        act.dma_start(wgate[rows, n, :, rows], w[two]).then_inc(w_in.up(16), 16)
                act.wait_ge(soft_in.sem, soft_in.at(1))
                nc.scalar.activation(vec[:, 1, :], vec[:, 0, :], ACT.Exp, scale=-1.0).then_inc(soft.up(), 1)

            def gate_dots(r):
                def work(pe):
                    if r == 0:
                        pe.wait_ge(w_in.sem, w_in.at(64))
                        pe.wait_ge(convolved.sem, convolved.at(1))
                    else:
                        pe.wait_ge(sigmoids.sem, sigmoids.at(r))
                    for i in range(4):
                        m = 4 * (r % 2) + i
                        last = nc.tensor.matmul(bank[6 + i // 2][:, (i % 2) * T:(i % 2 + 1) * T], wgate[:, r // 2, m, :], xc[:, m, :],
                                                start=True, stop=True)
                    last.then_inc(gated.up(), 1)
                return work

            def gate_sigmoids(r):
                def work(act):
                    dst, bias = ((rg, "hawk_gate_a_b_2"), (ig, "hawk_gate_x_b_2"))[r // 2]
                    act.wait_ge(gated.sem, gated.at(r + 1))
                    for i in range(4):
                        m = 4 * (r % 2) + i
                        ins = nc.scalar.activation(dst[:, m, :], bank[6 + i // 2][:, (i % 2) * T:(i % 2 + 1) * T], ACT.Sigmoid,
                                                   bias=col(bias, m, 1))
                    ins.then_inc(sigmoids.up(), 1)
                return work

            def decays(act):
                act.wait_ge(log_ready.sem, log_ready.at(1))
                nc.scalar.activation(den, rg, ACT.Tanh).then_inc(t_ready.up(), 1)
                act.wait_ge(t_ready.sem, t_ready.n)
                nc.scalar.activation(rg, rg, ACT.Exp).then_inc(a_ready.up(), 1)
                nc.scalar.activation(za[:, :, :], za[:, :, :], ACT.Silu).then_inc(z_ready.up(), 1)

            def roots(act):
                act.wait_ge(m_in.sem, m_in.at(1))
                nc.scalar.activation(den, den, ACT.Sqrt).then_inc(m_ready.up(), 1)

            def room_free(act):
                act.wait_ge(done.sem, done.at(1))

            def vector_work(dve, evacuated):
                nc.vector.memset(wgate, 0.0).then_inc(cleared.up(), 1)
                lam = col("hawk_lambda_2")
                nc.vector.scalar_tensor_tensor(vec[:, 0, :], lam, -1.0, lam, ALU.mult, ALU.max).then_inc(soft_in.up(), 1)
                dve.wait_ge(soft.sem, soft.at(1))
                nc.vector.tensor_scalar(vec[:, 2, :], vec[:, 1, :], 2.0, None, ALU.add).then_inc(vector_steps.up(), 1)
                dve.wait_ge(vector_steps.sem, vector_steps.n)
                nc.vector.reciprocal(vec[:, 2, :], vec[:, 2, :]).then_inc(vector_steps.up(), 1)
                dve.wait_ge(vector_steps.sem, vector_steps.n)
                nc.vector.tensor_tensor(vec[:, 0, :], vec[:, 1, :], vec[:, 2, :], ALU.mult).then_inc(vector_steps.up(), 1)
                dve.wait_ge(vector_steps.sem, vector_steps.n)
                nc.vector.tensor_tensor(vec[:, 1, :], vec[:, 0, :], vec[:, 0, :], ALU.mult).then_inc(vector_steps.up(), 1)
                dve.wait_ge(vector_steps.sem, vector_steps.n)
                nc.vector.memset(vec[:, 2, :], 1.0 / 17).then_inc(vector_steps.up(), 1)
                dve.wait_ge(vector_steps.sem, vector_steps.n)
                for odd in range(15, 0, -2):
                    nc.vector.tensor_tensor(vec[:, 2, :], vec[:, 2, :], vec[:, 1, :], ALU.mult).then_inc(vector_steps.up(), 1)
                    dve.wait_ge(vector_steps.sem, vector_steps.n)
                    nc.vector.tensor_scalar(vec[:, 2, :], vec[:, 2, :], 1.0 / odd, None, ALU.add).then_inc(vector_steps.up(), 1)
                    dve.wait_ge(vector_steps.sem, vector_steps.n)
                nc.vector.tensor_tensor(vec[:, 2, :], vec[:, 2, :], vec[:, 0, :], ALU.mult).then_inc(vector_steps.up(), 1)
                dve.wait_ge(vector_steps.sem, vector_steps.n)
                nc.vector.tensor_scalar(vec[:, 1, :], lam, -1.0, 0.0, ALU.mult, ALU.max).then_inc(vector_steps.up(), 1)
                dve.wait_ge(vector_steps.sem, vector_steps.n)
                nc.vector.scalar_tensor_tensor(vec[:, 2, :], vec[:, 2, :], 2.0, vec[:, 1, :], ALU.mult, ALU.add).then_inc(vector_steps.up(), 1)
                dve.wait_ge(vector_steps.sem, vector_steps.n)
                nc.vector.tensor_scalar(vec[:, 3, :], vec[:, 2, :], -LRU_C, None, ALU.mult).then_inc(vector_steps.up(), 1)
                dve.wait_ge(vector_steps.sem, vector_steps.n)
                dve.wait_ge(evacuated.sem, evacuated.at(2))
                convolve(dve, raw, xc, KD, "hawk_conv_w_2", "hawk_conv_b_2", convolved)
                dve.wait_ge(convolved.sem, convolved.n)
                dve.wait_ge(sigmoids.sem, sigmoids.at(2))
                nc.vector.tensor_tensor(rg, rg, vec[:, 3, :].unsqueeze(2).to_broadcast([P, KD, T]), ALU.mult).then_inc(log_ready.up(), 1)
                dve.wait_ge(sigmoids.sem, sigmoids.at(4))
                nc.vector.tensor_tensor(xc, xc, ig, ALU.mult).then_inc(vector_steps.up(), 1)
                dve.wait_ge(vector_steps.sem, vector_steps.n)
                dve.wait_ge(t_ready.sem, t_ready.at(1))
                nc.vector.tensor_scalar(ig, den, -1.0, 1.0, ALU.mult, ALU.add).then_inc(vector_steps.up(), 1)
                dve.wait_ge(vector_steps.sem, vector_steps.n)
                nc.vector.reciprocal(ig, ig).then_inc(vector_steps.up(), 1)
                dve.wait_ge(vector_steps.sem, vector_steps.n)
                nc.vector.scalar_tensor_tensor(den, den, -2.0, ig, ALU.mult, ALU.mult).then_inc(m_in.up(), 1)
                dve.wait_ge(m_ready.sem, m_ready.at(1))
                nc.vector.memset(den[:, :, 0:1], 1.0).then_inc(vector_steps.up(), 1)
                dve.wait_ge(vector_steps.sem, vector_steps.n)
                nc.vector.tensor_tensor(xc, xc, den, ALU.mult).then_inc(vector_steps.up(), 1)
                dve.wait_ge(vector_steps.sem, vector_steps.n)
                dve.wait_ge(a_ready.sem, a_ready.at(1))
                for m in range(KD):
                    ins = nc.vector.tensor_tensor_scan(ig[:, m, :], rg[:, m, :], xc[:, m, :], 0.0, ALU.mult, ALU.add)
                ins.then_inc(vector_steps.up(), 1)
                dve.wait_ge(vector_steps.sem, vector_steps.n)
                dve.wait_ge(z_ready.sem, z_ready.at(1))
                nc.vector.tensor_tensor(yT[:, 0:KD, :], ig, za[:, :, :], ALU.mult).then_inc(done.up(), 1)


            tensor_work = {4 + r: gate_dots(r) for r in range(4)}
            scalar_work = {0: load_gates, 8: decays, 9: roots, 10: room_free} | {4 + r: gate_sigmoids(r) for r in range(4)}
            return tensor_work, scalar_work, vector_work

        def hawk_layer():
            G = len(DIL)
            with ExitStack() as st:
                yT = sb(st, "hawk_yT", [P, 14, T])
                mem_kT = sb(st, "mem_kT", [P, 2, T])
                mem_v = sb(st, "mem_v", [P, TT, T])
                with ExitStack() as st_mem:
                    mem = sb(st_mem, "mem", [P, TT, D])
                    final_norm_stage("final_norm", x, mem)
                    memory_keys(mem, mem_kT, mem_v, nsa_mem_kT, nsa_mem_v)
                norm_stage(x, col("hawk_norm_2"), None, hT)
                with ExitStack() as st_a:
                    qT = sb(st_a, "dil_qT", [P, G * H, T])
                    kT = sb(st_a, "dil_kT", [P, G * H, T])
                    room = sb(st_a, "dil_v_gates", [P, TT * G * 512 + H * T])
                    v = room[:, 0:TT * G * 512].rearrange("p (t d) -> p t d", t=TT)
                    zb = room[:, TT * G * 512:].rearrange("p (h t) -> p h t", h=H)
                    mq = sb(st_a, "mem_q_gate", [P, 4, T])

                    def memory_query(pair):
                        return [(mq[:, 0:2, :], pair[0][:, :].rearrange("p (m t) -> p m t", m=2), HD ** -0.5),
                                (mq[:, 2:4, :], pair[1][:, :].rearrange("p (m t) -> p m t", m=2), 1.0)]
                    st_lru = st_a.enter_context(ExitStack())
                    za = sb(st_lru, "lru_za", [P, KD, T])
                    raw = sb(st_lru, "lru_raw", [P, KD, T + CONV - 1])

                    def to_raw(m0):
                        return lambda pair: [(raw[:, m0 + 2 * b:m0 + 2 * b + 2, CONV - 1:], pair[b][:, :].rearrange("p (m t) -> p m t", m=2), 1.0)
                                             for b in range(2)]
                    plan = [("channel", to_raw(0)), ("channel", to_raw(4)), ("channel", to_channels(za, 0)), ("channel", to_channels(za, 4))]
                    plan += [("channel", to_channels(qT, 4 * g, float(P) ** -0.5)) for g in range(G)]
                    plan += [("channel", to_channels(kT, 4 * g)) for g in range(G)]
                    plan += [("channel", memory_query), ("channel", to_channels(zb, 0))]
                    plan += [("token", to_tokens(v, 512 * g)) for g in range(G)]
                    tensor_work, scalar_work, vector_work = recurrence_work(st_lru, yT, za, raw, room)
                    scalar_work[12] = silu_of(zb, mq[:, 2:4, :])
                    project_stage(first["hawk_in"], plan, hT, 3, tensor_work, scalar_work, vector_work)
                    st_lru.close()
                    dist = sb(st_a, "dist", [P, 3, TT, T])
                    load_stage(dist, dists.rearrange("p (n t s) -> p n t s", n=4, t=TT)[:, 1:4])
                    units = []
                    for t in range(TT):
                        for h in range(H):
                            segs = [(qT[:, g * H + h, t * P:(t + 1) * P], kT[:, g * H + h, 0:(t + 1) * P], (t + 1) * P,
                                     (dist[:, g, t, :], SLOPES_DIL[g * H + h]),
                                     [(v[:, b, g * 512 + h * P:g * 512 + (h + 1) * P], P) for b in range(t + 1)]) for g in range(G)]
                            units.append({"segs": segs, "joint": True, "gates": None, "rows": (0, P),
                                          "out": (yT[:, KD + h, t * P:(t + 1) * P], zb[:, h, t * P:(t + 1) * P])})
                    units += memory_units(mq[:, 0:2, :], mem_kT, mem_v, yT, mq[:, 2:4, :], KD + H)
                    attention_stage(units, 1)
                out_stage(first["hawk_out"], [(0, 8), (8, 6)], yT, None)

        def load_stage(dst, src):
            loaded = signal("operands_in")
            with nc.Block() as block:
                @block.scalar
                def _(act):
                    act.dma_start(dst[:, :, :, :] if len(dst.shape) == 4 else dst, src).then_inc(loaded.up(16), 16)
                    act.wait_ge(loaded.sem, loaded.n)

        def nsa_layer():
            G = 2
            KV = 2 * G
            with ExitStack() as st:
                yT = sb(st, "nsa_yT", [P, 10, T])
                norm_stage(x, col("nsa_norm_2"), None, hT)
                qT = sb(st, "nsa_qT", [P, 8, T])
                pairT = sb(st, "cmp_pairT", [P, KV, T])
                kT = sb(st, "nsa_kT", [P, KV, T])
                vg = sb(st, "nsa_v_gates", [P, TT, 304])
                zT = sb(st, "nsa_zT", [P, 8, T])
                mq = sb(st, "nsa_mem_q_gate", [P, 4, T])

                def to_pairs(pair):
                    copies = []
                    for b in range(2):
                        src = pair[b][:, :].rearrange("p (m t) -> p m t", m=2)
                        copies.append((pairT[0:HD, 2 * b:2 * b + 2, :], src[0:HD], 1.0))
                        copies.append((pairT[HD:P, 2 * b:2 * b + 2, 0:T - 1], src[HD:P, :, 1:T], 1.0))
                    return copies

                def memory_query(pair):
                    return [(mq[:, 0:2, :], pair[0][:, :].rearrange("p (m t) -> p m t", m=2), HD ** -0.5),
                            (mq[:, 2:4, :], pair[1][:, :].rearrange("p (m t) -> p m t", m=2), 1.0)]

                gates = sb(st, "nsa_gates", [P, TT, 3 * NSA_H])
                cmp_kT = sb(st, "cmp_kT", [P, G * NCMP])
                cmp_v = sb(st, "cmp_v", [16, G, HD])
                dist = sb(st, "nsa_dist", [P, 1, TT, T])
                rows = sb(st, "cmp_rows", [P, 2, CMP_BLOCK // 2, 32])
                sig = sb(st, "nsa_sig", [P, TT, 3 * NSA_H])
                w2k = sb(st, "cmp_w2k", [P, 2, P])
                w2v = sb(st, "cmp_w2v", [P, 2, HD])
                w_in, sig_ready, gates_ready = signal("operands_in"), signal("nsa_sig_ready"), signal("nsa_gates_ready")

                def load_operands(act):
                    act.dma_start(dist[:, 0], dists.rearrange("p (n t s) -> p n t s", n=4, t=TT)[:, 0]).then_inc(w_in.up(16), 16)
                    for two in range(2):
                        act.dma_start(w2k[:, :, two * HD:(two + 1) * HD], A["nsa_phi_k_w2_2"][0].rearrange("(k p) d -> p k d", p=P)).then_inc(w_in.up(16), 16)
                    act.dma_start(w2v[:, :, :], A["nsa_phi_v_w2_2"][0].rearrange("(k p) d -> p k d", p=P)).then_inc(w_in.up(16), 16)

                def sigmoids(act):
                    act.wait_ge(evacuated_nsa.sem, evacuated_nsa.n)
                    nc.scalar.activation(sig[:, :, :], vg[:, :, 256:304], ACT.Sigmoid).then_inc(sig_ready.up(), 1)

                def rows_and_gates(dve, evacuated):
                    nc.vector.memset(rows[:, :, :, G * NCMP:], 0.0)
                    dve.wait_ge(evacuated.sem, evacuated.at(3))
                    for i, name in enumerate(("nsa_pe_k_2", "nsa_pe_v_2")):
                        for g in range(G):
                            src = pairT[:, 2 * i + g, :]
                            for m in range(CMP_BLOCK // 2):
                                nc.vector.tensor_scalar(rows[:, i, m, g * NCMP:(g + 1) * NCMP],
                                                        src[:, 2 * m:2 * m + CMP_STRIDE * (NCMP - 1) + 1:CMP_STRIDE],
                                                        col(name, m, 1), None, ALU.add)
                    dve.wait_ge(sig_ready.sem, sig_ready.at(1))
                    g3 = gates[:, :, :].rearrange("p t (h b) -> p t h b", b=3)
                    s3 = sig[:, :, :].rearrange("p t (h b) -> p t h b", b=3)
                    nc.vector.tensor_copy(g3[:, :, :, 0:2], s3[:, :, :, 1:3])
                    for t in range(TT):
                        ins = nc.vector.tensor_scalar(g3[:, t, :, 2], s3[:, t, :, 0], kc[:, C_ANY + t:C_ANY + t + 1], None, ALU.mult)
                    ins.then_inc(gates_ready.up(), 1)
                    dve.wait_ge(w_in.sem, w_in.at(64))

                evacuated_nsa = signal("chunk_evacuated")
                project_stage(first["nsa_in"], [("channel", to_channels(qT, 0, HD ** -0.5)), ("channel", to_channels(qT, 4, HD ** -0.5)),
                                                ("channel", to_pairs), ("channel", to_channels(kT, 0)), ("token", to_tokens(vg, 0, 304)),
                                                ("channel", to_channels(zT, 0)), ("channel", to_channels(zT, 4)), ("channel", memory_query)], hT,
                              scalar_work={0: load_operands, 4: sigmoids, 6: silu_of(zT[:, :, :]), 7: silu_of(mq[:, 2:4, :])},
                              vector_work=rows_and_gates)
                compress(rows, w2k, w2v, cmp_kT, cmp_v)
                units = []
                for t in range(TT):
                    for h in range(NSA_H):
                        g, lo = h // 8, (h % 2) * HD
                        rows = slice(lo, lo + HD)
                        q = qT[rows, h // 2, t * P:(t + 1) * P]
                        slope = SLOPES_NSA[h]
                        keys = (t + 1) * P
                        segs = [(q, cmp_kT[rows, g * NCMP:(g + 1) * NCMP], NCMP, (cmp_dist[:, t, :], slope), [(cmp_v[0:NCMP, g, :], NCMP)])]
                        for branch in range(2):
                            at = branch * P + g * HD
                            segs.append((q, kT[rows, branch * 2 + g, 0:keys], keys, (dist[:, 0, t, :], slope),
                                         [(vg[:, b, at:at + HD], P) for b in range(t + 1)]))
                        segs = [segs[1], segs[2], segs[0]]
                        units.append({"segs": segs, "joint": False, "gates": gates[:, t, 3 * h:3 * h + 3], "rows": (lo, HD),
                                      "out": (yT[rows, h // 2, t * P:(t + 1) * P], zT[rows, h // 2, t * P:(t + 1) * P])})
                units += memory_units(mq[:, 0:2, :], nsa_mem_kT, nsa_mem_v, yT, mq[:, 2:4, :], 8)
                attention_stage(units)
                out_stage(first["nsa_out"], [(0, 8), (8, 2)], yT, None)

        def silu_of(*tensors):
            def work(act):
                copied = signals["chunk_evacuated"]
                act.wait_ge(copied.sem, copied.n)
                for t in tensors:
                    nc.scalar.activation(t, t, ACT.Silu)
            return work

        def compress(rows, w2k, w2v, cmp_kT, cmp_v):
            c0 = first["nsa_phi"]
            frees(c0, 2)
            used0 = chunk_used.n
            G, STEPS = 2, CMP_BLOCK // 2
            n = G * NCMP
            with ExitStack() as st:
                hid = sb(st, "cmp_hid", [2 * 32, PHI])
                hidT = sb(st, "cmp_hidT", [P, 2, 2, 32])
                hid_ready, turned, hidT_ready, out_ready = (signal(s) for s in ("cmp_hid_ready", "tiles_turned", "cmp_hidT_ready", "cmp_out_ready"))
                with nc.Block() as block:
                    @block.sync
                    def _(sp):
                        fill_ring(sp, c0 + 1)

                    @block.scalar
                    def _(act):
                        act.wait_ge(chunk_used.sem, used0 + 2)
                        nc.scalar.activation(hid[:, :], bank[0][0:64, 0:PHI], ACT.Silu).then_inc(hid_ready.up(), 1)

                    @block.vector
                    def _(dve):
                        dve.wait_ge(turned.sem, turned.at(1))
                        nc.vector.tensor_copy(hidT[:, :, :, :].rearrange("p m i n -> p (m i n)"), bank[1][:, 0:128]).then_inc(hidT_ready.up(), 1)
                        dve.wait_ge(out_ready.sem, out_ready.at(1))
                        nc.vector.tensor_copy(cmp_kT[:, :], bank[2][:, 0:n])
                        nc.vector.tensor_copy(cmp_v[0:NCMP, :, :], bank[3][0:NCMP, 0:G * HD].rearrange("p (g d) -> p g d", g=G))

                    @block.tensor
                    def _(pe):
                        for i in range(2):
                            arrived(pe, c0 + i)
                        for s in range(STEPS):
                            for i in range(2):
                                last = nc.tensor.matmul(bank[0][32 * i:32 * i + 32, 0:PHI], rows[:, i, s, :], slot(c0 + i)[:, s, :],
                                                        start=(s == 0), stop=(s == STEPS - 1))
                                if s == STEPS - 1:
                                    last.then_inc(chunk_used.up(), 1)
                        pe.wait_ge(hid_ready.sem, hid_ready.at(1))
                        for m in range(2):
                            last = nc.tensor.transpose(bank[1][:, m * 64:(m + 1) * 64], hid[:, m * P:(m + 1) * P], ident[0:64, 0:64])
                        last.then_inc(turned.up(), 1)
                        pe.wait_ge(hidT_ready.sem, hidT_ready.at(1))
                        for m in range(2):
                            nc.tensor.matmul(bank[2][:, 0:n], w2k[:, m, :], hidT[:, m, 0, 0:n], start=(m == 0), stop=(m == 1))
                        for g in range(G):
                            for m in range(2):
                                last = nc.tensor.matmul(bank[3][0:NCMP, g * HD:(g + 1) * HD], hidT[:, m, 1, g * NCMP:(g + 1) * NCMP], w2v[:, m, :],
                                                        start=(m == 0), stop=(m == 1))
                        last.then_inc(out_ready.up(), 1)

        def store_stage():
            stored = signal("output_stored")
            with nc.Block() as block:
                @block.sync
                def _(sp):
                    sp.dma_start(out[0].rearrange("(t p) d -> p t d", p=P), x[:, :, :]).then_inc(stored.up(16), 16)
                    sp.wait_ge(stored.sem, stored.n)

        gates = [sb(st_first, f"gates{layer}", [P, 2, D]) for layer in range(2)]
        mod = [sb(st_first, f"mod{layer}", [P, 4, KD]) for layer in range(2)]
        modulation_stage(0, gates[0], mod[0])
        for layer in range(2):
            with ExitStack() as st:
                norm_stage(x, mod[layer][:, 0, :], mod[layer][:, 1, :], hT)
                with ExitStack() as st_m:
                    mixed = sb(st_m, "mixed", [P, TT, D])
                    (even_mixer, gla_mixer)[layer](mixed)
                    turn_stage(mixed, hT)
                out_stage(first[("even_out", "gla_out")[layer]], [(0, KD)], hT, gates[layer][:, 0, :])
                if last_stage == ("mix", layer):
                    store_stage()
                    return
                xn = sb(st, "xn_kept", [P, TT, D])
                norm_stage(x, mod[layer][:, 2, :], mod[layer][:, 3, :], hT, xn=xn)
                following = modulation_work(1, st, gates[1], mod[1]) if layer == 0 else None
                experts_stage(layer, gates[layer], xn, mod[layer][:, 2, :], mod[layer][:, 3, :], following)
            if last_stage == ("moe", layer):
                store_stage()
                return
        st_first.close()
        nsa_mem_kT = sb(ctx, "nsa_mem_kT", [P, 2, T])
        nsa_mem_v = sb(ctx, "nsa_mem_v", [P, TT, T])
        hawk_layer()
        if last_stage == "hawk":
            store_stage()
            return
        nsa_layer()
        final_norm_stage("final_norm_2", x)
        store_stage()


_INS = ['x', 'c', 'positions', 'ada_w', 'ada_b', 'norm_mix', 'norm_ffn', 'even_w_in', 'gdn_conv_w', 'gdn_a_log', 'gdn_dt_bias', 'gdn_out_norm',
        'even_w_out', 'gla_w_in', 'gla_w_gate2', 'gla_b_gate2', 'gla_out_norm', 'gla_w_out', 'router_group_w', 'router_group_b', 'router_exp_w',
        'router_exp_b', 'exp_w1', 'exp_w3', 'exp_w2', 'final_norm', 'mem_2', 'hawk_norm_2', 'hawk_w_in_2', 'hawk_conv_w_2', 'hawk_conv_b_2',
        'hawk_gate_a_w_2', 'hawk_gate_a_b_2', 'hawk_gate_x_w_2', 'hawk_gate_x_b_2', 'hawk_lambda_2', 'hawk_mem_norm_2', 'hawk_w_mem_kv_2',
        'hawk_w_out_2', 'nsa_norm_2', 'nsa_w_in_2', 'nsa_pe_k_2', 'nsa_pe_v_2', 'nsa_phi_k_w1_2', 'nsa_phi_k_w2_2', 'nsa_phi_v_w1_2',
        'nsa_phi_v_w2_2', 'nsa_mem_norm_2', 'nsa_w_mem_kv_2', 'nsa_w_out_2', 'final_norm_2']


LAST_STAGE = None


def kernel(**inputs):
    import concourse.bacc as _bacc
    from concourse.bass_utils import run_bass_kernel_spmd as _run

    nc = _bacc.Bacc("TRN2", target_bir_lowering=False, num_devices=1)
    arrays, args = {}, {}
    table, distances = constants()
    given = {name: inputs[name] for name in _INS}
    given["consts"], given["dists"] = table, distances
    for name, value in given.items():
        a = np.ascontiguousarray(value)
        arrays[f"in_{name}_dram"] = a
        args[name] = nc.dram_tensor(f"in_{name}_dram", a.shape, mybir.dt.from_np(a.dtype), kind="ExternalInput").ap()
    result = nc.dram_tensor("out_0_dram", (1, T, D), F32, kind="ExternalOutput").ap()
    program(nc, args, args["consts"], args["dists"], result, LAST_STAGE)
    r = _run(nc, [arrays], core_ids=[0])
    return r.results[0]["out_0_dram"]
```
